# Optimizing a Trainium2 kernel written in Bass

```python
import jax, jax.numpy as jnp
from jax import lax
import numpy as np

D_MODEL = 1024
BATCH = 1
SEQ = 256
DEPTH = 2

HEAD_DIM = 64
ROPE_THETA = 10000.0

RET_HEADS = 4
RET_DK = 64
RET_DV = 64
RET_CHUNK = 128

SWA_Q_HEADS = 6
SWA_KV_HEADS = 2
SWA_WINDOW = 128
SWA_BLOCK = 128

MLA_HEADS = 6
MLA_Q_RANK = 384
MLA_KV_RANK = 256
MLA_NOPE = 64
MLA_ROPE = 32
MLA_V = 64
MLA_BLOCK = 128

RET_W = RET_HEADS * RET_DV
SWA_W = SWA_Q_HEADS * HEAD_DIM
MLA_W = MLA_HEADS * MLA_V
D_MIX = RET_W + SWA_W + MLA_W

IN_SIZES = (
    RET_HEADS * RET_DK,
    RET_HEADS * RET_DK,
    RET_W,
    RET_W,
    SWA_Q_HEADS * HEAD_DIM,
    SWA_KV_HEADS * HEAD_DIM,
    SWA_KV_HEADS * HEAD_DIM,
    MLA_Q_RANK,
    MLA_KV_RANK,
    MLA_ROPE,
)
IN_COLS = sum(IN_SIZES)

N_EXPERTS = 16
N_GROUPS = 4
EXPERTS_PER_GROUP = N_EXPERTS // N_GROUPS
TOP_K = 2
D_EXPERT = 256

DEEPNORM_ALPHA = (2 * DEPTH) ** 0.25
DEEPNORM_BETA = (8 * DEPTH) ** -0.25
LN_EPS = 1e-5
RMS_EPS = 1e-6
NEG_INF = -1e30


def _split_points():
    return [int(s) for s in np.cumsum(np.array(IN_SIZES))[:-1]]

def layer_norm(x, g, b):
    xf = x.astype(jnp.float32)
    mu = jnp.mean(xf, -1, keepdims=True)
    var = jnp.mean(jnp.square(xf - mu), -1, keepdims=True)
    return ((xf - mu) * lax.rsqrt(var + LN_EPS) * g + b).astype(x.dtype)

def rms_norm(x, g):
    xf = x.astype(jnp.float32)
    return (xf * lax.rsqrt(jnp.mean(xf * xf, -1, keepdims=True) + RMS_EPS) * g).astype(x.dtype)

def rope(x, pos):
    d = x.shape[-1]
    inv = ROPE_THETA ** (-jnp.arange(0, d, 2, dtype=jnp.float32) / d)
    ang = pos.astype(jnp.float32)[:, None] * inv[None, :]
    cos = jnp.cos(ang)[:, None, :]
    sin = jnp.sin(ang)[:, None, :]
    x1, x2 = x[..., : d // 2], x[..., d // 2:]
    return jnp.concatenate([x1 * cos - x2 * sin, x1 * sin + x2 * cos], -1).astype(x.dtype)

def retention(q, k, v, g, gn_w):
    B, S, H, dk = q.shape
    dv = RET_DV
    C = RET_CHUNK
    NC = S // C
    gamma = 1.0 - 2.0 ** (-5.0 - jnp.arange(H, dtype=jnp.float32))
    log_g = jnp.log(gamma)
    idx = jnp.arange(C, dtype=jnp.float32)
    rel = idx[:, None] - idx[None, :]
    decay_in = jnp.where(rel[None] >= 0,
                         jnp.exp(jnp.maximum(rel, 0.0)[None] * log_g[:, None, None]), 0.0)
    xi = jnp.exp((idx[None, :] + 1.0) * log_g[:, None]).T
    zeta = jnp.exp((C - 1.0 - idx[None, :]) * log_g[:, None]).T
    chunk_decay = jnp.exp(C * log_g)

    qc = q.reshape(B, NC, C, H, dk).astype(jnp.float32)
    kc = (k * (dk ** -0.5)).reshape(B, NC, C, H, dk).astype(jnp.float32)
    vc = v.reshape(B, NC, C, H, dv).astype(jnp.float32)

    scores = jnp.einsum('bnihd,bnjhd->bnhij', qc, kc) * decay_in[None, None]
    inner = jnp.einsum('bnhij,bnjhe->bnihe', scores, vc)

    upd = jnp.einsum('bnjhd,bnjhe->bnhde', kc * zeta[None, None, :, :, None], vc)

    def step(state, u):
        return chunk_decay[None, :, None, None] * state + u, state

    init = jnp.zeros((B, H, dk, dv), jnp.float32)
    _, prev_states = lax.scan(step, init, jnp.moveaxis(upd, 1, 0))
    prev_states = jnp.moveaxis(prev_states, 0, 1)
    cross = jnp.einsum('bnihd,bnhde->bnihe', qc * xi[None, None, :, :, None], prev_states)

    o = (inner + cross).reshape(B, S, H, dv)
    mu = jnp.mean(o, -1, keepdims=True)
    var = jnp.mean(jnp.square(o - mu), -1, keepdims=True)
    o = (o - mu) * lax.rsqrt(var + LN_EPS) * gn_w.astype(jnp.float32).reshape(H, dv)
    o = o.reshape(B, S, H * dv) * jax.nn.silu(g.astype(jnp.float32))
    return o.astype(q.dtype)

def sliding_window_sink_attention(q, k, v, sinks):
    B, S, Hq, d = q.shape
    Hkv = k.shape[2]
    G = Hq // Hkv
    L = SWA_BLOCK
    NB = S // L
    qb = q.reshape(B, NB, L, Hkv, G, d)
    kb = k.reshape(B, NB, L, Hkv, d)
    vb = v.reshape(B, NB, L, Hkv, d)
    pad = ((0, 0), (1, 0), (0, 0), (0, 0), (0, 0))
    kwin = jnp.concatenate([jnp.pad(kb, pad)[:, :NB], kb], axis=2)
    vwin = jnp.concatenate([jnp.pad(vb, pad)[:, :NB], vb], axis=2)

    s = jnp.einsum('bnihgd,bnjhd->bnhgij', qb, kwin).astype(jnp.float32) * (d ** -0.5)
    i = jnp.arange(L)[:, None]
    j = jnp.arange(2 * L)[None, :]
    band = (j <= i + L) & (j > i + L - SWA_WINDOW)
    blk = jnp.arange(NB)[:, None]
    valid = (blk > 0) | (jnp.arange(2 * L)[None, :] >= L)
    mask = band[None] & valid[:, None, :]
    s = jnp.where(mask[None, :, None, None], s, NEG_INF)

    sink = sinks.astype(jnp.float32).reshape(1, 1, Hkv, G, 1, 1)
    m = jnp.maximum(jnp.max(s, -1, keepdims=True), sink)
    p = jnp.exp(s - m)
    denom = jnp.sum(p, -1, keepdims=True) + jnp.exp(sink - m)
    o = jnp.einsum('bnhgij,bnjhd->bnihgd', (p / denom).astype(v.dtype), vwin)
    return o.reshape(B, S, Hq * d)

def latent_attention(c_q, c_kv, k_rope, q_norm_w, kv_norm_w, w_uq, w_ukv, pos):
    B, S, _ = c_q.shape
    H = MLA_HEADS
    dq = MLA_NOPE + MLA_ROPE
    q = (rms_norm(c_q, q_norm_w) @ w_uq).reshape(B, S, H, dq)
    q = jnp.concatenate([q[..., :MLA_NOPE], rope(q[..., MLA_NOPE:], pos)], -1)
    kv = (rms_norm(c_kv, kv_norm_w) @ w_ukv).reshape(B, S, H, MLA_NOPE + MLA_V)
    k_nope, v = kv[..., :MLA_NOPE], kv[..., MLA_NOPE:]
    k_pe = rope(k_rope[:, :, None, :], pos)
    k = jnp.concatenate([k_nope, jnp.broadcast_to(k_pe, (B, S, H, MLA_ROPE))], -1)
    scale = dq ** -0.5
    L = MLA_BLOCK
    NB = S // L
    qb = jnp.moveaxis(q.reshape(B, NB, L, H, dq), 1, 0)
    kpos = jnp.arange(S)

    def block(args):
        q_blk, n = args
        s = jnp.einsum('bihd,bjhd->bhij', q_blk, k).astype(jnp.float32) * scale
        qpos = n * L + jnp.arange(L)
        s = jnp.where(kpos[None, :] <= qpos[:, None], s, NEG_INF)
        p = jax.nn.softmax(s, axis=-1)
        return jnp.einsum('bhij,bjhe->bihe', p.astype(v.dtype), v)

    o = lax.map(block, (qb, jnp.arange(NB)))
    return jnp.moveaxis(o, 0, 1).reshape(B, S, H * MLA_V)

def grouped_moe(x, router_w, router_bias, w_gate_up, w_down):
    B, S, D = x.shape
    t = x.reshape(-1, D)
    T = t.shape[0]
    scores = jax.nn.sigmoid((t @ router_w).astype(jnp.float32))
    biased = scores + router_bias.astype(jnp.float32)
    grp = biased.reshape(T, N_GROUPS, EXPERTS_PER_GROUP)
    grp_score = jnp.sum(lax.top_k(grp, TOP_K)[0], -1)
    sel_group = jnp.argmax(grp_score, -1)
    in_group = jnp.repeat(jax.nn.one_hot(sel_group, N_GROUPS) > 0, EXPERTS_PER_GROUP, axis=-1)
    _, top_idx = lax.top_k(jnp.where(in_group, biased, -jnp.inf), TOP_K)
    sel = jnp.take_along_axis(scores, top_idx, -1)
    weights = sel / jnp.sum(sel, -1, keepdims=True)
    gates = jnp.sum(jax.nn.one_hot(top_idx, N_EXPERTS, dtype=jnp.float32) * weights[..., None], 1)
    h = jnp.einsum('td,edf->tef', t, w_gate_up)
    a = jax.nn.silu(h[..., :D_EXPERT]) * h[..., D_EXPERT:] * gates[..., None].astype(h.dtype)
    y = jnp.einsum('tef,efd->td', a, w_down)
    return y.reshape(B, S, D)

def first_inputs(seed: int = 0) -> dict:
    key = jax.random.key(seed)
    ks = jax.random.split(key, 20)
    f32 = jnp.float32
    nrm = lambda k, shape, s: jax.random.normal(k, shape, f32) * s
    return {
        "x": nrm(ks[0], (BATCH, SEQ, D_MODEL), 1.0),
        "w_in": nrm(ks[1], (DEPTH, D_MODEL, IN_COLS), D_MODEL ** -0.5),
        "ret_gn_w": 1.0 + nrm(ks[2], (DEPTH, RET_W), 0.02),
        "swa_sinks": nrm(ks[3], (DEPTH, SWA_Q_HEADS), 0.5),
        "mla_q_norm_w": 1.0 + nrm(ks[4], (DEPTH, MLA_Q_RANK), 0.02),
        "mla_kv_norm_w": 1.0 + nrm(ks[5], (DEPTH, MLA_KV_RANK), 0.02),
        "mla_w_uq": nrm(ks[6], (DEPTH, MLA_Q_RANK, MLA_HEADS * (MLA_NOPE + MLA_ROPE)), MLA_Q_RANK ** -0.5),
        "mla_w_ukv": nrm(ks[7], (DEPTH, MLA_KV_RANK, MLA_HEADS * (MLA_NOPE + MLA_V)), MLA_KV_RANK ** -0.5),
        "w_out": nrm(ks[8], (DEPTH, D_MIX, D_MODEL), DEEPNORM_BETA * D_MIX ** -0.5),
        "ln1_g": 1.0 + nrm(ks[9], (DEPTH, D_MODEL), 0.02),
        "ln1_b": nrm(ks[10], (DEPTH, D_MODEL), 0.02),
        "router_w": nrm(ks[11], (D_MODEL, N_EXPERTS), D_MODEL ** -0.5),
        "router_bias": nrm(ks[12], (N_EXPERTS,), 0.01),
        "exp_w_gate_up": nrm(ks[13], (DEPTH, N_EXPERTS, D_MODEL, 2 * D_EXPERT), D_MODEL ** -0.5),
        "exp_w_down": nrm(ks[14], (DEPTH, N_EXPERTS, D_EXPERT, D_MODEL), DEEPNORM_BETA * D_EXPERT ** -0.5),
        "ln2_g": 1.0 + nrm(ks[15], (DEPTH, D_MODEL), 0.02),
        "ln2_b": nrm(ks[16], (DEPTH, D_MODEL), 0.02),
    }

def first_block(x, w_in, ret_gn_w, swa_sinks, mla_q_norm_w, mla_kv_norm_w, mla_w_uq, mla_w_ukv,
              w_out, ln1_g, ln1_b, router_w, router_bias, exp_w_gate_up, exp_w_down, ln2_g, ln2_b):
    B, S, _ = x.shape
    pos = jnp.arange(S)
    splits = _split_points()
    for l in range(DEPTH):
        (r_q, r_k, r_v, r_g, s_q, s_k, s_v, c_q, c_kv, k_rope) = jnp.split(x @ w_in[l], splits, axis=-1)
        rq = rope(r_q.reshape(B, S, RET_HEADS, RET_DK), pos)
        rk = rope(r_k.reshape(B, S, RET_HEADS, RET_DK), pos)
        ret_o = retention(rq, rk, r_v, r_g, ret_gn_w[l])
        swa_o = sliding_window_sink_attention(
            s_q.reshape(B, S, SWA_Q_HEADS, HEAD_DIM),
            s_k.reshape(B, S, SWA_KV_HEADS, HEAD_DIM),
            s_v.reshape(B, S, SWA_KV_HEADS, HEAD_DIM),
            swa_sinks[l])
        mla_o = latent_attention(c_q, c_kv, k_rope, mla_q_norm_w[l], mla_kv_norm_w[l],
                                 mla_w_uq[l], mla_w_ukv[l], pos)
        mix = jnp.concatenate([ret_o, swa_o, mla_o], axis=-1) @ w_out[l]
        x = layer_norm(DEEPNORM_ALPHA * x + mix, ln1_g[l], ln1_b[l])
        ffn = grouped_moe(x, router_w, router_bias, exp_w_gate_up[l], exp_w_down[l])
        x = layer_norm(DEEPNORM_ALPHA * x + ffn, ln2_g[l], ln2_b[l])
    return x


N_HEADS = 8
N_KV_HEADS = 2
GQA_GROUP = N_HEADS // N_KV_HEADS
ATTN_WIDTH = N_HEADS * HEAD_DIM
KV_WIDTH = N_KV_HEADS * HEAD_DIM
WINDOW = 128
BLOCK = 128
ROPE_THETA_2 = 500000.0
ROT_DIM = HEAD_DIM // 4
POOL_SIZES = (2, 4, 8, 16)
POOL_WIDTH = D_MODEL // 2
POOL_GROUP = POOL_WIDTH // len(POOL_SIZES)
N_BRANCHES = 2
IN_WIDTH = ATTN_WIDTH + 2 * KV_WIDTH + POOL_WIDTH + N_BRANCHES * D_MODEL
D_FF = 2816
EPS = 1e-6


def rms_norm_2(x, g):
    x32 = x.astype(jnp.float32)
    y = x32 * lax.rsqrt(jnp.mean(x32 * x32, axis=-1, keepdims=True) + EPS)
    return (y * g.astype(jnp.float32)).astype(x.dtype)

def swiglu(u, w1, w3, w2):
    return (jax.nn.silu(u @ w1) * (u @ w3)) @ w2

def rope_tables(s):
    inv_freq = 1.0 / (ROPE_THETA_2 ** (jnp.arange(0, ROT_DIM, 2, dtype=jnp.float32) / ROT_DIM))
    ang = jnp.arange(s, dtype=jnp.float32)[:, None] * inv_freq[None, :]
    return jnp.cos(ang), jnp.sin(ang)

def partial_rope(t, cos, sin):
    half = ROT_DIM // 2
    t32 = t.astype(jnp.float32)
    t1 = t32[..., :half]
    t2 = t32[..., half:ROT_DIM]
    c = cos[None, :, None, :]
    s = sin[None, :, None, :]
    rot = jnp.concatenate([t1 * c - t2 * s, t2 * c + t1 * s, t32[..., ROT_DIM:]], axis=-1)
    return rot.astype(t.dtype)

def banded_blocks(t):
    b, s = t.shape[0], t.shape[1]
    nb = s // BLOCK
    tp = jnp.pad(t, ((0, 0), (BLOCK, BLOCK), (0, 0), (0, 0)))
    parts = [tp[:, i * BLOCK:i * BLOCK + s].reshape(b, nb, BLOCK, t.shape[2], t.shape[3]) for i in range(3)]
    return jnp.concatenate(parts, axis=2)

def windowed_gqa(q, k, v, sink):
    b, s = q.shape[0], q.shape[1]
    nb = s // BLOCK
    qb = q.reshape(b, nb, BLOCK, N_KV_HEADS, GQA_GROUP, HEAD_DIM)
    kb = banded_blocks(k)
    vb = banded_blocks(v)
    scores = jnp.einsum('bnqhgd,bnkhd->bhgnqk', qb, kb).astype(jnp.float32) * (HEAD_DIM ** -0.5)
    blk = jnp.arange(nb)[:, None, None]
    qpos = blk * BLOCK + jnp.arange(BLOCK)[None, :, None]
    kpos = blk * BLOCK - BLOCK + jnp.arange(3 * BLOCK)[None, None, :]
    valid = (jnp.abs(qpos - kpos) <= WINDOW) & (kpos >= 0) & (kpos < s)
    scores = jnp.where(valid, scores, -1e30)
    sink_logit = jnp.broadcast_to(
        sink.astype(jnp.float32).reshape(1, N_KV_HEADS, GQA_GROUP, 1, 1, 1), scores.shape[:-1] + (1,))
    probs = jax.nn.softmax(jnp.concatenate([scores, sink_logit], axis=-1), axis=-1)[..., :-1]
    out = jnp.einsum('bhgnqk,bnkhd->bnqhgd', probs.astype(v.dtype), vb)
    return out.reshape(b, s, ATTN_WIDTH)

def multiscale_pool(p, pool_w, pool_scale):
    b, s, _ = p.shape
    p32 = p.astype(jnp.float32)
    cs = jnp.concatenate([jnp.zeros((b, 1, POOL_WIDTH), jnp.float32), jnp.cumsum(p32, axis=1)], axis=1)
    t = jnp.arange(s)
    outs = []
    for gi, w in enumerate(POOL_SIZES):
        sl = slice(gi * POOL_GROUP, (gi + 1) * POOL_GROUP)
        lo = jnp.clip(t - w // 2, 0, s)
        hi = jnp.clip(t + w // 2, 0, s)
        cnt = (hi - lo).astype(jnp.float32)[None, :, None]
        csg = cs[..., sl]
        mean = (jnp.take(csg, hi, axis=1) - jnp.take(csg, lo, axis=1)) / cnt
        outs.append(mean - p32[..., sl])
    pooled = jnp.stack(outs, axis=2).astype(p.dtype)
    mixed = jnp.einsum('bsgc,gcd->bsgd', pooled, pool_w).reshape(b, s, POOL_WIDTH)
    return mixed * pool_scale

def token_mixer(u, w_in, b_gate, attn_sink, pool_w, pool_scale, w_br_attn, w_br_pool, w_out, cos, sin):
    b, s, _ = u.shape
    proj = u @ w_in
    splits = np.cumsum([ATTN_WIDTH, KV_WIDTH, KV_WIDTH, POOL_WIDTH, D_MODEL]).tolist()
    q, k, v, p, ga, gb = jnp.split(proj, splits, axis=-1)
    q = partial_rope(q.reshape(b, s, N_HEADS, HEAD_DIM), cos, sin)
    k = partial_rope(k.reshape(b, s, N_KV_HEADS, HEAD_DIM), cos, sin)
    v = v.reshape(b, s, N_KV_HEADS, HEAD_DIM)
    y_attn = windowed_gqa(q, k, v, attn_sink) @ w_br_attn
    y_pool = multiscale_pool(p, pool_w, pool_scale) @ w_br_pool
    gate_a = jax.nn.sigmoid(ga + b_gate[:D_MODEL])
    gate_b = jax.nn.sigmoid(gb + b_gate[D_MODEL:])
    return (gate_a * y_attn + gate_b * y_pool) @ w_out

def _w(key, shape, fan_in):
    return jax.random.normal(key, shape, jnp.float32) * (fan_in ** -0.5)

def _gain(key, shape):
    return 1.0 + 0.05 * jax.random.normal(key, shape, jnp.float32)

def second_inputs(seed: int = 0) -> dict:
    key = jax.random.key(seed)
    ks = jax.random.split(key, 22)
    L = DEPTH
    return {
        "x": jax.random.normal(ks[0], (BATCH, SEQ, D_MODEL), jnp.float32),
        "ffn1_norm": _gain(ks[1], (L, D_MODEL)),
        "ffn1_w1": _w(ks[2], (L, D_MODEL, D_FF), D_MODEL),
        "ffn1_w3": _w(ks[3], (L, D_MODEL, D_FF), D_MODEL),
        "ffn1_w2": _w(ks[4], (L, D_FF, D_MODEL), D_FF),
        "mix_norm": _gain(ks[5], (L, D_MODEL)),
        "w_in": _w(ks[6], (L, D_MODEL, IN_WIDTH), D_MODEL),
        "b_gate": 0.02 * jax.random.normal(ks[7], (L, N_BRANCHES * D_MODEL), jnp.float32),
        "attn_sink": 0.5 * jax.random.normal(ks[8], (L, N_HEADS), jnp.float32),
        "pool_w": _w(ks[9], (L, len(POOL_SIZES), POOL_GROUP, POOL_GROUP), POOL_GROUP),
        "pool_scale": _gain(ks[10], (L, POOL_WIDTH)),
        "w_branch_attn": _w(ks[11], (L, ATTN_WIDTH, D_MODEL), ATTN_WIDTH),
        "w_branch_pool": _w(ks[12], (L, POOL_WIDTH, D_MODEL), POOL_WIDTH),
        "w_out": _w(ks[13], (L, D_MODEL, D_MODEL), D_MODEL),
        "ffn2_norm": _gain(ks[14], (L, D_MODEL)),
        "ffn2_w1": _w(ks[15], (L, D_MODEL, D_FF), D_MODEL),
        "ffn2_w3": _w(ks[16], (L, D_MODEL, D_FF), D_MODEL),
        "ffn2_w2": _w(ks[17], (L, D_FF, D_MODEL), D_FF),
        "final_norm": _gain(ks[18], (D_MODEL,)),
    }

def second_block(x, ffn1_norm, ffn1_w1, ffn1_w3, ffn1_w2, mix_norm, w_in, b_gate, attn_sink, pool_w,
              pool_scale, w_branch_attn, w_branch_pool, w_out, ffn2_norm, ffn2_w1, ffn2_w3, ffn2_w2,
              final_norm):
    cos, sin = rope_tables(x.shape[1])
    h = x
    for l in range(DEPTH):
        h = h + 0.5 * swiglu(rms_norm_2(h, ffn1_norm[l]), ffn1_w1[l], ffn1_w3[l], ffn1_w2[l])
        h = h + token_mixer(rms_norm_2(h, mix_norm[l]), w_in[l], b_gate[l], attn_sink[l], pool_w[l],
                            pool_scale[l], w_branch_attn[l], w_branch_pool[l], w_out[l], cos, sin)
        h = h + 0.5 * swiglu(rms_norm_2(h, ffn2_norm[l]), ffn2_w1[l], ffn2_w3[l], ffn2_w2[l])
    return rms_norm_2(h, final_norm)


def setup_inputs(seed=0):
    out = dict(first_inputs(seed))
    for name, value in second_inputs(seed + 1).items():
        if name != "x":
            out[name + "_2"] = value
    return out


def reference(
    x, w_in, ret_gn_w, swa_sinks, mla_q_norm_w, mla_kv_norm_w, mla_w_uq, mla_w_ukv, w_out,
    ln1_g, ln1_b, router_w, router_bias, exp_w_gate_up, exp_w_down, ln2_g, ln2_b, ffn1_norm_2,
    ffn1_w1_2, ffn1_w3_2, ffn1_w2_2, mix_norm_2, w_in_2, b_gate_2, attn_sink_2, pool_w_2,
    pool_scale_2, w_branch_attn_2, w_branch_pool_2, w_out_2, ffn2_norm_2, ffn2_w1_2, ffn2_w3_2,
    ffn2_w2_2, final_norm_2,
):
    x = first_block(
        x, w_in, ret_gn_w, swa_sinks, mla_q_norm_w, mla_kv_norm_w, mla_w_uq, mla_w_ukv, w_out,
        ln1_g, ln1_b, router_w, router_bias, exp_w_gate_up, exp_w_down, ln2_g, ln2_b,
    )
    return second_block(
        x, ffn1_norm_2, ffn1_w1_2, ffn1_w3_2, ffn1_w2_2, mix_norm_2, w_in_2, b_gate_2,
        attn_sink_2, pool_w_2, pool_scale_2, w_branch_attn_2, w_branch_pool_2, w_out_2,
        ffn2_norm_2, ffn2_w1_2, ffn2_w3_2, ffn2_w2_2, final_norm_2,
    )


_drawn_inputs = setup_inputs


def setup_inputs(seed=0):
    import zlib

    import numpy as np

    out = dict(_drawn_inputs(seed))
    spreads = {}
    factors = {'ret_gn_w': 8.0,
     'swa_sinks': 8.0,
     'mla_q_norm_w': 5.607,
     'mla_kv_norm_w': 5.541,
     'b_gate_2': 8.0,
     'attn_sink_2': 23.925}
    for name, (base, spread) in spreads.items():
        noise = np.random.default_rng([zlib.crc32(name.encode()), seed]).standard_normal(out[name].shape)
        drawn = base * np.exp(spread * noise) if base else spread * noise
        out[name] = __import__('jax').numpy.asarray(drawn.astype(out[name].dtype))
    for name, factor in factors.items():
        out[name] = (out[name] * factor).astype(out[name].dtype)
    return out
```

```python
import numpy as np
import concourse.bass as bass
from concourse import mybir
from contextlib import ExitStack

F32 = mybir.dt.float32
F32R = mybir.dt.float32r
I32 = mybir.dt.int32
ACT = mybir.ActivationFunctionType
ALU = mybir.AluOpType
AX = mybir.AxisListType

P = 128
T = 256
NC = T // P
D = 1024
DK = D // P
DEPTH = 2
ALPHA = (2 * DEPTH) ** 0.25
LN_EPS, RMS_EPS, NEG = 1e-5, 1e-6, -1e30

RQ, RK, RV, RG, SQ, SK, SV, CQ, CKV, KR, IN1 = 0, 256, 512, 768, 1024, 1408, 1536, 1664, 2048, 2304, 2336
MQ = IN1
MV = MQ + 576
KCAT = CQ
RH, HD = 4, 64
SWH, SWG = 6, 2
MH, MD, MN, MR = 6, 96, 64, 32
NE, FE = 16, 256
NG, GE = 4, 4
AQ, AK, AV, PP, GA, GB, IN2 = 0, 512, 640, 768, 1280, 2304, 3328
AH, AG = 8, 2
NU2 = 2816 // FE
POOLS = (2, 4, 8, 16)

RING = 3
SLAB = 2048
BLOCKS1 = [(SV, 512), (CKV, 288), (SQ, 512), (RQ, 512), (RV, 512)]
S1_UQ, S1_UKV, S1_RQ, S1_OUT, S1_ROUTER, S1_MOE = 6, 8, 9, 13, 17, 18
S1 = S1_MOE + 3 * NE
S2_Q = 3 * NU2
S2_KV, S2_P, S2_GATE = S2_Q + 2, S2_Q + 3, S2_Q + 5
S2_BR = S2_GATE + 8
S2_OUT = S2_BR + 4
S2_FFN2 = S2_OUT + 4
S2 = S2_FFN2 + 3 * NU2
BASE2 = DEPTH * S1
assert S1 % RING == 0 and S2 % RING == 0

CONST = {}


def _constants():
    f = np.float32
    parts = []

    def put(name, a):
        a = np.ascontiguousarray(a, dtype=f).reshape(P, -1)
        CONST[name] = (sum(p.shape[1] for p in parts), a.shape[1])
        parts.append(a)

    def rotary(theta, d):
        inv = (f(theta) ** (-np.arange(0, d, 2, dtype=f) / f(d))).astype(f)
        ang = np.arange(T, dtype=f)[:, None] * inv[None]
        by_chunk = lambda t: t.reshape(NC, P, d // 2).transpose(1, 0, 2)
        return by_chunk(np.cos(ang)), by_chunk(np.sin(ang))

    put("ident", np.eye(P))
    i = np.arange(P)[:, None]
    j = np.arange(P)[None, :]
    put("m_tri", np.where(j <= i, 0, NEG))
    put("m_gt", np.where(j > i, 0, NEG))
    put("m_ge", np.where(j >= i, 0, NEG))
    put("m_zero", np.zeros((P, P)))
    put("before", np.where(i < j, 1, 0))
    put("ones", np.ones((P, P)))
    put("slot", np.broadcast_to(j, (P, P)))
    for name, theta, d in (("r64", 1e4, HD), ("r32", 1e4, MR), ("r16", 5e5, 16)):
        cos, sin = rotary(theta, d)
        put("cos_" + name, cos)
        put("sin_" + name, sin)
    put("rank16", np.broadcast_to(np.arange(16, 0, -1), (P, NC, 16)))
    put("rank4", np.broadcast_to(np.arange(4, 0, -1), (P, NC, 4)))
    common = sum(p.shape[1] for p in parts)
    gamma = 1.0 - 2.0 ** (-5.0 - np.arange(RH))
    rel = np.arange(T)[None, :] - np.arange(P)[:, None]
    dec = [np.where(rel >= 0, g ** np.maximum(rel, 0), 0) * HD ** -0.5 for g in gamma]
    first = np.stack([np.concatenate([x, x[:, :P]], 1) for x in dec], 1).reshape(P, -1)
    t = np.arange(T)
    mats = []
    for w in POOLS:
        lo, hi = np.clip(t - w // 2, 0, T), np.clip(t + w // 2, 0, T)
        s = np.arange(T)[:, None]
        mats.append(np.where((s >= lo) & (s < hi), 1.0 / (hi - lo), 0.0) - (s == t))
    second = np.stack(mats, 1).reshape(NC, P, len(POOLS), T).transpose(1, 0, 2, 3).reshape(P, -1)
    first = np.pad(first, ((0, 0), (0, second.shape[1] - first.shape[1])))
    return np.concatenate([np.concatenate(parts, 1), first, second], 1).astype(f), common, second.shape[1]


CONSTANTS, COMMON, PER_BLOCK = _constants()

JOBS1 = (
    [("T_swa", "copied")] * 3 + [("s_swa", "masked")] * 6
    + [("T_mla", "copied")] * 6 + [("T_ret", "copied")] * 2 + [("p_swa", "copied")] * 6
    + [("s_mla", "masked")] * 6 + [("s_ret", "weighted")] * 4 + [("o_swa", "mix_lo")] * 2
    + [("o_ret", "ret_out")] + [("p_mla", "copied")] * 6 + [("T_ro", "mix_lo")] + [("o_mla", "mix_lo")] * 2
)
JOBS2 = (
    [("T_qk", "copied")] * 3 + [("s", "masked")] * 8 + [("pool", "copied")] * 2 + [("p", "copied")] * 8
    + [("mixed", "mix_lo")] * 2 + [("o", "mix_lo")] * 2
)


def job_table(jobs):
    at, count, release = {}, {}, []
    for n, (name, signal) in enumerate(jobs):
        at.setdefault(name, n)
        count[signal] = count.get(signal, 0) + 1
        release.append((signal, count[signal]))
    return at, release


AT1, RELEASE1 = job_table(JOBS1)
AT2, RELEASE2 = job_table(JOBS2)


class Signal:

    def __init__(self, sem, per_layer, first=0):
        self.sem, self.per_layer, self.first = sem, per_layer, first

    def after(self, l, n):
        return l * self.per_layer + (n + self.first)


def program(nc, a, out):
    ctx = ExitStack()
    with ctx:
        def sb(name, shape, dt=F32):
            return ctx.enter_context(nc.sbuf_tensor("sb_" + name, shape, dt))

        def signal(name, per_layer=0, first=0):
            return Signal(ctx.enter_context(nc.semaphore(name)), per_layer, first)

        raw = [sb(f"raw{i}", [P, SLAB]) for i in range(RING)]
        whi = [sb(f"whi{i}", [P, SLAB], F32R) for i in range(RING)]
        wlo = [sb(f"wlo{i}", [P, SLAB], F32R) for i in range(RING)]
        x = sb("x", [P, NC, D])
        op_hi = sb("op_hi", [P, DK, T], F32R)
        op_lo = sb("op_lo", [P, DK, T], F32R)
        lat_hi = sb("lat_hi", [P, 5, T], F32R)
        lat_lo = sb("lat_lo", [P, 5, T], F32R)
        act_hi, act_lo = lat_hi[:, 0:2, :], lat_lo[:, 0:2, :]
        zero = sb("zero", [1, P], F32R)
        const = sb("const", [P, COMMON])
        per_block = sb("per_block", [P, PER_BLOCK])
        table = sb("table", [P, 2, D])
        rows_of = sb("rows_of", [35 * DEPTH, P])
        cols = sb("cols", [P, 35 * DEPTH])
        col1 = cols[:, 0:7 * DEPTH].rearrange("p (l n) -> p l n", l=DEPTH)
        col2 = cols[:, 7 * DEPTH:].rearrange("p (l n) -> p l n", l=DEPTH)
        cur1 = sb("cur1", [P, 7])
        cur2 = sb("cur2", [P, 28])
        sinks = sb("sinks", [P, DEPTH, 2 * SWH])
        sinks2 = sb("sinks2", [P, DEPTH, 2 * AH])
        nsink = sb("nsink", [P, 2 * AH])
        rbias = sb("rbias", [P, 16])
        poolw = sb("poolw", [P, 4, P])
        half = sb("half", [P, 16])
        small = sb("small", [P, 512])
        overflow = sb("overflow", [P, 1], I32)
        with ExitStack() as turn:
            proj = turn.enter_context(nc.sbuf_tensor("sb_proj", [P, NC, IN2], F32))
            arena = turn.enter_context(nc.sbuf_tensor("sb_arena", [P, 11584], F32))
        unit_work = sb("unit_work", [P, 2 * NC * FE])
        xg_hi, xg_lo = sb("xg_hi", [P, DK, NG, P], F32R), sb("xg_lo", [P, DK, NG, P], F32R)
        yg_hi, yg_lo = sb("yg_hi", [P, D], F32R), sb("yg_lo", [P, D], F32R)
        xs_hi, xs_lo = sb("xs_hi", [P, NC, D], F32R), sb("xs_lo", [P, NC, D], F32R)
        in_slot, of_slot = sb("in_slot", [P, NC, NG, P], F32R), sb("of_slot", [P, NG, T], F32R)

        def c(name):
            o, n = CONST[name]
            return const[:, o:o + n]

        ident = c("ident")

        def carve(start):
            def take(n):
                nonlocal start
                o, start = start, start + n
                assert start <= arena.shape[1]
                return arena[:, o:o + n]
            return take

        take = carve(0)
        swa_t = take(5 * T).rearrange("p (n t) -> p n t", t=T)
        mla_t = take(12 * T).rearrange("p (n t) -> p n t", t=T)
        ret_t = take(4 * T).rearrange("p (n t) -> p n t", t=T)
        ret_w = mla_t[:, 0:6, :].rearrange("p n t -> p (n t)").rearrange("p (h n) -> p h n", h=RH)
        s1 = take(2 * 1152).rearrange("p (b h n) -> p b h n", b=2, h=3)
        pt1 = take(2 * 1152).rearrange("p (b s h n) -> p b s h n", b=2, s=3, h=3)
        sk2 = take(512).rearrange("p (c g e d) -> p c g e d", c=NC, g=2, e=2)
        rot1, rot2 = take(512), take(512)
        ret_c = rot1.rearrange("p (c n) -> p c n", c=NC)
        ret_s = rot2.rearrange("p (c n) -> p c n", c=NC)
        take = carve(0)
        qk_t = take(6 * T).rearrange("p (n t) -> p n t", t=T)
        s2 = take(2 * 2048).rearrange("p (b h n) -> p b h n", b=2, h=4)
        pt2 = take(2 * 2048).rearrange("p (b s h n) -> p b s h n", b=2, s=4, h=4)
        pooled_t = take(4 * T).rearrange("p (n t) -> p n t", t=T)
        ak2 = take(512).rearrange("p (c g e d) -> p c g e d", c=NC, g=2, e=2)
        rot3, rot4 = take(160), take(160)
        sg, av = (unit_work[:, o:o + NC * FE].rearrange("p (c n) -> p c n", c=NC) for o in (0, NC * FE))

        def scratch():
            at = 0

            def take(n, *shape):
                nonlocal at
                v = small[:, at:at + n]
                at += n
                return v
            return take

        take = scratch()
        ssq, mla_rstd = take(4), take(4)
        negm, rsum = take(16), take(16)
        es, dsink = take(16), take(16)
        gn = take(8 * 3)
        stats = take(24).rearrange("p (c n) -> p c n", c=NC)
        mv = take(4).rearrange("p (c n) -> p c n", c=NC)
        lve = take(2)
        lrstd = take(2)
        scores = take(32).rearrange("p (c e) -> p c e", c=NC)
        biased = take(32).rearrange("p (c e) -> p c e", c=NC)
        pairs = take(48).rearrange("p (c g n) -> p c g n", c=NC, g=4)
        gscore = take(8).rearrange("p (c g) -> p c g", c=NC)
        gtop, ghot = take(2), take(8).rearrange("p (c g) -> p c g", c=NC)
        cand = take(32).rearrange("p (c e) -> p c e", c=NC)
        ctop = take(2)
        hot1 = take(32).rearrange("p (c e) -> p c e", c=NC)
        hot2 = take(32).rearrange("p (c e) -> p c e", c=NC)
        gates = take(32).rearrange("p (c e) -> p c e", c=NC)
        ss2, rms2, ss_raw1, ss_raw2 = take(2), take(2), take(4), take(2)
        rden = take(16)
        ghot_rank = take(8).rearrange("p (c g) -> p c g", c=NC)
        slot_of = take(2)
        slot_gates = take(16)

        bank = [ctx.enter_context(nc.psum_tensor(f"bank{i}", [P, 512], F32)) for i in range(8)]
        TPB = 4
        HB, AB = 4, 6

        def ybank(ch, n):
            return bank[2 * ch + n]

        x_loaded, consts_in, block2_in = signal("x_loaded"), signal("consts_in"), signal("block2_in")
        cols_in, set_up, cols_turned = signal("cols_in"), signal("set_up"), signal("cols_turned")
        stored = signal("stored")
        raw_in = [signal(f"raw_in{i}") for i in range(RING)]
        hi_made, lo_made, slab_done = signal("hi_made"), signal("lo_made"), signal("slab_done")
        F = {}
        for name, n, first in (
            ("x_ready", 2, 2), ("cur", 1, 0), ("opT", 8, 0), ("op_hi", 8, 0), ("op_lo", 8, 0),
            ("blk_c0", 5, 0), ("proj", 10, 0), ("ss_raw", 4, 0), ("ssq", 1, 0), ("rstd", 1, 0), ("latT", 3, 0),
            ("lat_hi", 3, 0), ("lat_lo", 3, 0), ("mla_q", 4, 0), ("mla_kv", 8, 0),
            ("sk2", 1, 0), ("mla_rot", 1, 0), ("ret_rot", 1, 0),
            ("job", len(JOBS1), 0), ("copied", 23, 0), ("masked", 12, 0), ("weighted", 4, 0),
            ("mix_hi", 5, 0), ("mix_lo", 5, 0), ("ret_out", 1, 0), ("negm", 4, 0), ("exped", 4, 0),
            ("probs", 4, 0), ("silu_g", 1, 0), ("ret_var", 1, 0), ("ret_rstd", 1, 0), ("ro", 1, 0),
            ("mix_c0", 1, 0), ("ln_var", 4, 0), ("ln_rstd", 4, 0), ("ln1", 2, 0), ("table", 64, 0),
            ("routed", 1, 0), ("router", 1, 0), ("h_c0", NE, 0), ("sg", 2 * NE, 0), ("a", 2 * NE, 0),
            ("aT", NE, 0), ("a_hi", NE, 0), ("a_lo", NE, 0), ("y", 2, 0),
            ("xs_hi", 2, 0), ("xs_lo", 2, 0), ("ghot", 1, 0), ("ranked", 1, 0), ("in_slot", 2, 0),
            ("gathered", 2 * DK, 0), ("xg_hi", DK, 0), ("xg_lo", DK, 0), ("gates", 1, 0),
            ("slot_gates", 1, 0), ("turned", 2, 0), ("of_slot", 2, 0), ("yg_hi", NG, 0), ("yg_lo", NG, 0),
        ):
            F[name] = signal("f_" + name, n, first)
        G = {}
        for name, n, first in (
            ("x_ready", 3, 1), ("cur", 1, 0), ("opT", 16, 0), ("op_hi", 16, 0), ("op_lo", 16, 0),
            ("ss", 3, 0), ("rstd", 3, 0), ("q_c0", 7, 0), ("proj", 6, 0), ("gate_in", 8, 0),
            ("gate", 4, 0), ("k_rot", 1, 0), ("rot", 1, 0), ("job", len(JOBS2), 0), ("copied", 13, 0),
            ("masked", 8, 0), ("mix_hi", 4, 0), ("mix_lo", 4, 0), ("negm", 2, 0), ("exped", 2, 0),
            ("probs", 2, 0), ("br_c0", 2, 0), ("gated", 8, 0), ("z", 2, 0), ("out_c0", 1, 0),
            ("bgate", 16, 0), ("poolw", 16, 0), ("ss_raw", 6, 0),
            ("h_c0", 2 * NU2, 0), ("sg", 4 * NU2, 0), ("a", 4 * NU2, 0),
            ("aT", 2 * NU2, 0), ("a_hi", 2 * NU2, 0), ("a_lo", 2 * NU2, 0), ("y_c0", 2, 0),
        ):
            G[name] = signal("g_" + name, n, first)
        final_ss, final_rstd, final_out = signal("final_ss"), signal("final_rstd"), signal("final_out")

        def slab_number(base, per_layer, l, j):
            return l * per_layer + (j + base)

        def split_hi(act, raw_count, number, slot, n=SLAB):
            act.wait_ge(raw_in[slot].sem, raw_count)
            act.wait_ge(slab_done.sem, number + 1)
            nc.scalar.activation(whi[slot][:, 0:n], raw[slot][:, 0:n], ACT.Copy).then_inc(hi_made.sem, 1)

        def split_lo(dve, number, slot, n=SLAB):
            dve.wait_ge(hi_made.sem, number + 1)
            nc.vector.tensor_tensor(wlo[slot][:, 0:n], raw[slot][:, 0:n], whi[slot][:, 0:n].bitcast(F32),
                                    ALU.subtract).then_inc(lo_made.sem, 1)

        def products(ps, hi, lo, wh, wl, first, last):
            nc.tensor.matmul(ps, hi, wh, start=first, stop=False)
            nc.tensor.matmul(ps, hi, wl, start=False, stop=False)
            return nc.tensor.matmul(ps, lo, wh, start=False, stop=last)

        WIDTH1 = {2: 4 * 288, 3: 4 * 288, 6: 3 * 288, 7: 3 * 288, 8: 2 * 768, S1_ROUTER: 128}

        def count1(l, j):
            return l * (32 * S1 // RING) + 32 * (j // RING + 1)

        def count2(l, j):
            return l * (32 * S2 // RING) + 32 * (BASE2 // RING + j // RING + 1)

        block = ctx.enter_context(nc.Block())

        @block.sync
        def _(sp):
            sp.dma_start(x[:], a["x"].rearrange("b (c p) d -> p (b c) d", p=P)).then_inc(x_loaded.sem, 16)
            sp.dma_start(const[:], a["constants"][:, 0:COMMON]).then_inc(consts_in.sem, 16)

            def load(number, slot, pieces):
                sp.wait_ge(lo_made.sem, number + 1)
                for dst, src in pieces:
                    sp.dma_start(dst, src).then_inc(raw_in[slot].sem, 16)

            def rows(w, l, r0, nk, c0, n, slot):
                v = raw[slot][:, 0:nk * n].rearrange("p (k n) -> p k n", n=n)
                s = w[bass.ds(l, 1), r0:r0 + nk * P, c0:c0 + n].rearrange("l (k p) n -> p (l k) n", p=P)
                h = (nk + 1) // 2
                return [(v[:, h:nk, :], s[:, h:nk, :]), (v[:, 0:h, :], s[:, 0:h, :])]

            with sp.Fori(0, DEPTH) as l:
                def put(j, w, r0, nk, c0, n):
                    load(slab_number(0, S1, l, j), j % RING, rows(w, l, r0, nk, c0, n, j % RING))

                for b, (c0, n) in enumerate(BLOCKS1[:3]):
                    for h in range(2):
                        put(2 * b + h, a["w_in"], 512 * h, 4, c0, n)
                for h in range(2):
                    put(S1_UQ + h, a["mla_w_uq"], 0, 3, 288 * h, 288)
                put(S1_UKV, a["mla_w_ukv"], 0, 2, 0, 768)
                for b, (c0, n) in enumerate(BLOCKS1[3:]):
                    for h in range(2):
                        put(S1_RQ + 2 * b + h, a["w_in"], 512 * h, 4, c0, n)
                for i, name in enumerate(("ln1_g", "ln1_b")):
                    sp.wait_ge(F["x_ready"].sem, F["x_ready"].after(l, 0))
                    sp.dma_start(table[:, i, :], a[name][bass.ds(l, 1), :].to_broadcast([P, D])).then_inc(F["table"].sem, 16)
                for i in range(4):
                    put(S1_OUT + i, a["w_out"], 512 * (i // 2), 4, 512 * (i % 2), 512)
                v = raw[S1_ROUTER % RING][:, 0:128].rearrange("p (k n) -> p k n", n=16)
                s = a["router_w"].rearrange("(k p) n -> p k n", p=P)
                load(slab_number(0, S1, l, S1_ROUTER), S1_ROUTER % RING, [(v[:, 4 * h:4 * h + 4, :], s[:, 4 * h:4 * h + 4, :]) for h in range(2)])

                def gate_up(number, j, e):
                    for h in range(2):
                        slot = (j + h) % RING
                        v = raw[slot][:, :].rearrange("p (k n) -> p k n", n=512)
                        s = a["exp_w_gate_up"][bass.ds(l, 1), bass.ds(e, 1), 512 * h:512 * h + 512, :].rearrange("l e (k p) n -> p (l e k) n", p=P)
                        load(number + h, slot, [(v[:, 2 * i:2 * i + 2, :], s[:, 2 * i:2 * i + 2, :]) for i in range(2)])

                def down(number, j, e):
                    slot = j % RING
                    v = raw[slot][:, :].rearrange("p (k n) -> p k n", n=D)
                    s = a["exp_w_down"][bass.ds(l, 1), bass.ds(e, 1), :, :].rearrange("l e (k p) n -> p (l e k) n", p=P)
                    load(number, slot, [(v[:, i:i + 1, :], s[:, i:i + 1, :]) for i in range(2)])

                gate_up(slab_number(0, S1, l, S1_MOE), S1_MOE, 0)
                for i, name in enumerate(("ln2_g", "ln2_b")):
                    sp.wait_ge(F["ln1"].sem, F["ln1"].after(l, 2))
                    sp.dma_start(table[:, i, :], a[name][bass.ds(l, 1), :].to_broadcast([P, D])).then_inc(F["table"].sem, 16)
                with sp.Fori(1, NE) as u:
                    j = u * 3 + (S1_MOE - 1)
                    gate_up(slab_number(0, S1, l, j), S1_MOE + 2, u)
                    down(slab_number(0, S1, l, j + 2), S1_MOE + 4, u - 1)
                j = S1 - 1
                down(slab_number(0, S1, l, j), j, NE - 1)

            def ffn(l, j0, w1, w3, w2):
                def up(number, j, u):
                    for h in range(2):
                        slot = (j + h) % RING
                        v = raw[slot][:, :].rearrange("p (k n) -> p k n", n=512)
                        load(number + h, slot, [
                            (v[:, :, FE * i:FE * i + FE],
                             w[bass.ds(l, 1), 512 * h:512 * h + 512, bass.ds(u * FE, FE)].rearrange("l (k p) n -> p (l k) n", p=P))
                            for i, w in enumerate((w1, w3))])

                def down(number, j, u):
                    slot = j % RING
                    v = raw[slot][:, :].rearrange("p (k n) -> p k n", n=D)
                    s = w2[bass.ds(l, 1), bass.ds(u * FE, FE), :].rearrange("l (k p) n -> p (l k) n", p=P)
                    load(number, slot, [(v[:, i:i + 1, :], s[:, i:i + 1, :]) for i in range(2)])

                up(slab_number(BASE2, S2, l, j0), j0, 0)
                with sp.Fori(1, NU2) as u:
                    j = u * 3 + (j0 - 1)
                    up(slab_number(BASE2, S2, l, j), j0 + 2, u)
                    down(slab_number(BASE2, S2, l, j + 2), j0 + 4, u - 1)
                j = j0 + 3 * NU2 - 1
                down(slab_number(BASE2, S2, l, j), j, NU2 - 1)

            with sp.Fori(0, DEPTH) as l:
                def put(j, w, r0, nk, c0, n):
                    load(slab_number(BASE2, S2, l, j), j % RING, rows(w, l, r0, nk, c0, n, j % RING))

                ffn(l, 0, a["ffn1_w1_2"], a["ffn1_w3_2"], a["ffn1_w2_2"])
                for h in range(2):
                    put(S2_Q + h, a["w_in_2"], 512 * h, 4, AQ, 512)
                put(S2_KV, a["w_in_2"], 0, 8, AK, 256)
                sp.wait_ge(G["x_ready"].sem, G["x_ready"].after(l, 0))
                sp.dma_start(table[:, :, :].rearrange("p b d -> p (b d)"), a["b_gate_2"][bass.ds(l, 1), :].to_broadcast([P, 2 * D])).then_inc(G["bgate"].sem, 16)
                sp.dma_start(poolw[:], a["pool_w_2"][bass.ds(l, 1), :, :, :].rearrange("l g c d -> c (l g) d")).then_inc(G["poolw"].sem, 16)
                for h in range(2):
                    put(S2_P + h, a["w_in_2"], 512 * h, 4, PP, 512)
                for b in range(4):
                    for h in range(2):
                        put(S2_GATE + 2 * b + h, a["w_in_2"], 512 * h, 4, GA + 512 * b, 512)
                for i, w in enumerate((a["w_branch_attn_2"], a["w_branch_pool_2"])):
                    for n in range(2):
                        put(S2_BR + 2 * i + n, w, 0, 4, 512 * n, 512)
                for i in range(4):
                    put(S2_OUT + i, a["w_out_2"], 512 * (i // 2), 4, 512 * (i % 2), 512)
                ffn(l, S2_FFN2, a["ffn2_w1_2"], a["ffn2_w3_2"], a["ffn2_w2_2"])
            for i in range(2):
                sp.wait_ge(lo_made.sem, BASE2 + DEPTH * S2 + i + 1)
                sp.sem_inc(raw_in[i].sem, 32)
            sp.dma_start(table[:, 0, :], a["final_norm_2"].rearrange("(o n) -> o n", o=1).to_broadcast([P, D])).then_inc(block2_in.sem, 16)
            for ch in range(NC):
                sp.wait_ge(final_out.sem, ch + 1)
                sp.dma_start(out[0, ch * P:ch * P + P, :], x[:, ch, :]).then_inc(stored.sem, 16)
            sp.wait_ge(stored.sem, 32)

        @block.gpsimd
        def _(pool):
            pool.dma_start(per_block[:], a["constants"][:, COMMON:COMMON + PER_BLOCK]).then_inc(cols_in.sem, 16)
            small_loads = [(rbias[:], a["router_bias"].rearrange("(o n) -> o n", o=1).to_broadcast([P, 16]))]
            for l in range(DEPTH):
                r1, r2 = 7 * l, 7 * DEPTH + 28 * l
                for r, name, n in ((r1, "mla_q_norm_w", 3), (r1 + 3, "mla_kv_norm_w", 2), (r1 + 5, "ret_gn_w", 2), (r2, "ffn1_norm_2", 8),
                                   (r2 + 8, "mix_norm_2", 8), (r2 + 16, "ffn2_norm_2", 8), (r2 + 24, "pool_scale_2", 4)):
                    small_loads.append((rows_of[r:r + n, :], a[name][l, :].rearrange("(k p) -> k p", p=P)))
            for l in range(DEPTH):
                for ch in range(NC):
                    small_loads.append((sinks[:, l, SWH * ch:SWH * ch + SWH], a["swa_sinks"][l:l + 1, :].to_broadcast([P, SWH])))
                    small_loads.append((sinks2[:, l, AH * ch:AH * ch + AH], a["attn_sink_2"][l:l + 1, :].to_broadcast([P, AH])))
            for dst, src in small_loads:
                pool.dma_start(dst, src).then_inc(cols_in.sem, 16)
            nc.gpsimd.memset(half[:], -0.5)
            nc.gpsimd.memset(zero[:].bitcast(F32), 0.0).then_inc(set_up.sem, 1)
            pool.sem_inc(lo_made.sem, RING)
            pool.sem_inc(slab_done.sem, RING)
            pool.wait_ge(x_loaded.sem, 16)
            pool.sem_inc(F["x_ready"].sem, 2)
            pool.wait_ge(cols_in.sem, 16 * (1 + len(small_loads)))
            pool.wait_ge(consts_in.sem, 16)
            pool.sem_inc(set_up.sem, 1)

            def rotate(x1, x2, cos, sin, t1, t2):
                tt = nc.gpsimd.tensor_tensor
                tt(t1, x1, sin, ALU.mult)
                tt(t2, x2, sin, ALU.mult)
                pool.drain()
                tt(x1, x1, cos, ALU.mult)
                tt(x2, x2, cos, ALU.mult)
                pool.drain()
                tt(x1, x1, t2, ALU.subtract)
                tt(x2, x2, t1, ALU.add)
                pool.drain()

            def heads(view, h, d, tab, n):
                return view.rearrange("p (h d) -> p h d", d=d)

            with pool.Fori(0, DEPTH) as l:
                pool.wait_ge(F["ssq"].sem, F["ssq"].after(l, 1))
                nc.gpsimd.tensor_tensor(mla_rstd, ssq, half[:, 0:4], ALU.pow).then_inc(F["rstd"].sem, 1)
                pool.wait_ge(F["proj"].sem, F["proj"].after(l, 6))
                for ch in range(NC):
                    src = proj[:, ch, SK:SK + 128].rearrange("p (g d) -> p g d", g=SWG)
                    for e in range(2):
                        nc.gpsimd.tensor_tensor(sk2[:, ch, :, e, :], src, c("m_zero").rearrange("p (g d) -> p g d", g=SWG), ALU.add)
                pool.drain()
                pool.sem_inc(F["sk2"].sem, 1)
                pool.wait_ge(F["mla_q"].sem, F["mla_q"].after(l, 4))
                pool.wait_ge(F["mla_kv"].sem, F["mla_kv"].after(l, 8))
                cs = [c(n + "_r32").rearrange("p (c d) -> p c d", c=NC) for n in ("cos", "sin")]
                for ch in range(NC):
                    q = proj[:, ch, MQ:MQ + 576].rearrange("p (h d) -> p h d", d=MD)
                    tabs = [t[:, ch:ch + 1, :].to_broadcast([P, MH, 16]) for t in cs]
                    tmp = [t[:, 0:96].rearrange("p (h d) -> p h d", d=16) for t in (rot1, rot2)]
                    rotate(q[:, :, 64:80], q[:, :, 80:96], *tabs, *tmp)
                    k = proj[:, ch, KR:KR + 32]
                    rotate(k[:, 0:16], k[:, 16:32], cs[0][:, ch, :], cs[1][:, ch, :], rot1[:, 0:16], rot2[:, 0:16])
                    dst = proj[:, ch, KCAT:KCAT + 576].rearrange("p (h d) -> p h d", d=MD)[:, :, 64:96]
                    nc.gpsimd.tensor_copy(dst, proj[:, ch:ch + 1, KR:KR + 32].to_broadcast([P, MH, 32]))
                pool.drain()
                pool.sem_inc(F["mla_rot"].sem, 1)
                pool.wait_ge(F["proj"].sem, F["proj"].after(l, 8))
                cs = [c(n + "_r64").rearrange("p (c d) -> p c d", c=NC) for n in ("cos", "sin")]
                for ch in range(NC):
                    qk = proj[:, ch, RQ:RQ + 512].rearrange("p (h d) -> p h d", d=HD)
                    tabs = [t[:, ch:ch + 1, :].to_broadcast([P, 8, 32]) for t in cs]
                    tmp = [t[:, 0:256].rearrange("p (h d) -> p h d", d=32) for t in (rot1, rot2)]
                    rotate(qk[:, :, 0:32], qk[:, :, 32:64], *tabs, *tmp)
                pool.sem_inc(F["ret_rot"].sem, 1)
                pool.wait_ge(F["ret_var"].sem, F["ret_var"].after(l, 1))
                nc.gpsimd.tensor_tensor(gn[:, 16:24], gn[:, 8:16], half[:, 0:8], ALU.pow).then_inc(F["ret_rstd"].sem, 1)
                for n in range(4):
                    pool.wait_ge(F["ln_var"].sem, F["ln_var"].after(l, n + 1))
                    nc.gpsimd.tensor_tensor(lrstd[:, n % 2:n % 2 + 1], lve[:, n % 2:n % 2 + 1], half[:, 0:1], ALU.pow).then_inc(F["ln_rstd"].sem, 1)

            pool.wait_ge(F["x_ready"].sem, F["x_ready"].after(DEPTH, 0))
            pool.sem_inc(G["x_ready"].sem, 1)
            pool.dma_start(per_block[:], a["constants"][:, COMMON + PER_BLOCK:]).then_inc(cols_in.sem, 16)
            pool.wait_ge(cols_in.sem, 16 * (2 + len(small_loads)))
            pool.sem_inc(set_up.sem, 1)

            def rms(l, stage):
                pool.wait_ge(G["ss"].sem, G["ss"].after(l, stage + 1))
                nc.gpsimd.tensor_tensor(rms2, ss2, half[:, 0:2], ALU.pow).then_inc(G["rstd"].sem, 1)

            with pool.Fori(0, DEPTH) as l:
                rms(l, 0)
                rms(l, 1)
                pool.wait_ge(G["proj"].sem, G["proj"].after(l, 4))
                cs = [c(n + "_r16").rearrange("p (c d) -> p c d", c=NC) for n in ("cos", "sin")]
                for ch in range(NC):
                    qk = proj[:, ch, AQ:AQ + 640].rearrange("p (h d) -> p h d", d=HD)
                    tabs = [t[:, ch:ch + 1, :].to_broadcast([P, 10, 8]) for t in cs]
                    tmp = [t[:, 0:80].rearrange("p (h d) -> p h d", d=8) for t in (rot3, rot4)]
                    rotate(qk[:, :, 0:8], qk[:, :, 8:16], *tabs, *tmp)
                    src = proj[:, ch, AK:AK + 128].rearrange("p (g d) -> p g d", g=AG)
                    for e in range(2):
                        nc.gpsimd.tensor_copy(ak2[:, ch, :, e, :], src)
                pool.drain()
                pool.sem_inc(G["rot"].sem, 1)
                rms(l, 2)
            pool.wait_ge(final_ss.sem, 1)
            nc.gpsimd.tensor_tensor(rms2, ss2, half[:, 0:2], ALU.pow).then_inc(final_rstd.sem, 1)

        @block.tensor
        def _(pe):
            pe.wait_ge(set_up.sem, 2)
            n = 35 * DEPTH
            nc.tensor.transpose(bank[0][:, 0:n], rows_of[:, :], ident[0:n, 0:n]).then_inc(cols_turned.sem, 1)

            def wait(S, name, l, n):
                pe.wait_ge(S[name].sem, S[name].after(l, n))

            def slab_ready(number):
                pe.wait_ge(lo_made.sem, number + 1 + RING)

            def tile(slot, n, k, c0, width):
                o = k * n + c0
                return whi[slot][:, o:o + width], wlo[slot][:, o:o + width]

            def slab(number, slot, n, tiles, dst, opening, closing, c0_signal=None, hi=op_hi, lo=op_lo, cols=None, k0=0):
                slab_ready(number)
                c0, width = cols or (0, n)
                for ch in range(NC):
                    for k, t in enumerate(tiles):
                        tok = slice(ch * P, ch * P + P)
                        i = products(dst(ch), hi[:, t, tok], lo[:, t, tok], *tile(slot, n, k0 + k, c0, width),
                                     opening and k == 0, closing and k == len(tiles) - 1)
                    if ch == 0 and c0_signal is not None:
                        i.then_inc(c0_signal.sem, 1)
                i.then_inc(slab_done.sem, 1)

            def transposes_c(S, src, ready):
                for ch in range(NC):
                    ready(ch)
                    for h in range(2):
                        for k in range(4):
                            o = (4 * h + k) * P
                            i = nc.tensor.transpose(bank[TPB + 2 * ch + h][:, k * P:k * P + P], src(ch, o), ident)
                        i.then_inc(S["opT"].sem, 1)

            def unit_up(number, slot, h_signal):
                slab(number, slot, 512, range(0, 4), lambda ch: bank[HB + ch][:, :], True, False)
                slab(number + 1, (slot + 1) % RING, 512, range(4, 8), lambda ch: bank[HB + ch][:, :], False, True, h_signal)

            def unit_transposes(S, l, before, n):
                pe.wait_ge(S["a"].sem, S["a"].after(l, 2 * n))
                for f in range(2):
                    for ch in range(NC):
                        i = nc.tensor.transpose(bank[AB][:, f * T + ch * P:f * T + ch * P + P], av[:, ch, f * P:f * P + P], ident)
                i.then_inc(S["aT"].sem, 1)

            def unit_down(S, l, number, slot, n, closing, c0_signal=None):
                pe.wait_ge(S["a_lo"].sem, S["a_lo"].after(l, n))
                slab_ready(number)
                for ch in range(NC):
                    for nh in range(2):
                        for k in range(2):
                            tok = slice(ch * P, ch * P + P)
                            i = products(ybank(ch, nh)[:, :], act_hi[:, k, tok], act_lo[:, k, tok],
                                         *tile(slot, D, k, 512 * nh, 512), False, closing and k == 1)
                    if ch == 0 and c0_signal is not None:
                        i.then_inc(c0_signal.sem, 1)
                i.then_inc(slab_done.sem, 1)

            def open_sums():
                for ch in range(NC):
                    for nh in range(2):
                        nc.tensor.matmul(ybank(ch, nh)[:, :], zero[0:1, :],
                                         op_hi[0:1, 0:2, :].rearrange("p a b -> p (a b)"), start=True, stop=False)

            def units(S, l, base, per_layer, j0, count, n0, y_c0):
                num = lambda j: slab_number(base, per_layer, l, j)
                unit_up(num(j0), j0 % RING, S["h_c0"])
                unit_transposes(S, l, 0, n0 + 1)
                with pe.Fori(1, count) as u:
                    j = u * 3 + (j0 - 1)
                    unit_up(num(j), (j0 + 2) % RING, S["h_c0"])
                    unit_down(S, l, num(j + 2), (j0 + 4) % RING, u + n0, False)
                    unit_transposes(S, l, 0, u + (n0 + 1))
                j = j0 + 3 * count - 1
                unit_down(S, l, num(j), j % RING, n0 + count, True, y_c0)

            class Jobs:

                def __init__(self, S, l, release):
                    self.S, self.l, self.release, self.n = S, l, release, 0

                def take(self):
                    n, self.n = self.n, self.n + 1
                    if n >= 4:
                        name, count = self.release[n - 4]
                        wait(self.S, name, self.l, count)
                    return bank[4 + n % 4]

                def done(self, i):
                    i.then_inc(self.S["job"].sem, 1)

            def transposed_tiles(jobs, tiles):
                for o in range(0, len(tiles), 2):
                    b = jobs.take()
                    for n, view in enumerate(tiles[o:o + 2]):
                        for ch in range(NC):
                            v = view(ch)
                            i = nc.tensor.transpose(b[0:v.shape[1], n * T + ch * P:n * T + ch * P + P], v, ident)
                    jobs.done(i)

            with pe.Fori(0, DEPTH) as l:
                jobs = Jobs(F, l, RELEASE1)
                num = lambda j: slab_number(0, S1, l, j)
                transposes_c(F, lambda ch, o: x[:, ch, o:o + P], lambda ch: wait(F, "x_ready", l, ch + 1 - 2))
                wait(F, "op_lo", l, 4)

                def block1(b, j):
                    n = BLOCKS1[b][1]
                    at = 2 * (b % 2)
                    for h in range(2):
                        slab(num(j + h), (j + h) % RING, n, range(4 * h, 4 * h + 4), lambda ch: bank[at + ch][:, 0:n],
                             h == 0, h == 1, F["blk_c0"] if h else None)

                block1(0, 0)
                block1(1, 2)
                wait(F, "proj", l, 4)
                for t in range(5):
                    o = CQ + t * P
                    for ch in range(NC):
                        i = nc.tensor.transpose(bank[4 + t // 2][:, (t % 2) * T + ch * P:(t % 2) * T + ch * P + P], proj[:, ch, o:o + P], ident)
                    if t % 2 or t == 4:
                        i.then_inc(F["latT"].sem, 1)
                block1(2, 4)
                wait(F, "lat_lo", l, 3)
                for h in range(2):
                    slab(num(S1_UQ + h), (S1_UQ + h) % RING, 288, range(3), lambda ch: bank[2 + 2 * h + ch][:, 0:288], True, True, None, lat_hi, lat_lo)
                wait(F, "proj", l, 6)
                slab_ready(num(S1_UKV))
                for h in range(2):
                    for ch in range(NC):
                        dst = (bank[6 + ch] if h == 0 else bank[ch])[:, 0:384]
                        for k in range(2):
                            tok = slice(ch * P, ch * P + P)
                            i = products(dst, lat_hi[:, 3 + k, tok], lat_lo[:, 3 + k, tok], *tile(S1_UKV % RING, 768, k, 384 * h, 384), k == 0, k == 1)
                i.then_inc(slab_done.sem, 1)
                wait(F, "sk2", l, 1)
                wait(F, "mla_q", l, 4)
                wait(F, "mla_kv", l, 8)
                transposed_tiles(jobs, [lambda ch, t=t: proj[:, ch, SQ + t * P:SQ + t * P + P] for t in range(3)]
                                 + [lambda ch, g=g: sk2[:, ch, g, :, :].rearrange("p e d -> p (e d)") for g in range(2)])
                block1(3, S1_RQ)

                def softmax_scores(q, k, group, width):
                    for qc, kc in ((0, 0), (1, 0), (1, 1)):
                        b = jobs.take()
                        for h in range(3):
                            i = nc.tensor.matmul(b[:, h * P:h * P + P], q(2 * h + group, qc), k(2 * h + group, kc), start=True, stop=True)
                        jobs.done(i)

                def probs_transposed(S, group, s, nseg, nh):
                    wait(S, "probs", l, group + 1)
                    for seg in range(nseg):
                        b = jobs.take()
                        for h in range(nh):
                            i = nc.tensor.transpose(b[:, h * P:h * P + P], s[:, group % 2, h, seg * P:seg * P + P], ident)
                        jobs.done(i)

                def head_outputs(pairs, value, probs, tiles):
                    for o in range(0, len(tiles), 2):
                        b = jobs.take()
                        for n, t in enumerate(tiles[o:o + 2]):
                            for e in range(2):
                                h = 2 * t + e
                                r = slice(e * HD, e * HD + HD)
                                nc.tensor.matmul(b[r, n * T:n * T + T], value(h, 0), probs(h, slice(0, 2)), start=True, stop=False)
                                i = nc.tensor.matmul(b[r, n * T + P:n * T + T], value(h, 1), probs(h, 2), start=False, stop=True)
                        jobs.done(i)

                def swa_q(h, ch):
                    r = HD * (h % 2)
                    return swa_t[r:r + HD, h // 2, ch * P:ch * P + P]

                def swa_k(h, ch):
                    r = HD * (h % 2)
                    return swa_t[r:r + HD, 3 + h // 3, ch * P:ch * P + P]

                wait(F, "copied", l, 3)
                for g in range(2):
                    softmax_scores(swa_q, swa_k, g, HD)
                block1(4, S1_RQ + 2)
                wait(F, "mla_rot", l, 1)
                mq = [lambda ch, h=h: proj[:, ch, MQ + MD * h:MQ + MD * h + MD] for h in range(MH)]
                mk = [lambda ch, h=h: proj[:, ch, KCAT + MD * h:KCAT + MD * h + MD] for h in range(MH)]
                transposed_tiles(jobs, mq + mk)
                wait(F, "ret_rot", l, 1)
                transposed_tiles(jobs, [lambda ch, t=t: proj[:, ch, RQ + t * P:RQ + t * P + P] for t in range(4)])
                for g in range(2):
                    probs_transposed(F, g, s1, 3, 3)
                wait(F, "copied", l, 11)
                for g in range(2):
                    softmax_scores(lambda h, ch: mla_t[0:MD, h, ch * P:ch * P + P],
                                   lambda h, ch: mla_t[0:MD, MH + h, ch * P:ch * P + P], g, MD)
                for h in range(RH):
                    b = jobs.take()
                    r = slice(HD * (h % 2), HD * (h % 2) + HD)
                    q, k = ret_t[r, h // 2, :], ret_t[r, 2 + h // 2, :]
                    nc.tensor.matmul(b[:, 0:T], k[:, 0:P], q, start=True, stop=True)
                    jobs.done(nc.tensor.matmul(b[:, T:T + P], k[:, P:T], q[:, P:T], start=True, stop=True))
                wait(F, "copied", l, 17)
                head_outputs(3, lambda h, kc: proj[:, kc, SV + HD * (h // 3):SV + HD * (h // 3) + HD],
                             lambda h, s: pt1[:, h % 2, s, h // 2, :], range(3))
                wait(F, "weighted", l, 4)
                b = jobs.take()
                for ch in range(NC):
                    for h in range(RH):
                        o = b[:, ch * T + h * HD:ch * T + h * HD + HD]
                        v = [proj[:, kc, RV + h * HD:RV + h * HD + HD] for kc in range(NC)]
                        i = nc.tensor.matmul(o, ret_w[:, h, ch * P:ch * P + P], v[0], start=True, stop=ch == 0)
                        if ch:
                            i = nc.tensor.matmul(o, ret_w[:, h, T:T + P], v[1], start=False, stop=True)
                jobs.done(i)
                for g in range(2):
                    wait(F, "probs", l, 3 + g)
                    for seg in range(3):
                        b = jobs.take()
                        for h in range(3):
                            i = nc.tensor.transpose(b[:, h * P:h * P + P], s1[:, g, h, seg * P:seg * P + P], ident)
                        jobs.done(i)
                wait(F, "ro", l, 1)
                transposed_tiles(jobs, [lambda ch, t=t: ret_c[:, ch, t * P:t * P + P] for t in range(2)])
                wait(F, "copied", l, 23)
                head_outputs(3, lambda h, kc: proj[:, kc, MV + HD * h:MV + HD * h + HD],
                             lambda h, s: pt1[:, h % 2, s, h // 2, :], range(3))
                wait(F, "proj", l, 10)
                wait(F, "mix_lo", l, 3)
                for i in range(4):
                    if i == 2:
                        wait(F, "mix_lo", l, 5)
                    h, nh = i // 2, i % 2
                    slab(num(S1_OUT + i), (S1_OUT + i) % RING, 512, range(4 * h, 4 * h + 4), lambda ch: ybank(ch, nh)[:, :],
                         h == 0, h == 1, F["mix_c0"] if i == 3 else None)
                transposes_c(F, lambda ch, o: x[:, ch, o:o + P], lambda ch: wait(F, "ln1", l, ch + 1))
                wait(F, "op_lo", l, 8)
                slab_ready(num(S1_ROUTER))
                for ch in range(NC):
                    for k in range(DK):
                        tok = slice(ch * P, ch * P + P)
                        i = products(bank[7][:, 16 * ch:16 * ch + 16], op_hi[:, k, tok], op_lo[:, k, tok],
                                     *tile(S1_ROUTER % RING, 16, k, 0, 16), k == 0, k == DK - 1)
                i.then_inc(slab_done.sem, 1)

                wait(F, "ghot", l, 1)
                b = bank[6]
                before, ones = c("before"), c("ones")
                nc.tensor.matmul(b[:, 0:4], before, ghot[:, 0, :], start=True, stop=True)
                for o, last in ((4, before), (8, ones)):
                    nc.tensor.matmul(b[:, o:o + 4], ones, ghot[:, 0, :], start=True, stop=False)
                    i = nc.tensor.matmul(b[:, o:o + 4], last, ghot[:, 1, :], start=False, stop=True)
                i.then_inc(F["ranked"].sem, 1)
                wait(F, "xs_lo", l, 2)
                wait(F, "in_slot", l, 2)
                for n in range(2 * DK):
                    k = n // 2
                    if n >= 4:
                        wait(F, "xg_lo" if n % 2 else "xg_hi", l, k - 1)
                    src = xs_lo if n % 2 else xs_hi
                    for ch in range(NC):
                        i = nc.tensor.matmul(bank[4 + n % 4][:, :], src[:, ch, k * P:k * P + P],
                                             in_slot[:, ch, :, :].rearrange("p g n -> p (g n)"), start=ch == 0, stop=ch == 1)
                    i.then_inc(F["gathered"].sem, 1)
                open_sums()
                size = pe.value_load(overflow[0:1, 0:1], min_val=0, max_val=T)

                def expert_up(number, slot, g):
                    for h in range(2):
                        slab_ready(number + h)
                        for k in range(4):
                            hi, lo = xg_hi[:, 4 * h + k, g, :], xg_lo[:, 4 * h + k, g, :]
                            i = products(bank[HB][:, :], hi, lo, *tile((slot + h) % RING, 512, k, 0, 512), h == 0 and k == 0, h == 1 and k == 3)
                        i.then_inc(slab_done.sem, 1)

                def expert_turn(u):
                    wait(F, "a", l, u * 2 + 2)
                    for f in range(2):
                        i = nc.tensor.transpose(bank[5][:, f * P:f * P + P], av[:, 0, f * P:f * P + P], ident)
                    i.then_inc(F["aT"].sem, 1)

                def expert_down(u, e):
                    j = S1_MOE + 3 * u + 4 if u < NE - 1 else S1 - 1
                    wait(F, "a_lo", l, u + 1)
                    slab_ready(num(j))
                    for nh in range(2):
                        for k in range(2):
                            i = products(bank[6 + nh][:, :], act_hi[:, k, 0:P], act_lo[:, k, 0:P], *tile(j % RING, D, k, 512 * nh, 512),
                                         e == 0 and k == 0, e == GE - 1 and k == 1)
                    i.then_inc(slab_done.sem, 1)

                def scatter(g, n, closing):
                    wait(F, "yg_lo", l, n)
                    for ch in range(NC):
                        for nh in range(2):
                            to = of_slot[:, g, ch * P:ch * P + P]
                            cols = slice(512 * nh, 512 * nh + 512)
                            nc.tensor.matmul(ybank(ch, nh)[:, :], to, yg_hi[:, cols], start=False, stop=False)
                            i = nc.tensor.matmul(ybank(ch, nh)[:, :], to, yg_lo[:, cols], start=False, stop=closing)
                        if closing:
                            i.then_inc(F["y"].sem, 1)

                with pe.If(size > P):
                    wait(F, "xg_lo", l, DK)
                    wait(F, "xg_hi", l, DK)
                    units(F, l, 0, S1, S1_MOE, NE, 0, F["y"])
                    pe.drain()
                    pe.sem_inc(F["y"].sem, 1)
                    pe.sem_inc(F["slot_gates"].sem, 1)
                    pe.sem_inc(F["turned"].sem, 2)
                with pe.Else():
                    up_number = lambda u: slab_number(0, S1, l, u * 3 + (S1_MOE - 1))
                    wait(F, "xg_lo", l, DK)
                    wait(F, "xg_hi", l, DK)
                    expert_up(num(S1_MOE), S1_MOE % RING, 0)
                    wait(F, "gates", l, 1)
                    for g in range(NG):
                        for ch in range(NC):
                            i = nc.tensor.matmul(bank[5][:, GE * g:GE * g + GE], in_slot[:, ch, g, :].bitcast(F32), gates[:, ch, GE * g:GE * g + GE], start=ch == 0, stop=ch == 1)
                    i.then_inc(F["slot_gates"].sem, 1)
                    for n in range(2):
                        for g in range(2):
                            for ch in range(NC):
                                i = nc.tensor.transpose(bank[6 + n][:, g * T + ch * P:g * T + ch * P + P], in_slot[:, ch, 2 * n + g, :].bitcast(F32), ident)
                        i.then_inc(F["turned"].sem, 1)
                    expert_turn(0)
                    for e in range(1, GE):
                        expert_up(up_number(e), (S1_MOE + 2) % RING, 0)
                        if e == 1:
                            wait(F, "of_slot", l, 2)
                        expert_down(e - 1, e - 1)
                        expert_turn(e)
                    for g in range(1, NG):
                        for e in range(GE):
                            u = g * GE + e
                            expert_up(up_number(u), (S1_MOE + 2) % RING, g)
                            if e == 1:
                                wait(F, "yg_lo", l, g)
                            expert_down(u - 1, (e - 1) % GE)
                            expert_turn(u)
                            if e == 1:
                                scatter(g - 1, g, False)
                    expert_down(NE - 1, GE - 1)
                    scatter(NG - 1, NG, True)
                    pe.sem_inc(F["h_c0"].sem, NE)

            with pe.Fori(0, DEPTH) as l:
                jobs = Jobs(G, l, RELEASE2)
                num = lambda j: slab_number(BASE2, S2, l, j)

                def transposes_k(stage):
                    if stage == 0:
                        wait(G, "x_ready", l, 0)
                    else:
                        wait(G, "x_ready", l, stage)
                    for n in range(4):
                        for k in range(2):
                            for ch in range(NC):
                                o = (2 * n + k) * P
                                i = nc.tensor.transpose(bank[TPB + n][:, k * T + ch * P:k * T + ch * P + P], x[:, ch, o:o + P], ident)
                        i.then_inc(G["opT"].sem, 1)

                pe.wait_ge(set_up.sem, 3)
                transposes_k(0)
                wait(G, "op_lo", l, 4)
                open_sums()
                units(G, l, BASE2, S2, 0, NU2, 0, G["y_c0"])

                transposes_k(1)
                wait(G, "op_lo", l, 8)

                def block2(b, j, at):
                    for h in range(2):
                        slab(num(j + h), (j + h) % RING, 512, range(4 * h, 4 * h + 4), lambda ch: bank[at + ch][:, :],
                             h == 0, h == 1, G["q_c0"] if h else None)

                block2(0, S2_Q, 0)
                slab(num(S2_KV), S2_KV % RING, 256, range(8), lambda ch: bank[2 + ch][:, 0:256], True, True, G["q_c0"])
                wait(G, "proj", l, 2)
                block2(2, S2_P, 0)
                wait(G, "rot", l, 1)
                transposed_tiles(jobs, [lambda ch, t=t: proj[:, ch, AQ + t * P:AQ + t * P + P] for t in range(4)]
                                 + [lambda ch, g=g: ak2[:, ch, g, :, :].rearrange("p e d -> p (e d)") for g in range(2)])
                block2(3, S2_GATE, 2)

                def scores2(g):
                    for qc, kc in ((0, 0), (0, 1), (1, 0), (1, 1)):
                        b = jobs.take()
                        for n in range(4):
                            r = slice(HD * g, HD * g + HD)
                            i = nc.tensor.matmul(b[:, n * P:n * P + P], qk_t[r, n, qc * P:qc * P + P],
                                                 qk_t[r, 4 + n // 2, kc * P:kc * P + P], start=True, stop=True)
                        jobs.done(i)

                wait(G, "copied", l, 3)
                scores2(0)
                wait(G, "proj", l, 6)
                block2(4, S2_GATE + 2, 0)
                scores2(1)
                for o in range(0, 4, 2):
                    b = jobs.take()
                    for n in range(2):
                        g = o + n
                        for kc in range(NC):
                            mat = per_block[:, (kc * 4 + g) * T:(kc * 4 + g) * T + T]
                            i = nc.tensor.matmul(b[:, n * T:n * T + T], proj[:, kc, PP + g * P:PP + g * P + P], mat, start=kc == 0, stop=kc == 1)
                    jobs.done(i)
                wait(G, "gate_in", l, 2)
                block2(5, S2_GATE + 4, 2)

                def probs2(g):
                    wait(G, "probs", l, g + 1)
                    for seg in range(4):
                        b = jobs.take()
                        for n in range(4):
                            i = nc.tensor.transpose(b[:, n * P:n * P + P], s2[:, g, n, seg * P:seg * P + P], ident)
                        jobs.done(i)

                probs2(0)
                wait(G, "gate_in", l, 4)
                block2(6, S2_GATE + 6, 0)
                probs2(1)
                wait(G, "poolw", l, 16)
                wait(G, "copied", l, 5)
                for o in range(0, 4, 2):
                    b = jobs.take()
                    for n in range(2):
                        i = nc.tensor.matmul(b[:, n * T:n * T + T], poolw[:, o + n, :], pooled_t[:, o + n, :], start=True, stop=True)
                    jobs.done(i)
                wait(G, "copied", l, 13)
                for o in range(0, 4, 2):
                    b = jobs.take()
                    for n in range(2):
                        for e in range(2):
                            h = 2 * (o + n) + e
                            r = slice(e * HD, e * HD + HD)
                            v = [proj[:, kc, AV + HD * (h // 4):AV + HD * (h // 4) + HD] for kc in range(NC)]
                            pt = pt2[:, e, :, o + n, :]
                            nc.tensor.matmul(b[r, n * T:n * T + T], v[0], pt[:, 0:4:2, :], start=True, stop=False)
                            i = nc.tensor.matmul(b[r, n * T:n * T + T], v[1], pt[:, 1:4:2, :], start=False, stop=True)
                    jobs.done(i)
                wait(G, "gate_in", l, 8)
                wait(G, "mix_lo", l, 4)
                for nh in range(2):
                    slab(num(S2_BR + nh), (S2_BR + nh) % RING, 512, range(4), lambda ch: ybank(ch, nh)[:, :], True, True, G["br_c0"] if nh else None)
                for nh in range(2):
                    slab(num(S2_BR + 2 + nh), (S2_BR + 2 + nh) % RING, 512, range(4), lambda ch: bank[4 + 2 * ch + nh][:, :], True, True,
                         G["br_c0"] if nh else None, k0=0, hi=op_hi[:, 4:8, :], lo=op_lo[:, 4:8, :])
                for ch in range(NC):
                    wait(G, "z", l, ch + 1)
                    for h in range(2):
                        for k in range(4):
                            o = GA + (4 * h + k) * P
                            i = nc.tensor.transpose(ybank(ch, h)[:, k * P:k * P + P], proj[:, ch, o:o + P], ident)
                        i.then_inc(G["opT"].sem, 1)
                wait(G, "op_lo", l, 12)
                for i in range(4):
                    h, nh = i // 2, i % 2
                    slab(num(S2_OUT + i), (S2_OUT + i) % RING, 512, range(4 * h, 4 * h + 4), lambda ch: bank[4 + 2 * ch + nh][:, :],
                         h == 0, h == 1, G["out_c0"] if i == 3 else None)

                transposes_k(2)
                wait(G, "op_lo", l, 16)
                open_sums()
                units(G, l, BASE2, S2, S2_FFN2, NU2, NU2, G["y_c0"])

        @block.scalar
        def _(act):
            act.wait_ge(set_up.sem, 2)

            def wait(S, name, l, n):
                act.wait_ge(S[name].sem, S[name].after(l, n))

            def hi1(l, j):
                n = l * S1 + j
                split_hi(act, count1(l, j), n, j % RING, WIDTH1.get(j, SLAB))

            def hi2(l, j):
                split_hi(act, count2(l, j), slab_number(BASE2, S2, l, j), j % RING)

            def units_hi(S, l, base, per_layer, j0, count, n0, col):
                num = lambda j: slab_number(base, per_layer, l, j)
                ring = per_layer // RING

                def ahead(j_fixed, u):
                    split_hi(act, l * (32 * ring) + u * 32 + 32 * (base // RING + j_fixed // RING + 1),
                             l * per_layer + u * 3 + (base + j_fixed), j_fixed % RING)

                def silu(u, last_slab):
                    for ch in range(NC):
                        if ch == 0:
                            wait(S, "h_c0", l, u + (n0 + 1))
                        else:
                            act.wait_ge(slab_done.sem, last_slab + 1 + RING)
                        nc.scalar.activation(sg[:, ch, :], bank[HB + ch][:, 0:FE], ACT.Silu,
                                             scale=1.0 if col is None else col(ch)).then_inc(S["sg"].sem, 1)

                ahead(j0 + 3, 0)
                silu(0, num(j0 + 1))
                ahead(j0 + 4, 0)
                with act.Fori(1, count) as u:
                    j = u * 3 + (j0 - 1)
                    wait(S, "aT", l, u + n0)
                    nc.scalar.activation(act_hi[:, :, :].rearrange("p f t -> p (f t)"), bank[AB][:, :], ACT.Copy).then_inc(S["a_hi"].sem, 1)
                    ahead(j0 + 2, u)
                    silu(u, num(j + 1))
                    ahead(j0 + 3, u)
                    ahead(j0 + 4, u)
                wait(S, "aT", l, n0 + count)
                nc.scalar.activation(act_hi[:, :, :].rearrange("p f t -> p (f t)"), bank[AB][:, :], ACT.Copy).then_inc(S["a_hi"].sem, 1)

            def operand_hi_c(S, l, n0, banks):
                for n in range(4):
                    ch, h = n // 2, n % 2
                    wait(S, "opT", l, n0[0] + n + 1)
                    nc.scalar.activation(op_hi[:, 4 * h:4 * h + 4, ch * P:ch * P + P], bank[banks + n][:, :].rearrange("p (k t) -> p k t", k=4),
                                         ACT.Copy).then_inc(S["op_hi"].sem, 1)

            hi1(0, 0)
            hi1(0, 1)
            with act.Fori(0, DEPTH) as l:
                def block_out(b, j):
                    c0, n = BLOCKS1[b]
                    at = 2 * (b % 2)
                    for ch in range(NC):
                        if ch == 0:
                            wait(F, "blk_c0", l, b + 1)
                        else:
                            act.wait_ge(slab_done.sem, slab_number(0, S1, l, j + 1) + 1 + RING)
                        nc.scalar.activation(proj[:, ch, c0:c0 + n], bank[at + ch][:, 0:n], ACT.Copy).then_inc(F["proj"].sem, 1)

                def copies(dst, n0, count0):
                    for n, (d, rows, width) in enumerate(dst):
                        wait(F, "job", l, n0 + n + 1)
                        nc.scalar.activation(d, bank[4 + (n0 + n) % 4][0:rows, 0:width], ACT.Copy).then_inc(F["copied"].sem, 1)

                def exps(group, sinks_of):
                    wait(F, "negm", l, group + 1)
                    b = group % 2
                    for ch in range(NC):
                        seg = slice(0, P) if ch == 0 else slice(P, 3 * P)
                        for h in range(3):
                            m = ch * 3 + h + 8 * b
                            i = nc.scalar.activation(s1[:, b, h, seg], s1[:, b, h, seg], ACT.Exp, bias=negm[:, m:m + 1], accum_out=rsum[:, m:m + 1])
                    if sinks_of:
                        i = nc.scalar.activation(es[:, 8 * b:8 * b + 6], dsink[:, 8 * b:8 * b + 6], ACT.Exp)
                    i.then_inc(F["exped"].sem, 1)

                def mix_hi(n, job, t0, nt, scales=None):
                    wait(F, "job", l, job + 1)
                    b = bank[4 + job % 4]
                    if scales is None:
                        i = nc.scalar.activation(op_hi[:, t0:t0 + nt, :].rearrange("p k t -> p (k t)"), b[:, 0:nt * T], ACT.Copy)
                    else:
                        for k in range(nt):
                            i = nc.scalar.activation(op_hi[:, t0 + k, :], b[:, k * T:k * T + T], ACT.Copy, scale=scales[:, k:k + 1])
                    i.then_inc(F["mix_hi"].sem, 1)

                operand_hi_c(F, l, (0,), TPB)
                hi1(l, 2)
                hi1(l, 3)
                block_out(0, 0)
                hi1(l, 4)
                hi1(l, 5)
                block_out(1, 2)
                for n, (c0, w) in enumerate(((CQ, 384), (CKV, 256))):
                    for ch in range(NC):
                        act.drain()
                        nc.scalar.activation(rot1[:, 0:w], proj[:, ch, c0:c0 + w], ACT.Square, accum_out=ss_raw1[:, 2 * n + ch:2 * n + ch + 1]).then_inc(F["ss_raw"].sem, 1)
                wait(F, "cur", l, 1)
                for n, tiles in enumerate(((0, 1), (2, 3), (4,))):
                    wait(F, "latT", l, n + 1)
                    for t in tiles:
                        i = nc.scalar.activation(lat_hi[:, t, :], bank[4 + n][:, (t % 2) * T:(t % 2) * T + T], ACT.Copy, scale=cur1[:, t:t + 1])
                    i.then_inc(F["lat_hi"].sem, 1)
                hi1(l, 6)
                block_out(2, 4)
                hi1(l, 7)
                hi1(l, 8)
                wait(F, "rstd", l, 1)
                for h in range(2):
                    act.wait_ge(slab_done.sem, slab_number(0, S1, l, S1_UQ + h) + 1 + RING)
                    for ch in range(NC):
                        nc.scalar.activation(proj[:, ch, MQ + 288 * h:MQ + 288 * h + 288], bank[2 + 2 * h + ch][:, 0:288], ACT.Copy,
                                             scale=mla_rstd[:, ch:ch + 1]).then_inc(F["mla_q"].sem, 1)
                    hi1(l, 9 + h)
                act.wait_ge(slab_done.sem, slab_number(0, S1, l, S1_UKV) + 1 + RING)
                for h in range(2):
                    for ch in range(NC):
                        kv = (bank[6 + ch] if h == 0 else bank[ch])[:, 0:384].rearrange("p (h d) -> p h d", d=128)
                        kd = proj[:, ch, KCAT + 288 * h:KCAT + 288 * h + 288].rearrange("p (h d) -> p h d", d=MD)[:, :, 0:MN]
                        vd = proj[:, ch, MV + 192 * h:MV + 192 * h + 192].rearrange("p (h d) -> p h d", d=HD)
                        for d, s in ((kd, kv[:, :, 0:MN]), (vd, kv[:, :, MN:128])):
                            nc.scalar.activation(d, s, ACT.Copy, scale=mla_rstd[:, 2 + ch:3 + ch]).then_inc(F["mla_kv"].sem, 1)
                hi1(l, 11)
                flat = lambda t, o, n: t[:, o:o + n, :].rearrange("p n t -> p (n t)")
                copies([(flat(swa_t, 0, 2), P, 2 * T), (flat(swa_t, 2, 2), P, 2 * T), (swa_t[:, 4, :], P, T)], 0, 0)
                hi1(l, 12)
                block_out(3, S1_RQ)
                exps(0, True)
                block_out(4, S1_RQ + 2)
                copies([(mla_t[0:MD, 2 * n:2 * n + 2, :].rearrange("p n t -> p (n t)"), MD, 2 * T) for n in range(6)], AT1["T_mla"], 3)
                exps(1, True)
                copies([(flat(ret_t, 2 * n, 2), P, 2 * T) for n in range(2)], AT1["T_ret"], 9)
                copies([(pt1[:, g, s, :, :].rearrange("p h n -> p (h n)"), P, 384) for g in range(2) for s in range(3)], AT1["p_swa"], 11)
                hi1(l, 13)
                exps(2, False)
                hi1(l, 14)
                mix_hi(0, AT1["o_swa"], 2, 2)
                mix_hi(1, AT1["o_swa"] + 1, 4, 1)
                exps(3, False)
                nc.scalar.activation(proj[:, :, RG:RG + 256], proj[:, :, RG:RG + 256], ACT.Silu).then_inc(F["silu_g"].sem, 1)
                hi1(l, 15)
                copies([(pt1[:, g, s, :, :].rearrange("p h n -> p (h n)"), P, 384) for g in range(2) for s in range(3)], AT1["p_mla"], 17)
                mix_hi(2, AT1["T_ro"], 0, 2, cur1[:, 5:7])
                mix_hi(3, AT1["o_mla"], 5, 2)
                mix_hi(4, AT1["o_mla"] + 1, 7, 1)
                hi1(l, 16)
                hi1(l, 17)
                hi1(l, 18)
                operand_hi_c(F, l, (4,), TPB)
                for ch in range(NC):
                    nc.scalar.activation(xs_hi[:, ch, :], x[:, ch, :], ACT.Copy).then_inc(F["xs_hi"].sem, 1)
                hi1(l, 19)
                act.wait_ge(slab_done.sem, slab_number(0, S1, l, S1_ROUTER) + 1 + RING)
                nc.scalar.activation(scores.rearrange("p c e -> p (c e)"), bank[7][:, 0:32], ACT.Sigmoid).then_inc(F["routed"].sem, 1)
                hi1(l, 20)
                for k in range(DK):
                    wait(F, "gathered", l, 2 * k + 1)
                    nc.scalar.activation(xg_hi[:, k, :, :].rearrange("p g n -> p (g n)"), bank[4 + 2 * k % 4][:, :], ACT.Copy).then_inc(F["xg_hi"].sem, 1)
                size = act.value_load(overflow[0:1, 0:1], min_val=0, max_val=T)

                def ahead(j_fixed, u):
                    split_hi(act, l * (32 * S1 // RING) + u * 32 + 32 * (j_fixed // RING + 1), l * S1 + u * 3 + j_fixed, j_fixed % RING)

                def expert_silu(u, last_slab):
                    act.wait_ge(slab_done.sem, last_slab + 1 + RING)
                    nc.scalar.activation(sg[:, 0, :], bank[HB][:, 0:FE], ACT.Silu).then_inc(F["sg"].sem, 2)

                def expert_hi(n):
                    wait(F, "aT", l, n)
                    nc.scalar.activation(act_hi[:, :, 0:P], bank[5][:, 0:2 * P].rearrange("p (f n) -> p f n", f=2), ACT.Copy).then_inc(F["a_hi"].sem, 1)

                def group_hi(last_slab):
                    act.wait_ge(slab_done.sem, last_slab + 1 + RING)
                    for nh in range(2):
                        i = nc.scalar.activation(yg_hi[:, 512 * nh:512 * nh + 512], bank[6 + nh][:, :], ACT.Copy)
                    i.then_inc(F["yg_hi"].sem, 1)

                with act.If(size > P):
                    units_hi(F, l, 0, S1, S1_MOE, NE, 0, None)
                    act.sem_inc(F["of_slot"].sem, 2)
                    act.sem_inc(F["yg_hi"].sem, NG)
                with act.Else():
                    number = lambda j: slab_number(0, S1, l, j)

                    def expert(u, group_end):
                        expert_hi(u)
                        ahead(S1_MOE + 2, u)
                        expert_silu(u, number(u * 3 + S1_MOE))
                        if group_end:
                            group_hi(number(u * 3 + (S1_MOE + 1)))
                        ahead(S1_MOE + 3, u)
                        ahead(S1_MOE + 4, u)

                    ahead(S1_MOE + 3, 0)
                    expert_silu(0, number(S1_MOE + 1))
                    for n in range(2):
                        wait(F, "turned", l, n + 1)
                        nc.scalar.activation(of_slot[:, 2 * n:2 * n + 2, :].rearrange("p g t -> p (g t)"), bank[6 + n][:, :], ACT.Copy).then_inc(F["of_slot"].sem, 1)
                    ahead(S1_MOE + 4, 0)
                    for e in range(1, GE):
                        expert(e, False)
                    with act.Fori(1, NG) as g:
                        for e in range(GE):
                            expert(g * GE + e, e == 0)
                    expert_hi(NE)
                    group_hi(number(S1 - 1))

            with act.Fori(0, DEPTH) as l:
                def squares(stage):
                    for ch in range(NC):
                        act.drain()
                        if stage == 0:
                            wait(G, "x_ready", l, 0)
                        nc.scalar.activation(proj[:, ch, GA:GA + D], x[:, ch, :], ACT.Square, accum_out=ss_raw2[:, ch:ch + 1]).then_inc(G["ss_raw"].sem, 1)

                def operand_hi_k(stage):
                    for n in range(4):
                        wait(G, "opT", l, (0, 4, 12)[stage] + n + 1)
                        for k in range(2):
                            t = 2 * n + k
                            i = nc.scalar.activation(op_hi[:, t, :], bank[TPB + n][:, k * T:k * T + T], ACT.Copy,
                                                     scale=cur2[:, 8 * stage + t:8 * stage + t + 1])
                        i.then_inc(G["op_hi"].sem, 1)

                def column(ch):
                    return rms2[:, ch:ch + 1]

                wait(G, "cur", l, 1)
                operand_hi_k(0)
                squares(0)
                hi2(l, 2)
                wait(G, "rstd", l, 1)
                units_hi(G, l, BASE2, S2, 0, NU2, 0, column)

                operand_hi_k(1)
                squares(1)
                hi2(l, S2_Q + 2)
                hi2(l, S2_Q + 3)
                wait(G, "rstd", l, 2)

                def block_out(b, j, c0, n, at):
                    for ch in range(NC):
                        if ch == 0:
                            wait(G, "q_c0", l, b + 1)
                        else:
                            act.wait_ge(slab_done.sem, slab_number(BASE2, S2, l, j) + 1 + RING)
                        nc.scalar.activation(proj[:, ch, c0:c0 + n], bank[at + ch][:, 0:n], ACT.Copy, scale=column(ch)).then_inc(G["proj"].sem, 1)

                def copies(dst, n0):
                    for n, (d, width) in enumerate(dst):
                        wait(G, "job", l, n0 + n + 1)
                        nc.scalar.activation(d, bank[4 + (n0 + n) % 4][:, 0:width], ACT.Copy).then_inc(G["copied"].sem, 1)

                def exps(g):
                    wait(G, "negm", l, g + 1)
                    for ch in range(NC):
                        for h in range(4):
                            m = 8 * g + 4 * ch + h
                            seg = slice(ch * T, ch * T + T)
                            nc.scalar.activation(s2[:, g, h, seg], s2[:, g, h, seg], ACT.Exp, bias=negm[:, m:m + 1], accum_out=rsum[:, m:m + 1])
                    nc.scalar.activation(es[:, 8 * g:8 * g + 8], dsink[:, 8 * g:8 * g + 8], ACT.Exp).then_inc(G["exped"].sem, 1)

                def gate(b):
                    wait(G, "gate_in", l, 2 * b + 2)
                    o = GA + 512 * b
                    nc.scalar.activation(proj[:, :, o:o + 512], proj[:, :, o:o + 512], ACT.Sigmoid).then_inc(G["gate"].sem, 1)

                block_out(0, S2_Q + 1, AQ, 512, 0)
                hi2(l, S2_Q + 4)
                block_out(1, S2_KV, AK, 256, 2)
                hi2(l, S2_Q + 5)
                hi2(l, S2_Q + 6)
                block_out(2, S2_P + 1, PP, 512, 0)
                flat = lambda t, o, n: t[:, o:o + n, :].rearrange("p n t -> p (n t)")
                copies([(flat(qk_t, 2 * n, 2), 2 * T) for n in range(3)], AT2["T_qk"])
                hi2(l, S2_Q + 7)
                hi2(l, S2_Q + 8)
                hi2(l, S2_Q + 9)
                exps(0)
                hi2(l, S2_Q + 10)
                exps(1)
                copies([(flat(pooled_t, 2 * n, 2), 2 * T) for n in range(2)], AT2["pool"])
                copies([(pt2[:, 0, s, :, :].rearrange("p h n -> p (h n)"), 512) for s in range(4)], AT2["p"])
                hi2(l, S2_Q + 11)
                hi2(l, S2_Q + 12)
                copies([(pt2[:, 1, s, :, :].rearrange("p h n -> p (h n)"), 512) for s in range(4)], AT2["p"] + 4)
                hi2(l, S2_Q + 13)
                hi2(l, S2_Q + 14)
                for n in range(2):
                    job = AT2["mixed"] + n
                    wait(G, "job", l, job + 1)
                    for k in range(2):
                        t = 2 * n + k
                        i = nc.scalar.activation(op_hi[:, 4 + t, :], bank[4 + job % 4][:, k * T:k * T + T], ACT.Copy, scale=cur2[:, 24 + t:25 + t])
                    i.then_inc(G["mix_hi"].sem, 1)
                for n in range(2):
                    job = AT2["o"] + n
                    wait(G, "job", l, job + 1)
                    nc.scalar.activation(op_hi[:, 2 * n:2 * n + 2, :].rearrange("p k t -> p (k t)"), bank[4 + job % 4][:, :], ACT.Copy).then_inc(G["mix_hi"].sem, 1)
                for b in range(4):
                    gate(b)
                hi2(l, S2_Q + 15)
                hi2(l, S2_Q + 16)
                hi2(l, S2_Q + 17)
                hi2(l, S2_Q + 18)
                operand_hi_c(G, l, (8,), 0)
                hi2(l, S2_Q + 19)
                hi2(l, S2_Q + 20)
                hi2(l, S2_Q + 21)
                hi2(l, S2_Q + 22)

                operand_hi_k(2)
                squares(2)
                hi2(l, S2_FFN2 + 2)
                wait(G, "rstd", l, 3)
                units_hi(G, l, BASE2, S2, S2_FFN2, NU2, NU2, column)
            for ch in range(NC):
                act.wait_ge(G["x_ready"].sem, G["x_ready"].after(DEPTH, 0))
                act.drain()
                nc.scalar.activation(proj[:, ch, GA:GA + D], x[:, ch, :], ACT.Square, accum_out=ss_raw2[:, ch:ch + 1]).then_inc(G["ss_raw"].sem, 1)

        @block.vector
        def _(dve):
            tt, ts, stt = nc.vector.tensor_tensor, nc.vector.tensor_scalar, nc.vector.scalar_tensor_tensor
            dve.wait_ge(set_up.sem, 2)
            dve.wait_ge(cols_turned.sem, 1)
            nc.vector.tensor_copy(cols[:], bank[0][:, 0:35 * DEPTH])
            dve.drain()

            def wait(S, name, l, n):
                dve.wait_ge(S[name].sem, S[name].after(l, n))

            def lo1(l, j):
                split_lo(dve, l * S1 + j, j % RING, WIDTH1.get(j, SLAB))

            def lo2(l, j):
                split_lo(dve, slab_number(BASE2, S2, l, j), j % RING)

            def slab_is_done(number):
                dve.wait_ge(slab_done.sem, number + 1 + RING)

            def units_lo(S, l, base, per_layer, j0, count, n0, col):
                def ahead(j_fixed, u):
                    split_lo(dve, l * per_layer + u * 3 + (base + j_fixed), j_fixed % RING)

                def activations(u):
                    for ch in range(NC):
                        wait(S, "sg", l, u * 2 + (2 * n0 + ch + 1))
                        stt(out=av[:, ch, :], in0=bank[HB + ch][:, FE:2 * FE], scalar=col(u, ch), in1=sg[:, ch, :],
                            op0=ALU.mult, op1=ALU.mult).then_inc(S["a"].sem, 1)

                def lo_part(n):
                    wait(S, "a_hi", l, n)
                    tt(act_lo[:, :, :].rearrange("p f t -> p (f t)"), bank[AB][:, :],
                       act_hi[:, :, :].rearrange("p f t -> p (f t)").bitcast(F32), ALU.subtract).then_inc(S["a_lo"].sem, 1)

                ahead(j0 + 3, 0)
                activations(0)
                ahead(j0 + 4, 0)
                with dve.Fori(1, count) as u:
                    lo_part(u + n0)
                    ahead(j0 + 2, u)
                    activations(u)
                    ahead(j0 + 3, u)
                    ahead(j0 + 4, u)
                lo_part(n0 + count)

            def operand_lo_c(S, l, n0, banks):
                for n in range(4):
                    ch, h = n // 2, n % 2
                    wait(S, "op_hi", l, n0 + n + 1)
                    part = (slice(None), slice(4 * h, 4 * h + 4), slice(ch * P, ch * P + P))
                    tt(op_lo[part], bank[banks + n][:, :].rearrange("p (k t) -> p k t", k=4), op_hi[part].bitcast(F32),
                       ALU.subtract).then_inc(S["op_lo"].sem, 1)

            def row_max(dst, src):
                nc.vector.tensor_reduce(dst, src, axis=AX.X, op=ALU.max, negate=True)

            lo1(0, 0)
            lo1(0, 1)
            with dve.Fori(0, DEPTH) as l:
                nc.vector.tensor_copy(cur1[:], col1[:, bass.ds(l, 1), :].rearrange("p l n -> p (l n)"))
                ts(nsink[:, 0:12], sinks[:, bass.ds(l, 1), :].rearrange("p l n -> p (l n)"), -1.0, None, ALU.mult).then_inc(F["cur"].sem, 1)
                operand_lo_c(F, l, 0, TPB)
                for j in range(2, 6):
                    lo1(l, j)
                wait(F, "ss_raw", l, 4)
                ts(ssq[:, 0:2], ss_raw1[:, 0:2], 1.0 / 384, RMS_EPS, ALU.mult, ALU.add)
                ts(ssq[:, 2:4], ss_raw1[:, 2:4], 1.0 / 256, RMS_EPS, ALU.mult, ALU.add).then_inc(F["ssq"].sem, 1)
                for n, tiles in enumerate(((0, 1), (2, 3), (4,))):
                    wait(F, "lat_hi", l, n + 1)
                    for t in tiles:
                        i = stt(out=lat_lo[:, t, :], in0=bank[4 + n][:, (t % 2) * T:(t % 2) * T + T], scalar=cur1[:, t:t + 1],
                                in1=lat_hi[:, t, :].bitcast(F32), op0=ALU.mult, op1=ALU.subtract)
                    i.then_inc(F["lat_lo"].sem, 1)
                for j in range(6, 13):
                    lo1(l, j)

                def masked(group, job, scale, masks):
                    b = group % 2
                    for seg in range(3):
                        n = job + 3 * b + seg
                        wait(F, "job", l, n + 1)
                        m = c(masks[seg]).unsqueeze(1).to_broadcast([P, 3, P])
                        stt(out=s1[:, b, :, seg * P:seg * P + P], in0=bank[4 + n % 4][:, 0:384].rearrange("p (h n) -> p h n", h=3),
                            scalar=scale, in1=m, op0=ALU.mult, op1=ALU.add).then_inc(F["masked"].sem, 1)
                    dve.drain()
                    o = 8 * b
                    row_max(negm[:, o:o + 3], s1[:, b, :, 0:P])
                    nc.vector.tensor_reduce(negm[:, o + 3:o + 6], s1[:, b, :, P:3 * P], axis=AX.X, op=ALU.max, negate=True) \
                        if group < 2 else \
                        nc.vector.tensor_reduce(negm[:, o + 3:o + 6], s1[:, b, :, P:3 * P], axis=AX.X, op=ALU.max, negate=True).then_inc(F["negm"].sem, 1)
                    if group < 2:
                        dve.drain()
                        by = lambda t: t.rearrange("p (c h) -> p c h", c=NC)
                        m, ns = by(negm[:, o:o + 6]), nsink[:, 0:12].rearrange("p (c h e) -> p c h e", c=NC, e=2)[:, :, :, group]
                        tt(m, m, ns, ALU.min)
                        dve.drain()
                        tt(by(dsink[:, o:o + 6]), m, ns, ALU.subtract).then_inc(F["negm"].sem, 1)

                def probs(group):
                    b = group % 2
                    o = 8 * b
                    wait(F, "exped", l, group + 1)
                    if group < 2:
                        tt(rsum[:, o:o + 6], rsum[:, o:o + 6], es[:, o:o + 6], ALU.add)
                        dve.drain()
                    nc.vector.reciprocal(rden[:, o:o + 6], rsum[:, o:o + 6])
                    dve.drain()
                    for seg, k in ((slice(0, P), 0), (slice(P, 3 * P), 3)):
                        v = s1[:, b, :, seg]
                        i = tt(v, v, rden[:, o + k:o + k + 3].unsqueeze(2).to_broadcast([P, 3, seg.stop - seg.start]), ALU.mult)
                    i.then_inc(F["probs"].sem, 1)

                def mix_lo(n, job, t0, nt, scaled=False):
                    wait(F, "mix_hi", l, n + 1)
                    b = bank[4 + job % 4]
                    if not scaled:
                        flat = lambda t: t[:, t0:t0 + nt, :].rearrange("p k t -> p (k t)")
                        i = tt(flat(op_lo), b[:, 0:nt * T], flat(op_hi).bitcast(F32), ALU.subtract)
                    else:
                        for k in range(nt):
                            i = stt(out=op_lo[:, t0 + k, :], in0=b[:, k * T:k * T + T], scalar=cur1[:, 5 + k:6 + k],
                                    in1=op_hi[:, t0 + k, :].bitcast(F32), op0=ALU.mult, op1=ALU.subtract)
                    i.then_inc(F["mix_lo"].sem, 1)

                for g in range(2):
                    masked(g, AT1["s_swa"], HD ** -0.5, ("m_tri", "m_gt", "m_tri"))
                probs(0)
                probs(1)
                lo1(l, 13)
                for g in range(2):
                    masked(2 + g, AT1["s_mla"], MD ** -0.5, ("m_tri", "m_zero", "m_tri"))
                lo1(l, 14)
                decay = per_block[:, 0:RH * 384].rearrange("p (h n) -> p h n", h=RH)
                for h in range(RH):
                    n = AT1["s_ret"] + h
                    wait(F, "job", l, n + 1)
                    tt(ret_w[:, h, :], bank[4 + n % 4][:, 0:384], decay[:, h, :], ALU.mult).then_inc(F["weighted"].sem, 1)
                mix_lo(0, AT1["o_swa"], 2, 2)
                mix_lo(1, AT1["o_swa"] + 1, 4, 1)
                probs(2)
                probs(3)
                n = AT1["o_ret"]
                wait(F, "job", l, n + 1)
                heads = lambda t: t.rearrange("p (h d) -> p h d", d=HD)
                by_head = lambda o: gn[:, o:o + 8].unsqueeze(2).to_broadcast([P, 8, HD])
                o = heads(bank[4 + n % 4][:, :])
                nc.vector.tensor_reduce(gn[:, 0:8], o, axis=AX.X, op=ALU.add)
                dve.drain()
                ts(gn[:, 0:8], gn[:, 0:8], 1.0 / HD, None, ALU.mult)
                dve.drain()
                tt(heads(rot1), o, by_head(0), ALU.subtract).then_inc(F["ret_out"].sem, 1)
                dve.drain()
                tt(rot2, rot1, rot1, ALU.mult)
                dve.drain()
                nc.vector.tensor_reduce(gn[:, 8:16], heads(rot2), axis=AX.X, op=ALU.add)
                dve.drain()
                ts(gn[:, 8:16], gn[:, 8:16], 1.0 / HD, LN_EPS, ALU.mult, ALU.add).then_inc(F["ret_var"].sem, 1)
                wait(F, "ret_rstd", l, 1)
                tt(heads(rot1), heads(rot1), by_head(16), ALU.mult)
                dve.drain()
                wait(F, "silu_g", l, 1)
                tt(ret_c, ret_c, proj[:, :, RG:RG + 256], ALU.mult).then_inc(F["ro"].sem, 1)
                lo1(l, 15)
                mix_lo(2, AT1["T_ro"], 0, 2, True)
                mix_lo(3, AT1["o_mla"], 5, 2)
                mix_lo(4, AT1["o_mla"] + 1, 7, 1)
                lo1(l, 16)
                lo1(l, 17)
                lo1(l, 18)

                def layer_norm(n0, there, done):
                    for ch in range(NC):
                        there(ch)
                        for nh in range(2):
                            v = x[:, ch, 512 * nh:512 * nh + 512]
                            stt(out=v, in0=v, scalar=ALPHA, in1=ybank(ch, nh)[:, :], op0=ALU.mult, op1=ALU.add)
                        dve.drain()
                        for nh in range(2):
                            nc.vector.bn_stats(stats[:, ch, 6 * nh:6 * nh + 6], x[:, ch, 512 * nh:512 * nh + 512])
                        dve.drain()
                        nc.vector.bn_aggr(mv[:, ch, :], stats[:, ch, :])
                        dve.drain()
                        ts(lve[:, ch:ch + 1], mv[:, ch, 1:2], LN_EPS, None, ALU.add).then_inc(F["ln_var"].sem, 1)
                    wait(F, "table", l, 16 * (n0 + 2))
                    for ch in range(NC):
                        wait(F, "ln_rstd", l, n0 + ch + 1)
                        stt(out=x[:, ch, :], in0=x[:, ch, :], scalar=mv[:, ch, 0:1], in1=table[:, 0, :], op0=ALU.subtract, op1=ALU.mult)
                        dve.drain()
                        stt(out=x[:, ch, :], in0=x[:, ch, :], scalar=lrstd[:, ch:ch + 1], in1=table[:, 1, :],
                            op0=ALU.mult, op1=ALU.add).then_inc(F[done].sem, 1)

                def mixed(ch):
                    if ch == 0:
                        wait(F, "mix_c0", l, 1)
                    else:
                        slab_is_done(slab_number(0, S1, l, S1_OUT + 3))

                layer_norm(0, mixed, "ln1")
                operand_lo_c(F, l, 4, TPB)
                for ch in range(NC):
                    wait(F, "xs_hi", l, ch + 1)
                    tt(xs_lo[:, ch, :], x[:, ch, :], xs_hi[:, ch, :].bitcast(F32), ALU.subtract).then_inc(F["xs_lo"].sem, 1)
                lo1(l, 19)

                wait(F, "routed", l, 1)

                def step(i):
                    dve.drain()

                def wide(t, n):
                    return t.unsqueeze(2).to_broadcast([P, NC, n])

                group = lambda t: t.rearrange("p c (g n) -> p c g n", g=4)
                step(tt(biased, scores, rbias[:].unsqueeze(1).to_broadcast([P, NC, 16]), ALU.add))
                bg = group(biased)
                for o, n in ((0, 1), (3, 2), (5, 3)):
                    i = tt(pairs[:, :, :, o:o + 4 - n], bg[:, :, :, 0:4 - n], bg[:, :, :, n:4], ALU.add)
                step(i)
                step(nc.vector.tensor_reduce(gscore, pairs, axis=AX.X, op=ALU.max))

                def first_best(hot, values, rank, width):
                    cd = cand[:, :, 0:width]
                    step(nc.vector.tensor_reduce(gtop, values, axis=AX.X, op=ALU.max))
                    step(tt(cd, values, wide(gtop, width), ALU.is_equal))
                    step(tt(cd, cd, rank, ALU.mult))
                    step(nc.vector.tensor_reduce(ctop, cd, axis=AX.X, op=ALU.max))
                    step(tt(hot, cd, wide(ctop, width), ALU.is_equal))

                first_best(ghot, gscore, c("rank4").rearrange("p (c g) -> p c g", c=NC), 4)
                dve.sem_inc(F["ghot"].sem, 1)
                wait(F, "ranked", l, 1)
                step(tt(ghot_rank, ghot, bank[6][:, 0:8].rearrange("p (c g) -> p c g", c=NC), ALU.mult))
                nc.vector.tensor_reduce(ctop[:, 0:1], bank[6][:, 8:12], axis=AX.X, op=ALU.max)
                step(nc.vector.tensor_reduce(slot_of, ghot_rank, axis=AX.X, op=ALU.add))
                nc.vector.tensor_copy(overflow[:], ctop[:, 0:1])
                for ch in range(NC):
                    for g in range(NG):
                        i = ts(in_slot[:, ch, g, :], c("slot"), slot_of[:, ch:ch + 1], ghot[:, ch, g:g + 1], ALU.is_equal, ALU.mult)
                    i.then_inc(F["in_slot"].sem, 1)
                for k in range(DK):
                    wait(F, "gathered", l, 2 * k + 2)
                    nc.vector.tensor_copy(xg_lo[:, k, :, :].rearrange("p g n -> p (g n)"), bank[4 + (2 * k + 1) % 4][:, :]).then_inc(F["xg_lo"].sem, 1)
                in_group = lambda t: t.unsqueeze(3).to_broadcast([P, NC, 4, 4])
                tt(bg, bg, in_group(ghot), ALU.mult)
                step(ts(gscore, ghot, -NEG, NEG, ALU.mult, ALU.add))
                step(tt(bg, bg, in_group(gscore), ALU.add))
                rank = c("rank16").rearrange("p (c e) -> p c e", c=NC)
                first_best(hot1, biased, rank, 16)
                step(stt(out=biased, in0=hot1, scalar=2 * NEG, in1=biased, op0=ALU.mult, op1=ALU.add))
                first_best(hot2, biased, rank, 16)
                step(tt(hot1, hot1, hot2, ALU.add))
                step(tt(gates, scores, hot1, ALU.mult))
                step(nc.vector.tensor_reduce(gtop, gates, axis=AX.X, op=ALU.add))
                step(nc.vector.reciprocal(ctop, gtop))
                tt(gates, gates, wide(ctop, 16), ALU.mult).then_inc(F["gates"].sem, 1)
                dve.drain()
                lo1(l, 20)
                size = dve.value_load(overflow[0:1, 0:1], min_val=0, max_val=T)

                def ahead(j_fixed, u):
                    split_lo(dve, l * S1 + u * 3 + j_fixed, j_fixed % RING)

                def expert_act(u, gate):
                    wait(F, "sg", l, u * 2 + 2)
                    stt(out=av[:, 0, :], in0=bank[HB][:, FE:2 * FE], scalar=gate, in1=sg[:, 0, :], op0=ALU.mult, op1=ALU.mult).then_inc(F["a"].sem, 2)

                def expert_lo(n):
                    wait(F, "a_hi", l, n)
                    tt(act_lo[:, :, 0:P], bank[5][:, 0:2 * P].rearrange("p (f n) -> p f n", f=2), act_hi[:, :, 0:P].bitcast(F32),
                       ALU.subtract).then_inc(F["a_lo"].sem, 1)

                def group_lo(n):
                    wait(F, "yg_hi", l, n)
                    for nh in range(2):
                        cols_of = slice(512 * nh, 512 * nh + 512)
                        i = tt(yg_lo[:, cols_of], bank[6 + nh][:, :], yg_hi[:, cols_of].bitcast(F32), ALU.subtract)
                    i.then_inc(F["yg_lo"].sem, 1)

                with dve.If(size > P):
                    units_lo(F, l, 0, S1, S1_MOE, NE, 0, lambda u, ch: gates[:, ch, bass.ds(u, 1)])
                    dve.sem_inc(F["yg_lo"].sem, NG)
                with dve.Else():
                    def expert(u, groups_done):
                        expert_lo(u)
                        ahead(S1_MOE + 2, u)
                        expert_act(u, slot_gates[:, bass.ds(u, 1)])
                        if groups_done is not None:
                            group_lo(groups_done)
                        ahead(S1_MOE + 3, u)
                        ahead(S1_MOE + 4, u)

                    ahead(S1_MOE + 3, 0)
                    wait(F, "slot_gates", l, 1)
                    nc.vector.tensor_copy(slot_gates, bank[5][:, 0:16])
                    dve.drain()
                    expert_act(0, slot_gates[:, 0:1])
                    ahead(S1_MOE + 4, 0)
                    for e in range(1, GE):
                        expert(e, None)
                    with dve.Fori(1, NG) as g:
                        for e in range(GE):
                            expert(g * GE + e, g if e == 0 else None)
                    expert_lo(NE)
                    group_lo(NG)
                layer_norm(2, lambda ch: wait(F, "y", l, ch + 1), "x_ready")

            with dve.Fori(0, DEPTH) as l:
                nc.vector.tensor_copy(cur2[:], col2[:, bass.ds(l, 1), :].rearrange("p l n -> p (l n)"))
                ts(nsink[:, 0:16], sinks2[:, bass.ds(l, 1), :].rearrange("p l n -> p (l n)"), -1.0, None, ALU.mult).then_inc(G["cur"].sem, 1)

                def operand_lo_k(stage):
                    for n in range(4):
                        wait(G, "op_hi", l, (0, 4, 12)[stage] + n + 1)
                        for k in range(2):
                            t = 2 * n + k
                            i = stt(out=op_lo[:, t, :], in0=bank[TPB + n][:, k * T:k * T + T], scalar=cur2[:, 8 * stage + t:8 * stage + t + 1],
                                    in1=op_hi[:, t, :].bitcast(F32), op0=ALU.mult, op1=ALU.subtract)
                        i.then_inc(G["op_lo"].sem, 1)

                def mean_squares(stage):
                    wait(G, "ss_raw", l, 2 * stage + 2)
                    ts(ss2, ss_raw2, 1.0 / D, RMS_EPS, ALU.mult, ALU.add).then_inc(G["ss"].sem, 1)

                def ffn_residual(run, last_slab):
                    for ch in range(NC):
                        if ch == 0:
                            wait(G, "y_c0", l, run + 1)
                        else:
                            slab_is_done(last_slab)
                        for nh in range(2):
                            v = x[:, ch, 512 * nh:512 * nh + 512]
                            i = stt(out=v, in0=ybank(ch, nh)[:, :], scalar=0.5, in1=v, op0=ALU.mult, op1=ALU.add)
                    i.then_inc(G["x_ready"].sem, 1)

                column = lambda u, ch: rms2[:, ch:ch + 1]
                num = lambda j: slab_number(BASE2, S2, l, j)

                operand_lo_k(0)
                mean_squares(0)
                lo2(l, 2)
                units_lo(G, l, BASE2, S2, 0, NU2, 0, column)
                ffn_residual(0, num(S2_Q - 1))

                operand_lo_k(1)
                mean_squares(1)
                for j in range(2, 9):
                    lo2(l, S2_Q + j)

                def gate_in(b):
                    for ch in range(NC):
                        if ch == 0:
                            wait(G, "q_c0", l, 3 + b + 1)
                        else:
                            slab_is_done(num(S2_GATE + 2 * b + 1))
                        stt(out=proj[:, ch, GA + 512 * b:GA + 512 * b + 512], in0=bank[(2 if b % 2 == 0 else 0) + ch][:, :], scalar=rms2[:, ch:ch + 1],
                            in1=table[:, b // 2, 512 * (b % 2):512 * (b % 2) + 512], op0=ALU.mult, op1=ALU.add).then_inc(G["gate_in"].sem, 1)

                def masked(g):
                    for seg, name in enumerate(("m_zero", "m_tri", "m_ge", "m_zero")):
                        n = AT2["s"] + 4 * g + seg
                        wait(G, "job", l, n + 1)
                        stt(out=s2[:, g, :, seg * P:seg * P + P], in0=bank[4 + n % 4][:, :].rearrange("p (h n) -> p h n", h=4), scalar=HD ** -0.5,
                            in1=c(name).unsqueeze(1).to_broadcast([P, 4, P]), op0=ALU.mult, op1=ALU.add).then_inc(G["masked"].sem, 1)
                    dve.drain()
                    o = 8 * g
                    for ch in range(NC):
                        row_max(negm[:, o + 4 * ch:o + 4 * ch + 4], s2[:, g, :, ch * T:ch * T + T])
                    dve.drain()
                    by = lambda t: t.rearrange("p (c h) -> p c h", c=NC)
                    m, ns = by(negm[:, o:o + 8]), nsink[:, 0:16].rearrange("p (c h e) -> p c h e", c=NC, e=2)[:, :, :, g]
                    tt(m, m, ns, ALU.min)
                    dve.drain()
                    tt(by(dsink[:, o:o + 8]), m, ns, ALU.subtract).then_inc(G["negm"].sem, 1)

                def probs(g):
                    o = 8 * g
                    wait(G, "exped", l, g + 1)
                    tt(rsum[:, o:o + 8], rsum[:, o:o + 8], es[:, o:o + 8], ALU.add)
                    dve.drain()
                    nc.vector.reciprocal(rden[:, o:o + 8], rsum[:, o:o + 8])
                    dve.drain()
                    for ch in range(NC):
                        v = s2[:, g, :, ch * T:ch * T + T]
                        i = tt(v, v, rden[:, o + 4 * ch:o + 4 * ch + 4].unsqueeze(2).to_broadcast([P, 4, T]), ALU.mult)
                    i.then_inc(G["probs"].sem, 1)

                wait(G, "bgate", l, 16)
                gate_in(0)
                masked(0)
                lo2(l, S2_Q + 9)
                lo2(l, S2_Q + 10)
                probs(0)
                gate_in(1)
                masked(1)
                lo2(l, S2_Q + 11)
                lo2(l, S2_Q + 12)
                probs(1)
                gate_in(2)
                gate_in(3)
                lo2(l, S2_Q + 13)
                lo2(l, S2_Q + 14)
                for n in range(2):
                    job = AT2["mixed"] + n
                    wait(G, "mix_hi", l, n + 1)
                    for k in range(2):
                        t = 2 * n + k
                        i = stt(out=op_lo[:, 4 + t, :], in0=bank[4 + job % 4][:, k * T:k * T + T], scalar=cur2[:, 24 + t:25 + t],
                                in1=op_hi[:, 4 + t, :].bitcast(F32), op0=ALU.mult, op1=ALU.subtract)
                    i.then_inc(G["mix_lo"].sem, 1)
                for n in range(2):
                    job = AT2["o"] + n
                    wait(G, "mix_hi", l, 2 + n + 1)
                    flat = lambda t: t[:, 2 * n:2 * n + 2, :].rearrange("p k t -> p (k t)")
                    tt(flat(op_lo), bank[4 + job % 4][:, :], flat(op_hi).bitcast(F32), ALU.subtract).then_inc(G["mix_lo"].sem, 1)
                lo2(l, S2_Q + 15)

                def gated(branch, nh):
                    wait(G, "gate", l, 2 * branch + nh + 1)
                    for ch in range(NC):
                        if nh == 0 or ch == 1:
                            slab_is_done(num(S2_BR + 2 * branch + nh))
                        else:
                            wait(G, "br_c0", l, branch + 1)
                        v = proj[:, ch, GA + D * branch + 512 * nh:GA + D * branch + 512 * nh + 512]
                        b = ybank(ch, nh) if branch == 0 else bank[4 + 2 * ch + nh]
                        tt(v, b[:, :], v, ALU.mult).then_inc(G["gated"].sem, 1)

                gated(0, 0)
                lo2(l, S2_Q + 16)
                gated(0, 1)
                lo2(l, S2_Q + 17)
                gated(1, 0)
                lo2(l, S2_Q + 18)
                gated(1, 1)
                dve.drain()
                for ch in range(NC):
                    tt(proj[:, ch, GA:GA + D], proj[:, ch, GA:GA + D], proj[:, ch, GB:GB + D], ALU.add).then_inc(G["z"].sem, 1)
                operand_lo_c(G, l, 8, 0)
                for j in range(19, 23):
                    lo2(l, S2_Q + j)
                for ch in range(NC):
                    if ch == 0:
                        wait(G, "out_c0", l, 1)
                    else:
                        slab_is_done(num(S2_OUT + 3))
                    for nh in range(2):
                        v = x[:, ch, 512 * nh:512 * nh + 512]
                        i = tt(v, bank[4 + 2 * ch + nh][:, :], v, ALU.add)
                i.then_inc(G["x_ready"].sem, 1)

                operand_lo_k(2)
                mean_squares(2)
                lo2(l, S2_FFN2 + 2)
                units_lo(G, l, BASE2, S2, S2_FFN2, NU2, NU2, column)
                ffn_residual(1, num(S2 - 1))

            dve.wait_ge(G["ss_raw"].sem, G["ss_raw"].after(DEPTH, 2))
            ts(ss2, ss_raw2, 1.0 / D, RMS_EPS, ALU.mult, ALU.add).then_inc(final_ss.sem, 1)
            dve.wait_ge(block2_in.sem, 16)
            dve.wait_ge(final_rstd.sem, 1)
            for ch in range(NC):
                stt(out=x[:, ch, :], in0=x[:, ch, :], scalar=rms2[:, ch:ch + 1], in1=table[:, 0, :], op0=ALU.mult, op1=ALU.mult).then_inc(final_out.sem, 1)


NAMES = (
    "x", "w_in", "ret_gn_w", "swa_sinks", "mla_q_norm_w", "mla_kv_norm_w", "mla_w_uq", "mla_w_ukv", "w_out",
    "ln1_g", "ln1_b", "router_w", "router_bias", "exp_w_gate_up", "exp_w_down", "ln2_g", "ln2_b", "ffn1_norm_2",
    "ffn1_w1_2", "ffn1_w3_2", "ffn1_w2_2", "mix_norm_2", "w_in_2", "b_gate_2", "attn_sink_2", "pool_w_2",
    "pool_scale_2", "w_branch_attn_2", "w_branch_pool_2", "w_out_2", "ffn2_norm_2", "ffn2_w1_2", "ffn2_w3_2",
    "ffn2_w2_2", "final_norm_2",
)


def kernel(**inputs):
    import concourse.bacc as bacc
    from concourse.bass_utils import run_bass_kernel_spmd

    nc = bacc.Bacc("TRN2", target_bir_lowering=False, num_devices=1)
    arrays = {name: np.ascontiguousarray(inputs[name]) for name in NAMES}
    arrays["constants"] = CONSTANTS
    aps = {n: nc.dram_tensor(n, v.shape, mybir.dt.from_np(v.dtype), kind="ExternalInput").ap() for n, v in arrays.items()}
    out = nc.dram_tensor("out", (1, T, D), F32, kind="ExternalOutput").ap()
    program(nc, aps, out)
    result = run_bass_kernel_spmd(nc, [arrays], core_ids=[0])
    return result.results[0]["out"]
```

```python
import numpy as np
import concourse.bass as bass
from concourse import mybir
from contextlib import ExitStack

F32 = mybir.dt.float32
F32R = mybir.dt.float32r
I32 = mybir.dt.int32
ACT = mybir.ActivationFunctionType
ALU = mybir.AluOpType
AX = mybir.AxisListType

P = 128
T = 256
NC = T // P
D = 1024
DK = D // P
DEPTH = 2
ALPHA = (2 * DEPTH) ** 0.25
LN_EPS, RMS_EPS, NEG = 1e-5, 1e-6, -1e30

RQ, RK, RV, RG, SQ, SK, SV, CQ, CKV, KR, IN1 = 0, 256, 512, 768, 1024, 1408, 1536, 1664, 2048, 2304, 2336
MQ = IN1
MV = MQ + 576
KCAT = CQ
RH, HD = 4, 64
SWH, SWG = 6, 2
MH, MD, MN, MR = 6, 96, 64, 32
NE, FE = 16, 256
NG, GE = 4, 4
AQ, AK, AV, PP, GA, GB, IN2 = 0, 512, 640, 768, 1280, 2304, 3328
AH, AG = 8, 2
NU2 = 2816 // FE
POOLS = (2, 4, 8, 16)
GATES = (GB, GB + 512, GA, GA + 512)

RING = 3
SLAB = 2048
HALF = SLAB // 2
BLOCKS1 = [(SV, 512), (CKV, 288), (SQ, 512), (RQ, 512), (RV, 512)]
S1_UQ, S1_UKV, S1_RQ, S1_OUT, S1_ROUTER, S1_MOE = 6, 8, 9, 13, 17, 18
S1 = S1_MOE + 3 * NE
S2_Q = 3 * NU2
S2_KV, S2_P, S2_GATE = S2_Q + 2, S2_Q + 3, S2_Q + 5
S2_BR = S2_GATE + 8
S2_OUT = S2_BR + 4
S2_FFN2 = S2_OUT + 4
S2 = S2_FFN2 + 3 * NU2
BASE2 = DEPTH * S1
assert S1 % RING == 0 and S2 % RING == 0

CONST = {}


def _constants():
    f = np.float32
    parts = []

    def put(name, a):
        a = np.ascontiguousarray(a, dtype=f).reshape(P, -1)
        CONST[name] = (sum(p.shape[1] for p in parts), a.shape[1])
        parts.append(a)

    def rotary(theta, d):
        inv = (f(theta) ** (-np.arange(0, d, 2, dtype=f) / f(d))).astype(f)
        ang = np.arange(T, dtype=f)[:, None] * inv[None]
        by_chunk = lambda t: t.reshape(NC, P, d // 2).transpose(1, 0, 2)
        return by_chunk(np.cos(ang)), by_chunk(np.sin(ang))

    put("ident", np.eye(P))
    i = np.arange(P)[:, None]
    j = np.arange(P)[None, :]
    put("m_tri", np.where(j <= i, 0, NEG))
    put("m_gt", np.where(j > i, 0, NEG))
    put("m_ge", np.where(j >= i, 0, NEG))
    put("m_zero", np.zeros((P, P)))
    put("alpha", np.eye(P) * ALPHA)
    put("before", np.where(i < j, 1, 0))
    put("ones", np.ones((P, P)))
    put("slot", np.broadcast_to(j + 1, (P, P)))
    for name, theta, d in (("r64", 1e4, HD), ("r32", 1e4, MR), ("r16", 5e5, 16)):
        cos, sin = rotary(theta, d)
        put("cos_" + name, cos)
        put("sin_" + name, sin)
    put("rank16", np.broadcast_to(np.arange(16, 0, -1), (P, NC, 16)))
    put("rank4", np.broadcast_to(np.arange(4, 0, -1), (P, NC, 4)))
    common = sum(p.shape[1] for p in parts)
    gamma = 1.0 - 2.0 ** (-5.0 - np.arange(RH))
    rel = np.arange(T)[None, :] - np.arange(P)[:, None]
    dec = [np.where(rel >= 0, g ** np.maximum(rel, 0), 0) * HD ** -0.5 for g in gamma]
    first = np.stack([np.concatenate([x, x[:, :P]], 1) for x in dec], 1).reshape(P, -1)
    t = np.arange(T)
    mats = []
    for w in POOLS:
        lo, hi = np.clip(t - w // 2, 0, T), np.clip(t + w // 2, 0, T)
        s = np.arange(T)[:, None]
        mats.append(np.where((s >= lo) & (s < hi), 1.0 / (hi - lo), 0.0) - (s == t))
    second = np.stack(mats, 1).reshape(NC, P, len(POOLS), T).transpose(1, 0, 2, 3).reshape(P, -1)
    first = np.pad(first, ((0, 0), (0, second.shape[1] - first.shape[1])))
    return np.concatenate([np.concatenate(parts, 1), first, second], 1).astype(f), common, second.shape[1]


CONSTANTS, COMMON, PER_BLOCK = _constants()

JOBS1 = (
    [("T_swa", "copied")] * 3 + [("s_swa", "masked")] * 6 + [("p_swa", "copied")] * 6
    + [("T_mla", "copied")] * 6 + [("s_mla", "masked")] * 6 + [("T_ret", "copied")] * 2
    + [("s_ret", "weighted")] * 4 + [("o_swa", "mix_lo")] * 2
    + [("o_ret", "ret_out")] + [("p_mla", "copied")] * 6 + [("T_ro", "mix_lo")] + [("o_mla", "mix_lo")] * 2
)
JOBS2 = (
    [("T_qk", "copied")] * 3 + [("s", "masked")] * 8 + [("pool", "copied")] * 2 + [("p0", "copied")] * 4
    + [("mixed", "mix_lo")] * 2 + [("p1", "copied")] * 4 + [("o", "mix_lo")] * 2
)


def job_table(jobs):
    at, count, release = {}, {}, []
    for n, (name, signal) in enumerate(jobs):
        at.setdefault(name, n)
        count[signal] = count.get(signal, 0) + 1
        release.append((signal, count[signal]))
    return at, release


AT1, RELEASE1 = job_table(JOBS1)
AT2, RELEASE2 = job_table(JOBS2)


VECTORS1 = (("mla_q_norm_w", 3), ("mla_kv_norm_w", 2), ("ret_gn_w", 2))
VECTORS2 = (("ffn1_norm_2", 8), ("mix_norm_2", 8), ("ffn2_norm_2", 8), ("pool_scale_2", 4))


class Signal:

    def __init__(self, sem, per_layer, first=0):
        self.sem, self.per_layer, self.first = sem, per_layer, first

    def after(self, l, n):
        return l * self.per_layer + (n + self.first)


def program(nc, a, out):
    ctx = ExitStack()
    with ctx:
        def sb(name, shape, dt=F32):
            return ctx.enter_context(nc.sbuf_tensor("sb_" + name, shape, dt))

        def signal(name, per_layer=0, first=0):
            return Signal(ctx.enter_context(nc.semaphore(name)), per_layer, first)

        raw = [sb(f"raw{i}", [P, SLAB]) for i in range(RING)]
        whi = [sb(f"whi{i}", [P, SLAB], F32R) for i in range(RING)]
        wlo = [sb(f"wlo{i}", [P, SLAB], F32R) for i in range(RING)]
        x = sb("x", [P, NC, D])
        op_hi = sb("op_hi", [P, DK, T], F32R)
        op_lo = sb("op_lo", [P, DK, T], F32R)
        lat_hi = sb("lat_hi", [P, 5, T], F32R)
        lat_lo = sb("lat_lo", [P, 5, T], F32R)
        act_hi, act_lo = lat_hi[:, 0:2, :], lat_lo[:, 0:2, :]
        zero = sb("zero", [1, 512], F32R)
        const = sb("const", [P, COMMON])
        per_block = sb("per_block", [P, PER_BLOCK])
        table = sb("table", [P, 2, D])
        rows_of = sb("rows_of", [35 * DEPTH, P])
        cols = sb("cols", [P, 35 * DEPTH])
        cur1 = sb("cur1", [P, 7])
        cur2 = sb("cur2", [P, 28])
        sinks = sb("sinks", [P, DEPTH, SWH])
        sinks2 = sb("sinks2", [P, DEPTH, AH])
        nsink = sb("nsink", [P, 2 * AH])
        rbias = sb("rbias", [P, 16])
        poolw = sb("poolw", [P, 4, P])
        half = sb("half", [P, 16])
        small = sb("small", [P, 512])
        overflow = sb("overflow", [P, 1], I32)
        with ExitStack() as turn:
            proj = turn.enter_context(nc.sbuf_tensor("sb_proj", [P, NC, IN2], F32))
            arena = turn.enter_context(nc.sbuf_tensor("sb_arena", [P, 11584], F32))
        unit_work = sb("unit_work", [P, 2 * NC * FE])
        xg_hi, xg_lo = sb("xg_hi", [P, DK, NG, P], F32R), sb("xg_lo", [P, DK, NG, P], F32R)
        yg_hi, yg_lo = sb("yg_hi", [P, D], F32R), sb("yg_lo", [P, D], F32R)
        xs_hi, xs_lo = sb("xs_hi", [P, NC, D], F32R), sb("xs_lo", [P, NC, D], F32R)
        in_slot, of_slot = sb("in_slot", [P, NC, NG, P], F32R), sb("of_slot", [P, NG, T], F32R)

        def c(name):
            o, n = CONST[name]
            return const[:, o:o + n]

        ident = c("ident")

        def carve(start):
            def take(n):
                nonlocal start
                o, start = start, start + n
                assert start <= arena.shape[1]
                return arena[:, o:o + n]
            return take

        take = carve(0)
        swa_t = take(5 * T).rearrange("p (n t) -> p n t", t=T)
        mla_t = take(12 * T).rearrange("p (n t) -> p n t", t=T)
        ret_t = take(4 * T).rearrange("p (n t) -> p n t", t=T)
        ret_w = mla_t[:, 0:6, :].rearrange("p n t -> p (n t)").rearrange("p (h n) -> p h n", h=RH)
        s1 = take(2 * 1152).rearrange("p (b h n) -> p b h n", b=2, h=3)
        pt1 = take(2 * 1152).rearrange("p (b s h n) -> p b s h n", b=2, s=3, h=3)
        sk2 = take(512).rearrange("p (c g e d) -> p c g e d", c=NC, g=2, e=2)
        rot1, rot2 = take(512), take(512)
        ret_c = rot1.rearrange("p (c n) -> p c n", c=NC)
        ret_s = rot2.rearrange("p (c n) -> p c n", c=NC)
        take = carve(0)
        qk_t = take(6 * T).rearrange("p (n t) -> p n t", t=T)
        s2 = take(2 * 2048).rearrange("p (b h n) -> p b h n", b=2, h=4)
        pt2 = take(2 * 2048).rearrange("p (b s h n) -> p b s h n", b=2, s=4, h=4)
        pooled_t = take(4 * T).rearrange("p (n t) -> p n t", t=T)
        ak2 = take(512).rearrange("p (c g e d) -> p c g e d", c=NC, g=2, e=2)
        rot3, rot4 = take(160), take(160)
        sg, av = (unit_work[:, o:o + NC * FE].rearrange("p (c n) -> p c n", c=NC) for o in (0, NC * FE))

        def scratch():
            at = 0

            def take(n, *shape):
                nonlocal at
                v = small[:, at:at + n]
                at += n
                return v
            return take

        take = scratch()
        ssq, mla_rstd = take(4), take(4)
        negm, rsum = take(16), take(16)
        es, dsink = take(16), take(16)
        gn = take(8 * 3)
        stats = take(24).rearrange("p (c n) -> p c n", c=NC)
        mv = take(4).rearrange("p (c n) -> p c n", c=NC)
        lve = take(2)
        lrstd = take(2)
        scores = take(32).rearrange("p (c e) -> p c e", c=NC)
        biased = take(32).rearrange("p (c e) -> p c e", c=NC)
        pairs = take(48).rearrange("p (c g n) -> p c g n", c=NC, g=4)
        gscore = take(8).rearrange("p (c g) -> p c g", c=NC)
        gtop, ghot = take(2), take(8).rearrange("p (c g) -> p c g", c=NC)
        cand = take(32).rearrange("p (c e) -> p c e", c=NC)
        ctop = take(2)
        hot1 = take(32).rearrange("p (c e) -> p c e", c=NC)
        hot2 = take(32).rearrange("p (c e) -> p c e", c=NC)
        gates = take(32).rearrange("p (c e) -> p c e", c=NC)
        ss2, rms2, ss_raw1, ss_raw2 = take(2), take(2), take(4), take(2)
        rden = take(16)
        slot_of = take(8).rearrange("p (c g) -> p c g", c=NC)
        slot_gates = take(16)

        bank = [ctx.enter_context(nc.psum_tensor(f"bank{i}", [P, 512], F32)) for i in range(8)]
        TPB = 4
        HB, AB = 4, 6

        def ybank(ch, n):
            return bank[2 * ch + n]

        x_loaded, ident_in, block2_in = signal("x_loaded"), signal("ident_in"), signal("block2_in")
        cols_in, small_in, zero_set, set_up = signal("cols_in"), signal("small_in"), signal("zero_set"), signal("set_up")
        stored = signal("stored")
        raw_in = [[signal(f"raw_in{i}_{half}") for half in range(2)] for i in range(RING)]
        hi_made, lo_made, slab_done = signal("hi_made"), signal("lo_made"), signal("slab_done")
        F = {}
        for name, n, first in (
            ("x_ready", 2, 2), ("cols", 1, 0), ("cur", 1, 0), ("opT", 8, 0), ("op_hi", 8, 0), ("op_lo", 8, 0),
            ("blk_c0", 5, 0), ("proj", 10, 0), ("ss_raw", 4, 0), ("ssq", 1, 0), ("rstd", 1, 0), ("latT", 3, 0),
            ("lat_hi", 3, 0), ("lat_lo", 3, 0), ("mla_q", 4, 0), ("mla_kv", 8, 0),
            ("sk2", 1, 0), ("mla_rot", 1, 0), ("ret_rot", 1, 0),
            ("job", len(JOBS1), 0), ("copied", 23, 0), ("masked", 12, 0), ("weighted", 4, 0),
            ("mix_hi", 5, 0), ("mix_lo", 5, 0), ("ret_out", 1, 0), ("negm", 4, 0), ("exped", 4, 0),
            ("probs", 4, 0), ("silu_g", 1, 0), ("ret_var", 1, 0), ("ret_rstd", 1, 0), ("ro", 1, 0),
            ("mix_c0", 1, 0), ("ln_var", 4, 0), ("ln_rstd", 4, 0), ("ln1", 2, 0), ("table", 64, 0),
            ("routed", 1, 0), ("router", 1, 0), ("h_c0", NE, 0), ("sg", 2 * NE, 0), ("a", 2 * NE, 0),
            ("aT", NE, 0), ("a_hi", NE, 0), ("a_lo", NE, 0), ("y", 2, 0),
            ("xs_hi", 2, 0), ("xs_lo", 2, 0), ("ghot", 1, 0), ("ranked", 1, 0), ("sized", 1, 0), ("in_slot", 2, 0),
            ("gathered", 2 * DK, 0), ("xg_hi", DK, 0), ("xg_lo", DK, 0), ("gates", 1, 0),
            ("slot_gates", 1, 0), ("turned", 2, 0), ("of_slot", 2, 0), ("yg_hi", NG, 0), ("yg_lo", NG, 0),
        ):
            F[name] = signal("f_" + name, n, first)
        G = {}
        for name, n, first in (
            ("x_ready", 6, 2), ("cur", 1, 0), ("opT", 16, 0), ("op_hi", 16, 0), ("op_lo", 16, 0),
            ("ss", 3, 0), ("rstd", 3, 0), ("q_c0", 7, 0), ("proj", 6, 0), ("gate_in", 8, 0),
            ("gate", 4, 0), ("k_rot", 1, 0), ("rot", 1, 0), ("job", len(JOBS2), 0), ("copied", 13, 0),
            ("masked", 8, 0), ("mix_hi", 4, 0), ("mix_lo", 4, 0), ("negm", 2, 0), ("exped", 2, 0),
            ("probs", 2, 0), ("br_c0", 2, 0), ("z", 4, 0), ("out_c0", 1, 0),
            ("bgate", 16, 0), ("poolw", 16, 0), ("ss_raw", 6, 0),
            ("h_c0", 2 * NU2, 0), ("sg", 4 * NU2, 0), ("a", 4 * NU2, 0),
            ("aT", 2 * NU2, 0), ("a_hi", 2 * NU2, 0), ("a_lo", 2 * NU2, 0), ("y_c0", 2, 0),
        ):
            G[name] = signal("g_" + name, n, first)
        final_ss, final_rstd, final_out = signal("final_ss"), signal("final_rstd"), signal("final_out")

        def slab_number(base, per_layer, l, j):
            return l * per_layer + (j + base)

        def halves(buffers, first, second):
            return [[t[:, o:o + n] for t in buffers] for o, n in ((0, first), (HALF, second))]

        def split_hi(act, raw_count, number, slot, first=HALF, second=HALF):
            for i, (r, h) in enumerate(halves((raw[slot], whi[slot]), first, second)):
                if i == 0:
                    act.wait_ge(slab_done.sem, number + 1)
                act.wait_ge(raw_in[slot][i].sem, raw_count)
                nc.scalar.activation(h, r, ACT.Copy).then_inc(hi_made.sem, 1)

        def split_lo(dve, number, slot, first=HALF, second=HALF):
            for i, (r, h, o) in enumerate(halves((raw[slot], whi[slot], wlo[slot]), first, second)):
                dve.wait_ge(hi_made.sem, number * 2 + (i + 1))
                nc.vector.tensor_tensor(o, r, h.bitcast(F32), ALU.subtract).then_inc(lo_made.sem, 1)

        def products(ps, hi, lo, wh, wl, first, last):
            nc.tensor.matmul(ps, hi, wh, start=first, stop=False)
            nc.tensor.matmul(ps, hi, wl, start=False, stop=False)
            return nc.tensor.matmul(ps, lo, wh, start=False, stop=last)

        WIDTH1 = {2: (2 * 288, 2 * 288), 3: (2 * 288, 2 * 288), 6: (2 * 288, 288), 7: (2 * 288, 288), 8: (768, 768), S1_ROUTER: (64, 64)}
        WHOLE = (HALF, HALF)

        def count1(l, j):
            return l * (16 * S1 // RING) + 16 * (j // RING + 1)

        def count2(l, j):
            return l * (16 * S2 // RING) + 16 * (BASE2 // RING + j // RING + 1)

        block = ctx.enter_context(nc.Block())

        @block.sync
        def _(sp):
            sp.dma_start(ident, a["constants"][:, 0:P]).then_inc(ident_in.sem, 16)
            sp.dma_start(x[:], a["x"].rearrange("b (c p) d -> p (b c) d", p=P)).then_inc(x_loaded.sem, 16)

            def load(number, slot, pieces, at_once=False):
                if at_once:
                    sp.wait_ge(lo_made.sem, number * 2 + 2)
                for i in (1, 0) if at_once else (0, 1):
                    if not at_once:
                        sp.wait_ge(lo_made.sem, number * 2 + (i + 1))
                    dst, src = pieces[i]
                    sp.dma_start(dst, src).then_inc(raw_in[slot][i].sem, 16)

            def half_of(slot, half, nk, n):
                return raw[slot][:, HALF * half:HALF * half + nk * n].rearrange("p (k n) -> p k n", n=n)

            def rows(w, l, r0, nk, c0, n, slot):
                s = w[bass.ds(l, 1), r0:r0 + nk * P, c0:c0 + n].rearrange("l (k p) n -> p (l k) n", p=P)
                h = (nk + 1) // 2
                return [(half_of(slot, 0, h, n), s[:, 0:h, :]), (half_of(slot, 1, nk - h, n), s[:, h:nk, :])]

            with sp.Fori(0, DEPTH) as l:
                def put(j, w, r0, nk, c0, n):
                    load(slab_number(0, S1, l, j), j % RING, rows(w, l, r0, nk, c0, n, j % RING), r0 == 0 and c0 == 0)

                for b, (c0, n) in enumerate(BLOCKS1[:3]):
                    for h in range(2):
                        put(2 * b + h, a["w_in"], 512 * h, 4, c0, n)
                for h in range(2):
                    put(S1_UQ + h, a["mla_w_uq"], 0, 3, 288 * h, 288)
                put(S1_UKV, a["mla_w_ukv"], 0, 2, 0, 768)
                for b, (c0, n) in enumerate(BLOCKS1[3:]):
                    for h in range(2):
                        put(S1_RQ + 2 * b + h, a["w_in"], 512 * h, 4, c0, n)
                for i, name in enumerate(("ln1_g", "ln1_b")):
                    sp.wait_ge(F["x_ready"].sem, F["x_ready"].after(l, 0))
                    sp.dma_start(table[:, i, :], a[name][bass.ds(l, 1), :].to_broadcast([P, D])).then_inc(F["table"].sem, 16)
                for i in range(4):
                    put(S1_OUT + i, a["w_out"], 512 * (i // 2), 4, 512 * (i % 2), 512)
                s = a["router_w"].rearrange("(k p) n -> p k n", p=P)
                load(slab_number(0, S1, l, S1_ROUTER), S1_ROUTER % RING,
                     [(half_of(S1_ROUTER % RING, h, 4, 16), s[:, 4 * h:4 * h + 4, :]) for h in range(2)])

                def gate_up(number, j, e):
                    for h in range(2):
                        slot = (j + h) % RING
                        v = raw[slot][:, :].rearrange("p (k n) -> p k n", n=512)
                        s = a["exp_w_gate_up"][bass.ds(l, 1), bass.ds(e, 1), 512 * h:512 * h + 512, :].rearrange("l e (k p) n -> p (l e k) n", p=P)
                        load(number + h, slot, [(v[:, 2 * i:2 * i + 2, :], s[:, 2 * i:2 * i + 2, :]) for i in range(2)])

                def down(number, j, e):
                    slot = j % RING
                    v = raw[slot][:, :].rearrange("p (k n) -> p k n", n=D)
                    s = a["exp_w_down"][bass.ds(l, 1), bass.ds(e, 1), :, :].rearrange("l e (k p) n -> p (l e k) n", p=P)
                    load(number, slot, [(v[:, i:i + 1, :], s[:, i:i + 1, :]) for i in range(2)])

                gate_up(slab_number(0, S1, l, S1_MOE), S1_MOE, 0)
                for i, name in enumerate(("ln2_g", "ln2_b")):
                    sp.wait_ge(F["ln1"].sem, F["ln1"].after(l, 2))
                    sp.dma_start(table[:, i, :], a[name][bass.ds(l, 1), :].to_broadcast([P, D])).then_inc(F["table"].sem, 16)
                with sp.Fori(1, NE) as u:
                    j = u * 3 + (S1_MOE - 1)
                    gate_up(slab_number(0, S1, l, j), S1_MOE + 2, u)
                    down(slab_number(0, S1, l, j + 2), S1_MOE + 4, u - 1)
                j = S1 - 1
                down(slab_number(0, S1, l, j), j, NE - 1)

            def ffn(l, j0, w1, w3, w2):
                def up(number, j, u):
                    for h in range(2):
                        slot = (j + h) % RING
                        load(number + h, slot, [
                            (half_of(slot, i, 4, FE),
                             w[bass.ds(l, 1), 512 * h:512 * h + 512, bass.ds(u * FE, FE)].rearrange("l (k p) n -> p (l k) n", p=P))
                            for i, w in enumerate((w1, w3))])

                def down(number, j, u):
                    slot = j % RING
                    v = raw[slot][:, :].rearrange("p (k n) -> p k n", n=D)
                    s = w2[bass.ds(l, 1), bass.ds(u * FE, FE), :].rearrange("l (k p) n -> p (l k) n", p=P)
                    load(number, slot, [(v[:, i:i + 1, :], s[:, i:i + 1, :]) for i in range(2)])

                up(slab_number(BASE2, S2, l, j0), j0, 0)
                with sp.Fori(1, NU2) as u:
                    j = u * 3 + (j0 - 1)
                    up(slab_number(BASE2, S2, l, j), j0 + 2, u)
                    down(slab_number(BASE2, S2, l, j + 2), j0 + 4, u - 1)
                j = j0 + 3 * NU2 - 1
                down(slab_number(BASE2, S2, l, j), j, NU2 - 1)

            with sp.Fori(0, DEPTH) as l:
                def put(j, w, r0, nk, c0, n):
                    load(slab_number(BASE2, S2, l, j), j % RING, rows(w, l, r0, nk, c0, n, j % RING), r0 == 0 and c0 == 0)

                ffn(l, 0, a["ffn1_w1_2"], a["ffn1_w3_2"], a["ffn1_w2_2"])
                for h in range(2):
                    put(S2_Q + h, a["w_in_2"], 512 * h, 4, AQ, 512)
                put(S2_KV, a["w_in_2"], 0, 8, AK, 256)
                sp.wait_ge(G["x_ready"].sem, G["x_ready"].after(l, 0))
                sp.dma_start(table[:, :, :].rearrange("p b d -> p (b d)"), a["b_gate_2"][bass.ds(l, 1), :].to_broadcast([P, 2 * D])).then_inc(G["bgate"].sem, 16)
                sp.dma_start(poolw[:], a["pool_w_2"][bass.ds(l, 1), :, :, :].rearrange("l g c d -> c (l g) d")).then_inc(G["poolw"].sem, 16)
                for h in range(2):
                    put(S2_P + h, a["w_in_2"], 512 * h, 4, PP, 512)
                for b in range(4):
                    for h in range(2):
                        put(S2_GATE + 2 * b + h, a["w_in_2"], 512 * h, 4, GATES[b], 512)
                for i, w in enumerate((a["w_branch_pool_2"], a["w_branch_attn_2"])):
                    for n in range(2):
                        put(S2_BR + 2 * i + n, w, 0, 4, 512 * n, 512)
                for i in range(4):
                    put(S2_OUT + i, a["w_out_2"], 512 * (i // 2), 4, 512 * (i % 2), 512)
                ffn(l, S2_FFN2, a["ffn2_w1_2"], a["ffn2_w3_2"], a["ffn2_w2_2"])
            for i in range(2):
                sp.wait_ge(lo_made.sem, 2 * (BASE2 + DEPTH * S2 + i) + 2)
                for half in range(2):
                    sp.sem_inc(raw_in[i][half].sem, 16)
            sp.dma_start(table[:, 0, :], a["final_norm_2"].rearrange("(o n) -> o n", o=1).to_broadcast([P, D])).then_inc(block2_in.sem, 16)
            for ch in range(NC):
                sp.wait_ge(final_out.sem, ch + 1)
                sp.dma_start(out[0, ch * P:ch * P + P, :], x[:, ch, :]).then_inc(stored.sem, 16)
            sp.wait_ge(stored.sem, 32)

        @block.gpsimd
        def _(pool):
            nc.gpsimd.memset(half[:], -0.5)
            nc.gpsimd.memset(zero[:].bitcast(F32), 0.0).then_inc(zero_set.sem, 1)
            pool.sem_inc(lo_made.sem, 2 * RING)
            pool.sem_inc(slab_done.sem, RING)
            small_loads = (
                (const[:, P:COMMON], a["constants"][:, P:COMMON]),
                (sinks[:].rearrange("p l h -> p (l h)"), a["swa_sinks"].rearrange("(o l) h -> o (l h)", o=1).to_broadcast([P, DEPTH * SWH])),
                (sinks2[:].rearrange("p l h -> p (l h)"), a["attn_sink_2"].rearrange("(o l) h -> o (l h)", o=1).to_broadcast([P, DEPTH * AH])),
                (rbias[:], a["router_bias"].rearrange("(o n) -> o n", o=1).to_broadcast([P, 16])),
                (per_block[:], a["constants"][:, COMMON:COMMON + PER_BLOCK]),
            )
            pool.wait_ge(x_loaded.sem, 16)
            pool.sem_inc(F["x_ready"].sem, 2)
            r = 0
            for name, n in VECTORS1 + VECTORS2:
                pool.dma_start(rows_of[r:r + DEPTH * n, :], a[name].rearrange("l (k p) -> (l k) p", p=P)).then_inc(cols_in.sem, 16)
                r += DEPTH * n
            for dst, src in small_loads:
                pool.dma_start(dst, src).then_inc(small_in.sem, 16)
            pool.wait_ge(small_in.sem, 16 * len(small_loads))
            pool.sem_inc(set_up.sem, 1)

            def rotate(x1, x2, cos, sin, t1, t2):
                tt = nc.gpsimd.tensor_tensor
                tt(t1, x1, sin, ALU.mult)
                tt(t2, x2, sin, ALU.mult)
                pool.drain()
                tt(x1, x1, cos, ALU.mult)
                tt(x2, x2, cos, ALU.mult)
                pool.drain()
                tt(x1, x1, t2, ALU.subtract)
                tt(x2, x2, t1, ALU.add)
                pool.drain()

            def heads(view, h, d, tab, n):
                return view.rearrange("p (h d) -> p h d", d=d)

            with pool.Fori(0, DEPTH) as l:
                pool.wait_ge(F["ssq"].sem, F["ssq"].after(l, 1))
                nc.gpsimd.tensor_tensor(mla_rstd, ssq, half[:, 0:4], ALU.pow).then_inc(F["rstd"].sem, 1)
                pool.wait_ge(F["proj"].sem, F["proj"].after(l, 6))
                for ch in range(NC):
                    src = proj[:, ch, SK:SK + 128].rearrange("p (g d) -> p g d", g=SWG)
                    for e in range(2):
                        nc.gpsimd.tensor_tensor(sk2[:, ch, :, e, :], src, c("m_zero").rearrange("p (g d) -> p g d", g=SWG), ALU.add)
                pool.drain()
                pool.sem_inc(F["sk2"].sem, 1)
                pool.wait_ge(F["mla_q"].sem, F["mla_q"].after(l, 4))
                pool.wait_ge(F["mla_kv"].sem, F["mla_kv"].after(l, 8))
                cs = [c(n + "_r32").rearrange("p (c d) -> p c d", c=NC) for n in ("cos", "sin")]
                for ch in range(NC):
                    q = proj[:, ch, MQ:MQ + 576].rearrange("p (h d) -> p h d", d=MD)
                    tabs = [t[:, ch:ch + 1, :].to_broadcast([P, MH, 16]) for t in cs]
                    tmp = [t[:, 0:96].rearrange("p (h d) -> p h d", d=16) for t in (rot1, rot2)]
                    rotate(q[:, :, 64:80], q[:, :, 80:96], *tabs, *tmp)
                    k = proj[:, ch, KR:KR + 32]
                    rotate(k[:, 0:16], k[:, 16:32], cs[0][:, ch, :], cs[1][:, ch, :], rot1[:, 0:16], rot2[:, 0:16])
                    dst = proj[:, ch, KCAT:KCAT + 576].rearrange("p (h d) -> p h d", d=MD)[:, :, 64:96]
                    nc.gpsimd.tensor_copy(dst, proj[:, ch:ch + 1, KR:KR + 32].to_broadcast([P, MH, 32]))
                pool.drain()
                pool.sem_inc(F["mla_rot"].sem, 1)
                pool.wait_ge(F["proj"].sem, F["proj"].after(l, 8))
                cs = [c(n + "_r64").rearrange("p (c d) -> p c d", c=NC) for n in ("cos", "sin")]
                for ch in range(NC):
                    qk = proj[:, ch, RQ:RQ + 512].rearrange("p (h d) -> p h d", d=HD)
                    tabs = [t[:, ch:ch + 1, :].to_broadcast([P, 8, 32]) for t in cs]
                    tmp = [t[:, 0:256].rearrange("p (h d) -> p h d", d=32) for t in (rot1, rot2)]
                    rotate(qk[:, :, 0:32], qk[:, :, 32:64], *tabs, *tmp)
                pool.sem_inc(F["ret_rot"].sem, 1)
                pool.wait_ge(F["ret_var"].sem, F["ret_var"].after(l, 1))
                nc.gpsimd.tensor_tensor(gn[:, 16:24], gn[:, 8:16], half[:, 0:8], ALU.pow).then_inc(F["ret_rstd"].sem, 1)
                for n in range(4):
                    pool.wait_ge(F["ln_var"].sem, F["ln_var"].after(l, n + 1))
                    nc.gpsimd.tensor_tensor(lrstd[:, n % 2:n % 2 + 1], lve[:, n % 2:n % 2 + 1], half[:, 0:1], ALU.pow).then_inc(F["ln_rstd"].sem, 1)

            for ch in range(NC):
                pool.wait_ge(F["x_ready"].sem, F["x_ready"].after(DEPTH, ch + 1 - NC))
                pool.sem_inc(G["x_ready"].sem, 1)
            pool.dma_start(per_block[:], a["constants"][:, COMMON + PER_BLOCK:]).then_inc(small_in.sem, 16)
            pool.wait_ge(small_in.sem, 16 * (1 + len(small_loads)))
            pool.sem_inc(set_up.sem, 1)

            def rms(l, stage):
                pool.wait_ge(G["ss"].sem, G["ss"].after(l, stage + 1))
                nc.gpsimd.tensor_tensor(rms2, ss2, half[:, 0:2], ALU.pow).then_inc(G["rstd"].sem, 1)

            with pool.Fori(0, DEPTH) as l:
                rms(l, 0)
                rms(l, 1)
                pool.wait_ge(G["proj"].sem, G["proj"].after(l, 4))
                cs = [c(n + "_r16").rearrange("p (c d) -> p c d", c=NC) for n in ("cos", "sin")]
                for ch in range(NC):
                    qk = proj[:, ch, AQ:AQ + 640].rearrange("p (h d) -> p h d", d=HD)
                    tabs = [t[:, ch:ch + 1, :].to_broadcast([P, 10, 8]) for t in cs]
                    tmp = [t[:, 0:80].rearrange("p (h d) -> p h d", d=8) for t in (rot3, rot4)]
                    rotate(qk[:, :, 0:8], qk[:, :, 8:16], *tabs, *tmp)
                    src = proj[:, ch, AK:AK + 128].rearrange("p (g d) -> p g d", g=AG)
                    for e in range(2):
                        nc.gpsimd.tensor_copy(ak2[:, ch, :, e, :], src)
                pool.drain()
                pool.sem_inc(G["rot"].sem, 1)
                rms(l, 2)
            pool.wait_ge(final_ss.sem, 1)
            nc.gpsimd.tensor_tensor(rms2, ss2, half[:, 0:2], ALU.pow).then_inc(final_rstd.sem, 1)

        @block.tensor
        def _(pe):
            pe.wait_ge(zero_set.sem, 1)
            pe.wait_ge(ident_in.sem, 16)

            def wait(S, name, l, n):
                pe.wait_ge(S[name].sem, S[name].after(l, n))

            def slab_ready(number):
                pe.wait_ge(lo_made.sem, number * 2 + 2 * (1 + RING))

            def tile(slot, n, half, k, c0, width):
                o = (k * n if k < half else HALF + (k - half) * n) + c0
                return whi[slot][:, o:o + width], wlo[slot][:, o:o + width]

            def tile_pair(slot, k):
                return (t[slot][:, :].rearrange("p (i k n) -> p i k n", i=2, n=FE)[:, :, k, :] for t in (whi, wlo))

            def slab(number, slot, n, tiles, dst, opening, closing, c0_signal=None, hi=op_hi, lo=op_lo, before=None, paired=False):
                slab_ready(number)
                for ch in range(NC):
                    for k, t in enumerate(tiles):
                        if before is not None:
                            before(ch, t)
                        tok = slice(ch * P, ch * P + P)
                        w = tile_pair(slot, k) if paired else tile(slot, n, (len(tiles) + 1) // 2, k, 0, n)
                        i = products(dst(ch), hi[:, t, tok], lo[:, t, tok], *w,
                                     opening and k == 0, closing and k == len(tiles) - 1)
                    if ch == 0 and c0_signal is not None:
                        i.then_inc(c0_signal.sem, 1)
                i.then_inc(slab_done.sem, 1)

            def transposes_c(S, src, ready):
                for ch in range(NC):
                    ready(ch)
                    for h in range(2):
                        for k in range(4):
                            o = (4 * h + k) * P
                            i = nc.tensor.transpose(bank[TPB + 2 * ch + h][:, k * P:k * P + P], src(ch, o), ident)
                        i.then_inc(S["opT"].sem, 1)

            def halves_ready(S, l, n0):
                def before(ch, t):
                    if t % 4 == 0:
                        wait(S, "op_lo", l, n0 + 2 * ch + t // 4 + 1)
                return before

            def unit_up(number, slot, h_signal, before, paired):
                slab(number, slot, 512, range(0, 4), lambda ch: bank[HB + ch][:, :], True, False, before=before, paired=paired)
                slab(number + 1, (slot + 1) % RING, 512, range(4, 8), lambda ch: bank[HB + ch][:, :], False, True, h_signal, before=before, paired=paired)

            def unit_transposes(S, l, before, n):
                pe.wait_ge(S["a"].sem, S["a"].after(l, 2 * n))
                for f in range(2):
                    for ch in range(NC):
                        i = nc.tensor.transpose(bank[AB][:, f * T + ch * P:f * T + ch * P + P], av[:, ch, f * P:f * P + P], ident)
                i.then_inc(S["aT"].sem, 1)

            def unit_down(S, l, number, slot, n, closing, c0_signal=None):
                pe.wait_ge(S["a_lo"].sem, S["a_lo"].after(l, n))
                slab_ready(number)
                for ch in range(NC):
                    for nh in range(2):
                        for k in range(2):
                            tok = slice(ch * P, ch * P + P)
                            i = products(ybank(ch, nh)[:, :], act_hi[:, k, tok], act_lo[:, k, tok],
                                         *tile(slot, D, 1, k, 512 * nh, 512), False, closing and k == 1)
                    if ch == 0 and c0_signal is not None:
                        i.then_inc(c0_signal.sem, 1)
                i.then_inc(slab_done.sem, 1)

            def open_sums():
                for ch in range(NC):
                    for nh in range(2):
                        nc.tensor.matmul(ybank(ch, nh)[:, :], zero[0:1, 0:P], zero[0:1, :], start=True, stop=False)

            def open_residual(ch):
                for nh in range(2):
                    nc.tensor.matmul(ybank(ch, nh)[:, :], c("alpha"), x[:, ch, 512 * nh:512 * nh + 512], start=True, stop=False)

            def units(S, l, base, per_layer, j0, count, n0, y_c0, before=None, paired=True, opened=False):
                num = lambda j: slab_number(base, per_layer, l, j)
                unit_up(num(j0), j0 % RING, S["h_c0"], before, paired)
                if not opened:
                    open_sums()
                unit_transposes(S, l, 0, n0 + 1)
                with pe.Fori(1, count) as u:
                    j = u * 3 + (j0 - 1)
                    unit_up(num(j), (j0 + 2) % RING, S["h_c0"], None, paired)
                    unit_down(S, l, num(j + 2), (j0 + 4) % RING, u + n0, False)
                    unit_transposes(S, l, 0, u + (n0 + 1))
                j = j0 + 3 * count - 1
                unit_down(S, l, num(j), j % RING, n0 + count, True, y_c0)

            class Jobs:

                def __init__(self, S, l, release):
                    self.S, self.l, self.release, self.n = S, l, release, 0

                def take(self):
                    n, self.n = self.n, self.n + 1
                    if n >= 4:
                        name, count = self.release[n - 4]
                        wait(self.S, name, self.l, count)
                    return bank[4 + n % 4]

                def done(self, i):
                    i.then_inc(self.S["job"].sem, 1)

            def transposed_tiles(jobs, tiles):
                for o in range(0, len(tiles), 2):
                    b = jobs.take()
                    for n, view in enumerate(tiles[o:o + 2]):
                        for ch in range(NC):
                            v = view(ch)
                            i = nc.tensor.transpose(b[0:v.shape[1], n * T + ch * P:n * T + ch * P + P], v, ident)
                    jobs.done(i)

            with pe.Fori(0, DEPTH) as l:
                jobs = Jobs(F, l, RELEASE1)
                num = lambda j: slab_number(0, S1, l, j)
                transposes_c(F, lambda ch, o: x[:, ch, o:o + P], lambda ch: wait(F, "x_ready", l, ch + 1 - 2))

                def block1(b, j, before=None, halves=range(2)):
                    n = BLOCKS1[b][1]
                    at = 2 * (b % 2)
                    for h in halves:
                        slab(num(j + h), (j + h) % RING, n, range(4 * h, 4 * h + 4), lambda ch: bank[at + ch][:, 0:n],
                             h == 0, h == 1, F["blk_c0"] if h else None, before=before)

                block1(0, 0, halves_ready(F, l, 0))
                block1(1, 2)
                pe.wait_ge(cols_in.sem, 16 * (len(VECTORS1) + len(VECTORS2)))
                n = 35 * DEPTH
                nc.tensor.transpose(bank[7][:, 0:n], rows_of[:, :], ident[0:n, 0:n]).then_inc(F["cols"].sem, 1)
                wait(F, "proj", l, 4)
                for t in range(5):
                    o = CQ + t * P
                    for ch in range(NC):
                        i = nc.tensor.transpose(bank[4 + t // 2][:, (t % 2) * T + ch * P:(t % 2) * T + ch * P + P], proj[:, ch, o:o + P], ident)
                    if t % 2 or t == 4:
                        i.then_inc(F["latT"].sem, 1)
                block1(2, 4)
                wait(F, "lat_lo", l, 3)
                for h in range(2):
                    slab(num(S1_UQ + h), (S1_UQ + h) % RING, 288, range(3), lambda ch: bank[2 + 4 * h + ch][:, 0:288], True, True, None, lat_hi, lat_lo)
                slab_ready(num(S1_UKV))
                for h in range(2):
                    if h == 0:
                        wait(F, "proj", l, 6)
                    else:
                        wait(F, "mla_q", l, 2)
                    for ch in range(NC):
                        dst = bank[2 * h + ch][:, 0:384]
                        for k in range(2):
                            tok = slice(ch * P, ch * P + P)
                            i = products(dst, lat_hi[:, 3 + k, tok], lat_lo[:, 3 + k, tok], *tile(S1_UKV % RING, 768, 1, k, 384 * h, 384), k == 0, k == 1)
                i.then_inc(slab_done.sem, 1)
                wait(F, "sk2", l, 1)
                wait(F, "mla_q", l, 4)
                transposed_tiles(jobs, [lambda ch, t=t: proj[:, ch, SQ + t * P:SQ + t * P + P] for t in range(3)]
                                 + [lambda ch, g=g: sk2[:, ch, g, :, :].rearrange("p e d -> p (e d)") for g in range(2)])
                wait(F, "mla_kv", l, 4)
                block1(3, S1_RQ, halves=(0,))

                def softmax_scores(q, k, group, width):
                    for qc, kc in ((0, 0), (1, 0), (1, 1)):
                        b = jobs.take()
                        for h in range(3):
                            i = nc.tensor.matmul(b[:, h * P:h * P + P], q(2 * h + group, qc), k(2 * h + group, kc), start=True, stop=True)
                        jobs.done(i)

                def probs_transposed(S, group, s, nseg, nh):
                    wait(S, "probs", l, group + 1)
                    for seg in range(nseg):
                        b = jobs.take()
                        for h in range(nh):
                            i = nc.tensor.transpose(b[:, h * P:h * P + P], s[:, group % 2, h, seg * P:seg * P + P], ident)
                        jobs.done(i)

                def head_outputs(pairs, value, probs, tiles):
                    for o in range(0, len(tiles), 2):
                        b = jobs.take()
                        for n, t in enumerate(tiles[o:o + 2]):
                            for e in range(2):
                                h = 2 * t + e
                                r = slice(e * HD, e * HD + HD)
                                nc.tensor.matmul(b[r, n * T:n * T + T], value(h, 0), probs(h, slice(0, 2)), start=True, stop=False)
                                i = nc.tensor.matmul(b[r, n * T + P:n * T + T], value(h, 1), probs(h, 2), start=False, stop=True)
                        jobs.done(i)

                def swa_q(h, ch):
                    r = HD * (h % 2)
                    return swa_t[r:r + HD, h // 2, ch * P:ch * P + P]

                def swa_k(h, ch):
                    r = HD * (h % 2)
                    return swa_t[r:r + HD, 3 + h // 3, ch * P:ch * P + P]

                wait(F, "copied", l, 3)
                for g in range(2):
                    softmax_scores(swa_q, swa_k, g, HD)
                block1(3, S1_RQ, halves=(1,))
                wait(F, "mla_kv", l, 8)
                block1(4, S1_RQ + 2, halves=(0,))
                for g in range(2):
                    probs_transposed(F, g, s1, 3, 3)
                wait(F, "mla_rot", l, 1)
                mq = [lambda ch, h=h: proj[:, ch, MQ + MD * h:MQ + MD * h + MD] for h in range(MH)]
                mk = [lambda ch, h=h: proj[:, ch, KCAT + MD * h:KCAT + MD * h + MD] for h in range(MH)]
                transposed_tiles(jobs, mq + mk)
                wait(F, "copied", l, 15)
                for g in range(2):
                    softmax_scores(lambda h, ch: mla_t[0:MD, h, ch * P:ch * P + P],
                                   lambda h, ch: mla_t[0:MD, MH + h, ch * P:ch * P + P], g, MD)
                wait(F, "ret_rot", l, 1)
                transposed_tiles(jobs, [lambda ch, t=t: proj[:, ch, RQ + t * P:RQ + t * P + P] for t in range(4)])
                block1(4, S1_RQ + 2, halves=(1,))
                wait(F, "copied", l, 17)
                for h in range(RH):
                    b = jobs.take()
                    r = slice(HD * (h % 2), HD * (h % 2) + HD)
                    q, k = ret_t[r, h // 2, :], ret_t[r, 2 + h // 2, :]
                    nc.tensor.matmul(b[:, 0:T], k[:, 0:P], q, start=True, stop=True)
                    jobs.done(nc.tensor.matmul(b[:, T:T + P], k[:, P:T], q[:, P:T], start=True, stop=True))
                head_outputs(3, lambda h, kc: proj[:, kc, SV + HD * (h // 3):SV + HD * (h // 3) + HD],
                             lambda h, s: pt1[:, h % 2, s, h // 2, :], range(3))
                wait(F, "weighted", l, 4)
                wait(F, "proj", l, 10)
                b = jobs.take()
                for ch in range(NC):
                    for h in range(RH):
                        o = b[:, ch * T + h * HD:ch * T + h * HD + HD]
                        v = [proj[:, kc, RV + h * HD:RV + h * HD + HD] for kc in range(NC)]
                        i = nc.tensor.matmul(o, ret_w[:, h, ch * P:ch * P + P], v[0], start=True, stop=ch == 0)
                        if ch:
                            i = nc.tensor.matmul(o, ret_w[:, h, T:T + P], v[1], start=False, stop=True)
                jobs.done(i)
                for g in range(2):
                    wait(F, "probs", l, 3 + g)
                    for seg in range(3):
                        b = jobs.take()
                        for h in range(3):
                            i = nc.tensor.transpose(b[:, h * P:h * P + P], s1[:, g, h, seg * P:seg * P + P], ident)
                        jobs.done(i)
                open_residual(0)
                open_residual(1)
                wait(F, "ro", l, 1)
                transposed_tiles(jobs, [lambda ch, t=t: ret_c[:, ch, t * P:t * P + P] for t in range(2)])
                wait(F, "copied", l, 23)
                head_outputs(3, lambda h, kc: proj[:, kc, MV + HD * h:MV + HD * h + HD],
                             lambda h, s: pt1[:, h % 2, s, h // 2, :], range(3))
                wait(F, "mix_lo", l, 3)
                for i in range(4):
                    if i == 2:
                        wait(F, "mix_lo", l, 5)
                    h, nh = i // 2, i % 2
                    slab(num(S1_OUT + i), (S1_OUT + i) % RING, 512, range(4 * h, 4 * h + 4), lambda ch: ybank(ch, nh)[:, :],
                         False, h == 1, F["mix_c0"] if i == 3 else None)
                transposes_c(F, lambda ch, o: x[:, ch, o:o + P], lambda ch: wait(F, "ln1", l, ch + 1))
                slab_ready(num(S1_ROUTER))
                operand = halves_ready(F, l, 4)
                for ch in range(NC):
                    for k in range(DK):
                        operand(ch, k)
                        tok = slice(ch * P, ch * P + P)
                        i = products(bank[4][:, 16 * ch:16 * ch + 16], op_hi[:, k, tok], op_lo[:, k, tok],
                                     *tile(S1_ROUTER % RING, 16, 4, k, 0, 16), k == 0, k == DK - 1)
                i.then_inc(slab_done.sem, 1)

                open_residual(0)
                wait(F, "ghot", l, 1)
                b = bank[6]
                before, ones = c("before"), c("ones")
                nc.tensor.matmul(b[:, 0:4], before, ghot[:, 0, :], start=True, stop=True)
                for o, last in ((4, before), (8, ones)):
                    nc.tensor.matmul(b[:, o:o + 4], ones, ghot[:, 0, :], start=True, stop=False)
                    i = nc.tensor.matmul(b[:, o:o + 4], last, ghot[:, 1, :], start=False, stop=True)
                i.then_inc(F["ranked"].sem, 1)
                open_residual(1)
                wait(F, "xs_lo", l, 2)
                wait(F, "in_slot", l, 2)
                for n in range(2 * DK):
                    k = n // 2
                    if n == 2:
                        wait(F, "sized", l, 1)
                    if n >= 4:
                        wait(F, "xg_lo" if n % 2 else "xg_hi", l, k - 1)
                    src = xs_lo if n % 2 else xs_hi
                    for ch in range(NC):
                        i = nc.tensor.matmul(bank[4 + n % 4][:, :], src[:, ch, k * P:k * P + P],
                                             in_slot[:, ch, :, :].rearrange("p g n -> p (g n)"), start=ch == 0, stop=ch == 1)
                    i.then_inc(F["gathered"].sem, 1)
                size = pe.value_load(overflow[0:1, 0:1], min_val=0, max_val=T)

                def expert_up(number, slot, g):
                    for h in range(2):
                        slab_ready(number + h)
                        for k in range(4):
                            hi, lo = xg_hi[:, 4 * h + k, g, :], xg_lo[:, 4 * h + k, g, :]
                            i = products(bank[HB][:, :], hi, lo, *tile((slot + h) % RING, 512, 2, k, 0, 512), h == 0 and k == 0, h == 1 and k == 3)
                        i.then_inc(slab_done.sem, 1)

                def expert_turn(u):
                    wait(F, "a", l, u * 2 + 2)
                    for f in range(2):
                        i = nc.tensor.transpose(bank[5][:, f * P:f * P + P], av[:, 0, f * P:f * P + P], ident)
                    i.then_inc(F["aT"].sem, 1)

                def expert_down(u, e):
                    j = S1_MOE + 3 * u + 4 if u < NE - 1 else S1 - 1
                    wait(F, "a_lo", l, u + 1)
                    slab_ready(num(j))
                    for nh in range(2):
                        for k in range(2):
                            i = products(bank[6 + nh][:, :], act_hi[:, k, 0:P], act_lo[:, k, 0:P], *tile(j % RING, D, 1, k, 512 * nh, 512),
                                         e == 0 and k == 0, e == GE - 1 and k == 1)
                    i.then_inc(slab_done.sem, 1)

                def scatter(g, n, closing):
                    wait(F, "yg_lo", l, n)
                    for ch in range(NC):
                        for nh in range(2):
                            to = of_slot[:, g, ch * P:ch * P + P]
                            cols = slice(512 * nh, 512 * nh + 512)
                            nc.tensor.matmul(ybank(ch, nh)[:, :], to, yg_hi[:, cols], start=False, stop=False)
                            i = nc.tensor.matmul(ybank(ch, nh)[:, :], to, yg_lo[:, cols], start=False, stop=closing)
                        if closing:
                            i.then_inc(F["y"].sem, 1)

                with pe.If(size > P):
                    wait(F, "xg_lo", l, DK)
                    wait(F, "xg_hi", l, DK)
                    units(F, l, 0, S1, S1_MOE, NE, 0, F["y"], paired=False, opened=True)
                    pe.drain()
                    pe.sem_inc(F["y"].sem, 1)
                    pe.sem_inc(F["slot_gates"].sem, 1)
                    pe.sem_inc(F["turned"].sem, 2)
                with pe.Else():
                    up_number = lambda u: slab_number(0, S1, l, u * 3 + (S1_MOE - 1))
                    wait(F, "xg_lo", l, DK)
                    wait(F, "xg_hi", l, DK)
                    expert_up(num(S1_MOE), S1_MOE % RING, 0)
                    wait(F, "gates", l, 1)
                    for g in range(NG):
                        for ch in range(NC):
                            i = nc.tensor.matmul(bank[5][:, GE * g:GE * g + GE], in_slot[:, ch, g, :].bitcast(F32), gates[:, ch, GE * g:GE * g + GE], start=ch == 0, stop=ch == 1)
                    i.then_inc(F["slot_gates"].sem, 1)
                    for n in range(2):
                        for g in range(2):
                            for ch in range(NC):
                                i = nc.tensor.transpose(bank[6 + n][:, g * T + ch * P:g * T + ch * P + P], in_slot[:, ch, 2 * n + g, :].bitcast(F32), ident)
                        i.then_inc(F["turned"].sem, 1)
                    expert_turn(0)
                    for e in range(1, GE):
                        expert_up(up_number(e), (S1_MOE + 2) % RING, 0)
                        if e == 1:
                            wait(F, "of_slot", l, 2)
                        expert_down(e - 1, e - 1)
                        expert_turn(e)
                    for g in range(1, NG):
                        for e in range(GE):
                            u = g * GE + e
                            expert_up(up_number(u), (S1_MOE + 2) % RING, g)
                            if e == 1:
                                wait(F, "yg_lo", l, g)
                            expert_down(u - 1, (e - 1) % GE)
                            expert_turn(u)
                            if e == 1:
                                scatter(g - 1, g, False)
                    expert_down(NE - 1, GE - 1)
                    scatter(NG - 1, NG, True)
                    pe.sem_inc(F["h_c0"].sem, NE)

            with pe.Fori(0, DEPTH) as l:
                jobs = Jobs(G, l, RELEASE2)
                num = lambda j: slab_number(BASE2, S2, l, j)

                def transposes_k(stage, banks=TPB):
                    for ch in range(NC):
                        wait(G, "x_ready", l, 2 * stage + ch + 1 - NC)
                        for n in range(4):
                            for k in range(2):
                                o = (2 * n + k) * P
                                i = nc.tensor.transpose(bank[banks + n][:, k * T + ch * P:k * T + ch * P + P], x[:, ch, o:o + P], ident)
                            if ch == NC - 1:
                                i.then_inc(G["opT"].sem, 1)

                def pairs_ready(n0):
                    def before(ch, t):
                        if ch == 0 and t % 2 == 0:
                            wait(G, "op_lo", l, n0 + t // 2 + 1)
                    return before

                transposes_k(0)
                units(G, l, BASE2, S2, 0, NU2, 0, G["y_c0"], pairs_ready(0))

                transposes_k(1)

                def block2(b, j, at, before=None):
                    for h in range(2):
                        slab(num(j + h), (j + h) % RING, 512, range(4 * h, 4 * h + 4), lambda ch: bank[at + ch][:, :],
                             h == 0, h == 1, G["q_c0"] if h else None, before=before)

                block2(0, S2_Q, 0, pairs_ready(4))
                slab(num(S2_KV), S2_KV % RING, 256, range(8), lambda ch: bank[2 + ch][:, 0:256], True, True, G["q_c0"])
                wait(G, "proj", l, 2)
                block2(2, S2_P, 0)
                wait(G, "rot", l, 1)
                transposed_tiles(jobs, [lambda ch, t=t: proj[:, ch, AQ + t * P:AQ + t * P + P] for t in range(4)]
                                 + [lambda ch, g=g: ak2[:, ch, g, :, :].rearrange("p e d -> p (e d)") for g in range(2)])
                block2(3, S2_GATE, 2)

                def scores2(g):
                    for qc, kc in ((0, 0), (0, 1), (1, 0), (1, 1)):
                        b = jobs.take()
                        for n in range(4):
                            r = slice(HD * g, HD * g + HD)
                            i = nc.tensor.matmul(b[:, n * P:n * P + P], qk_t[r, n, qc * P:qc * P + P],
                                                 qk_t[r, 4 + n // 2, kc * P:kc * P + P], start=True, stop=True)
                        jobs.done(i)

                wait(G, "copied", l, 3)
                scores2(0)
                wait(G, "proj", l, 6)
                block2(4, S2_GATE + 2, 0)
                scores2(1)
                wait(G, "gate_in", l, 2)
                block2(5, S2_GATE + 4, 2)
                pe.wait_ge(set_up.sem, 2)
                for o in range(0, 4, 2):
                    b = jobs.take()
                    for n in range(2):
                        g = o + n
                        for kc in range(NC):
                            mat = per_block[:, (kc * 4 + g) * T:(kc * 4 + g) * T + T]
                            i = nc.tensor.matmul(b[:, n * T:n * T + T], proj[:, kc, PP + g * P:PP + g * P + P], mat, start=kc == 0, stop=kc == 1)
                    jobs.done(i)

                def probs2(g):
                    wait(G, "probs", l, g + 1)
                    for seg in range(4):
                        b = jobs.take()
                        for n in range(4):
                            i = nc.tensor.transpose(b[:, n * P:n * P + P], s2[:, g, n, seg * P:seg * P + P], ident)
                        jobs.done(i)

                probs2(0)
                wait(G, "poolw", l, 16)
                wait(G, "copied", l, 5)
                for o in range(0, 4, 2):
                    b = jobs.take()
                    for n in range(2):
                        i = nc.tensor.matmul(b[:, n * T:n * T + T], poolw[:, o + n, :], pooled_t[:, o + n, :], start=True, stop=True)
                    jobs.done(i)
                wait(G, "gate_in", l, 4)
                block2(6, S2_GATE + 6, 0)
                probs2(1)
                wait(G, "gate_in", l, 8)
                wait(G, "mix_lo", l, 2)
                pool_branch = lambda nh: slab(num(S2_BR + nh), (S2_BR + nh) % RING, 512, range(4), lambda ch: ybank(ch, nh)[:, :], True, True,
                                              G["br_c0"] if nh else None, hi=lat_hi, lo=lat_lo)
                pool_branch(0)
                wait(G, "copied", l, 13)
                for o in range(0, 4, 2):
                    b = jobs.take()
                    for n in range(2):
                        for e in range(2):
                            h = 2 * (o + n) + e
                            r = slice(e * HD, e * HD + HD)
                            v = [proj[:, kc, AV + HD * (h // 4):AV + HD * (h // 4) + HD] for kc in range(NC)]
                            pt = pt2[:, e, :, o + n, :]
                            nc.tensor.matmul(b[r, n * T:n * T + T], v[0], pt[:, 0:4:2, :], start=True, stop=False)
                            i = nc.tensor.matmul(b[r, n * T:n * T + T], v[1], pt[:, 1:4:2, :], start=False, stop=True)
                    jobs.done(i)
                pool_branch(1)
                wait(G, "mix_lo", l, 4)
                for nh in range(2):
                    slab(num(S2_BR + 2 + nh), (S2_BR + 2 + nh) % RING, 512, range(4), lambda ch: bank[4 + 2 * ch + nh][:, :], True, True,
                         G["br_c0"] if nh else None)
                for h in range(2):
                    for ch in range(NC):
                        wait(G, "z", l, 2 * h + ch + 1)
                        for k in range(4):
                            o = GA + (4 * h + k) * P
                            i = nc.tensor.transpose(ybank(ch, h)[:, k * P:k * P + P], proj[:, ch, o:o + P], ident)
                        i.then_inc(G["opT"].sem, 1)

                def z_ready(ch, t):
                    if t % 4 == 0:
                        wait(G, "op_lo", l, 8 + 2 * (t // 4) + ch + 1)

                for i in range(4):
                    h, nh = i // 2, i % 2
                    slab(num(S2_OUT + i), (S2_OUT + i) % RING, 512, range(4 * h, 4 * h + 4), lambda ch: bank[4 + 2 * ch + nh][:, :],
                         h == 0, h == 1, G["out_c0"] if i == 3 else None, before=z_ready if nh == 0 else None)

                transposes_k(2, 0)
                units(G, l, BASE2, S2, S2_FFN2, NU2, NU2, G["y_c0"], pairs_ready(12))

        @block.scalar
        def _(act):
            def wait(S, name, l, n):
                act.wait_ge(S[name].sem, S[name].after(l, n))

            def hi1(l, j):
                n = l * S1 + j
                split_hi(act, count1(l, j), n, j % RING, *WIDTH1.get(j, WHOLE))

            def hi2(l, j):
                split_hi(act, count2(l, j), slab_number(BASE2, S2, l, j), j % RING)

            def units_hi(S, l, base, per_layer, j0, count, n0, col):
                num = lambda j: slab_number(base, per_layer, l, j)
                ring = per_layer // RING

                def ahead(j_fixed, u):
                    split_hi(act, l * (16 * ring) + u * 16 + 16 * (base // RING + j_fixed // RING + 1),
                             l * per_layer + u * 3 + (base + j_fixed), j_fixed % RING)

                def silu(u, last_slab):
                    for ch in range(NC):
                        if ch == 0:
                            wait(S, "h_c0", l, u + (n0 + 1))
                        else:
                            act.wait_ge(slab_done.sem, last_slab + 1 + RING)
                        nc.scalar.activation(sg[:, ch, :], bank[HB + ch][:, 0:FE], ACT.Silu,
                                             scale=1.0 if col is None else col(ch)).then_inc(S["sg"].sem, 1)

                ahead(j0 + 3, 0)
                silu(0, num(j0 + 1))
                ahead(j0 + 4, 0)
                def hi_part(n):
                    wait(S, "aT", l, n)
                    nc.scalar.activation(act_hi.rearrange("p f t -> p (f t)"), bank[AB][:, :], ACT.Copy).then_inc(S["a_hi"].sem, 1)

                def unit(u):
                    hi_part(u + n0)
                    ahead(j0 + 2, u)
                    silu(u, num(u * 3 + j0))

                with act.Fori(1, count - 1) as u:
                    unit(u)
                    ahead(j0 + 3, u)
                    ahead(j0 + 4, u)
                unit(count - 1)
                hi_part(n0 + count)
                ahead(j0 + 3, count - 1)
                ahead(j0 + 4, count - 1)

            def operand_hi_c(S, l, n0, banks, order=((0, 0), (0, 1), (1, 0), (1, 1))):
                for n, (ch, h) in enumerate(order):
                    wait(S, "opT", l, n0 + n + 1)
                    nc.scalar.activation(op_hi[:, 4 * h:4 * h + 4, ch * P:ch * P + P], bank[banks + 2 * ch + h][:, :].rearrange("p (k t) -> p k t", k=4),
                                         ACT.Copy).then_inc(S["op_hi"].sem, 1)

            hi1(0, 0)
            hi1(0, 1)
            with act.Fori(0, DEPTH) as l:
                def block_out(b, j):
                    c0, n = BLOCKS1[b]
                    at = 2 * (b % 2)
                    for ch in range(NC):
                        if ch == 0:
                            wait(F, "blk_c0", l, b + 1)
                        else:
                            act.wait_ge(slab_done.sem, slab_number(0, S1, l, j + 1) + 1 + RING)
                        nc.scalar.activation(proj[:, ch, c0:c0 + n], bank[at + ch][:, 0:n], ACT.Copy).then_inc(F["proj"].sem, 1)

                def copies(dst, n0, count0):
                    for n, (d, rows, width) in enumerate(dst):
                        wait(F, "job", l, n0 + n + 1)
                        nc.scalar.activation(d, bank[4 + (n0 + n) % 4][0:rows, 0:width], ACT.Copy).then_inc(F["copied"].sem, 1)

                def exps(group, sinks_of):
                    wait(F, "negm", l, group + 1)
                    b = group % 2
                    for ch in range(NC):
                        seg = slice(0, P) if ch == 0 else slice(P, 3 * P)
                        for h in range(3):
                            m = ch * 3 + h + 8 * b
                            i = nc.scalar.activation(s1[:, b, h, seg], s1[:, b, h, seg], ACT.Exp, bias=negm[:, m:m + 1], accum_out=rsum[:, m:m + 1])
                    if sinks_of:
                        i = nc.scalar.activation(es[:, 8 * b:8 * b + 6], dsink[:, 8 * b:8 * b + 6], ACT.Exp)
                    i.then_inc(F["exped"].sem, 1)

                def mix_hi(n, job, t0, nt, scales=None):
                    wait(F, "job", l, job + 1)
                    b = bank[4 + job % 4]
                    if scales is None:
                        i = nc.scalar.activation(op_hi[:, t0:t0 + nt, :].rearrange("p k t -> p (k t)"), b[:, 0:nt * T], ACT.Copy)
                    else:
                        for k in range(nt):
                            i = nc.scalar.activation(op_hi[:, t0 + k, :], b[:, k * T:k * T + T], ACT.Copy, scale=scales[:, k:k + 1])
                    i.then_inc(F["mix_hi"].sem, 1)

                operand_hi_c(F, l, 0, TPB)
                hi1(l, 2)
                hi1(l, 3)
                block_out(0, 0)
                hi1(l, 4)
                hi1(l, 5)
                block_out(1, 2)
                for n, (c0, w) in enumerate(((CQ, 384), (CKV, 256))):
                    for ch in range(NC):
                        act.drain()
                        nc.scalar.activation(rot1[:, 0:w], proj[:, ch, c0:c0 + w], ACT.Square, accum_out=ss_raw1[:, 2 * n + ch:2 * n + ch + 1]).then_inc(F["ss_raw"].sem, 1)
                wait(F, "cur", l, 1)
                for n, tiles in enumerate(((0, 1), (2, 3), (4,))):
                    wait(F, "latT", l, n + 1)
                    for t in tiles:
                        i = nc.scalar.activation(lat_hi[:, t, :], bank[4 + n][:, (t % 2) * T:(t % 2) * T + T], ACT.Copy, scale=cur1[:, t:t + 1])
                    i.then_inc(F["lat_hi"].sem, 1)
                hi1(l, 6)
                block_out(2, 4)
                hi1(l, 7)
                hi1(l, 8)
                wait(F, "rstd", l, 1)
                for h in range(2):
                    act.wait_ge(slab_done.sem, slab_number(0, S1, l, S1_UQ + h) + 1 + RING)
                    for ch in range(NC):
                        nc.scalar.activation(proj[:, ch, MQ + 288 * h:MQ + 288 * h + 288], bank[2 + 4 * h + ch][:, 0:288], ACT.Copy,
                                             scale=mla_rstd[:, ch:ch + 1]).then_inc(F["mla_q"].sem, 1)
                    if h == 0:
                        hi1(l, 9)
                act.wait_ge(slab_done.sem, slab_number(0, S1, l, S1_UKV) + 1 + RING)
                for h in (1, 0):
                    for ch in range(NC):
                        kv = bank[2 * h + ch][:, 0:384].rearrange("p (h d) -> p h d", d=128)
                        kd = proj[:, ch, KCAT + 288 * h:KCAT + 288 * h + 288].rearrange("p (h d) -> p h d", d=MD)[:, :, 0:MN]
                        vd = proj[:, ch, MV + 192 * h:MV + 192 * h + 192].rearrange("p (h d) -> p h d", d=HD)
                        for d, s in ((kd, kv[:, :, 0:MN]), (vd, kv[:, :, MN:128])):
                            nc.scalar.activation(d, s, ACT.Copy, scale=mla_rstd[:, 2 + ch:3 + ch]).then_inc(F["mla_kv"].sem, 1)
                flat = lambda t, o, n: t[:, o:o + n, :].rearrange("p n t -> p (n t)")
                copies([(flat(swa_t, 0, 2), P, 2 * T), (flat(swa_t, 2, 2), P, 2 * T), (swa_t[:, 4, :], P, T)], AT1["T_swa"], 0)
                hi1(l, 10)
                hi1(l, 11)
                exps(0, True)
                exps(1, True)
                hi1(l, 12)
                block_out(3, S1_RQ)
                copies([(pt1[:, g, s, :, :].rearrange("p h n -> p (h n)"), P, 384) for g in range(2) for s in range(3)], AT1["p_swa"], 3)
                copies([(mla_t[0:MD, 2 * n:2 * n + 2, :].rearrange("p n t -> p (n t)"), MD, 2 * T) for n in range(6)], AT1["T_mla"], 9)
                hi1(l, 13)
                copies([(flat(ret_t, 2 * n, 2), P, 2 * T) for n in range(2)], AT1["T_ret"], 15)
                exps(2, False)
                block_out(4, S1_RQ + 2)
                exps(3, False)
                hi1(l, 14)
                mix_hi(0, AT1["o_swa"], 2, 2)
                mix_hi(1, AT1["o_swa"] + 1, 4, 1)
                act.drain()
                nc.scalar.activation(proj[:, :, RG:RG + 256], proj[:, :, RG:RG + 256], ACT.Silu).then_inc(F["silu_g"].sem, 1)
                hi1(l, 15)
                copies([(pt1[:, g, s, :, :].rearrange("p h n -> p (h n)"), P, 384) for g in range(2) for s in range(3)], AT1["p_mla"], 17)
                mix_hi(2, AT1["T_ro"], 0, 2, cur1[:, 5:7])
                mix_hi(3, AT1["o_mla"], 5, 2)
                mix_hi(4, AT1["o_mla"] + 1, 7, 1)
                hi1(l, 16)
                hi1(l, 17)
                hi1(l, 18)
                operand_hi_c(F, l, 4, TPB)
                for ch in range(NC):
                    nc.scalar.activation(xs_hi[:, ch, :], x[:, ch, :], ACT.Copy).then_inc(F["xs_hi"].sem, 1)
                hi1(l, 19)
                act.wait_ge(slab_done.sem, slab_number(0, S1, l, S1_ROUTER) + 1 + RING)
                nc.scalar.activation(scores.rearrange("p c e -> p (c e)"), bank[4][:, 0:32], ACT.Sigmoid).then_inc(F["routed"].sem, 1)
                hi1(l, 20)
                for k in range(DK):
                    wait(F, "gathered", l, 2 * k + 1)
                    nc.scalar.activation(xg_hi[:, k, :, :].rearrange("p g n -> p (g n)"), bank[4 + 2 * k % 4][:, :], ACT.Copy).then_inc(F["xg_hi"].sem, 1)
                size = act.value_load(overflow[0:1, 0:1], min_val=0, max_val=T)

                def ahead(j_fixed, u):
                    split_hi(act, l * (16 * S1 // RING) + u * 16 + 16 * (j_fixed // RING + 1), l * S1 + u * 3 + j_fixed, j_fixed % RING)

                def expert_silu(u, last_slab):
                    act.wait_ge(slab_done.sem, last_slab + 1 + RING)
                    nc.scalar.activation(sg[:, 0, :], bank[HB][:, 0:FE], ACT.Silu).then_inc(F["sg"].sem, 2)

                def expert_hi(n):
                    wait(F, "aT", l, n)
                    nc.scalar.activation(act_hi[:, :, 0:P], bank[5][:, 0:2 * P].rearrange("p (f n) -> p f n", f=2), ACT.Copy).then_inc(F["a_hi"].sem, 1)

                def group_hi(last_slab):
                    act.wait_ge(slab_done.sem, last_slab + 1 + RING)
                    for nh in range(2):
                        i = nc.scalar.activation(yg_hi[:, 512 * nh:512 * nh + 512], bank[6 + nh][:, :], ACT.Copy)
                    i.then_inc(F["yg_hi"].sem, 1)

                with act.If(size > P):
                    units_hi(F, l, 0, S1, S1_MOE, NE, 0, None)
                    act.sem_inc(F["of_slot"].sem, 2)
                    act.sem_inc(F["yg_hi"].sem, NG)
                with act.Else():
                    number = lambda j: slab_number(0, S1, l, j)

                    def expert(u, group_end, last=False):
                        ahead(S1_MOE + 2, u)
                        expert_silu(u, number(u * 3 + S1_MOE))
                        if last:
                            expert_hi(NE)
                        ahead(S1_MOE + 3, u)
                        if last:
                            group_hi(number(S1 - 1))
                        else:
                            expert_hi(u + 1)
                        ahead(S1_MOE + 4, u)
                        if group_end:
                            group_hi(number(u * 3 + (S1_MOE + 1)))

                    ahead(S1_MOE + 3, 0)
                    expert_silu(0, number(S1_MOE + 1))
                    for n in range(2):
                        wait(F, "turned", l, n + 1)
                        nc.scalar.activation(of_slot[:, 2 * n:2 * n + 2, :].rearrange("p g t -> p (g t)"), bank[6 + n][:, :], ACT.Copy).then_inc(F["of_slot"].sem, 1)
                    expert_hi(1)
                    ahead(S1_MOE + 4, 0)
                    for e in range(1, GE):
                        expert(e, False)
                    with act.Fori(1, NG - 1) as g:
                        for e in range(GE):
                            expert(g * GE + e, e == 0)
                    for e in range(GE):
                        expert((NG - 1) * GE + e, e == 0, e == GE - 1)

            with act.Fori(0, DEPTH) as l:
                def squares(stage):
                    for ch in range(NC):
                        act.drain()
                        if stage == 0:
                            wait(G, "x_ready", l, 0)
                        nc.scalar.activation(proj[:, ch, GA:GA + D], x[:, ch, :], ACT.Square, accum_out=ss_raw2[:, ch:ch + 1]).then_inc(G["ss_raw"].sem, 1)

                def operand_hi_k(stage, banks=TPB):
                    for n in range(4):
                        wait(G, "opT", l, (0, 4, 12)[stage] + n + 1)
                        for k in range(2):
                            t = 2 * n + k
                            i = nc.scalar.activation(op_hi[:, t, :], bank[banks + n][:, k * T:k * T + T], ACT.Copy,
                                                     scale=cur2[:, 8 * stage + t:8 * stage + t + 1])
                        i.then_inc(G["op_hi"].sem, 1)

                def column(ch):
                    return rms2[:, ch:ch + 1]

                wait(G, "cur", l, 1)
                operand_hi_k(0)
                squares(0)
                hi2(l, 2)
                wait(G, "rstd", l, 1)
                units_hi(G, l, BASE2, S2, 0, NU2, 0, column)

                operand_hi_k(1)
                squares(1)
                hi2(l, S2_Q + 2)
                hi2(l, S2_Q + 3)
                wait(G, "rstd", l, 2)

                def block_out(b, j, c0, n, at):
                    for ch in range(NC):
                        if ch == 0:
                            wait(G, "q_c0", l, b + 1)
                        else:
                            act.wait_ge(slab_done.sem, slab_number(BASE2, S2, l, j) + 1 + RING)
                        nc.scalar.activation(proj[:, ch, c0:c0 + n], bank[at + ch][:, 0:n], ACT.Copy, scale=column(ch)).then_inc(G["proj"].sem, 1)

                def copies(dst, n0):
                    for n, (d, width) in enumerate(dst):
                        wait(G, "job", l, n0 + n + 1)
                        nc.scalar.activation(d, bank[4 + (n0 + n) % 4][:, 0:width], ACT.Copy).then_inc(G["copied"].sem, 1)

                def exps(g):
                    wait(G, "negm", l, g + 1)
                    for ch in range(NC):
                        for h in range(4):
                            m = 8 * g + 4 * ch + h
                            seg = slice(ch * T, ch * T + T)
                            nc.scalar.activation(s2[:, g, h, seg], s2[:, g, h, seg], ACT.Exp, bias=negm[:, m:m + 1], accum_out=rsum[:, m:m + 1])
                    nc.scalar.activation(es[:, 8 * g:8 * g + 8], dsink[:, 8 * g:8 * g + 8], ACT.Exp).then_inc(G["exped"].sem, 1)

                def gate(b):
                    wait(G, "gate_in", l, 2 * b + 2)
                    o = GATES[b]
                    nc.scalar.activation(proj[:, :, o:o + 512], proj[:, :, o:o + 512], ACT.Sigmoid).then_inc(G["gate"].sem, 1)

                block_out(0, S2_Q + 1, AQ, 512, 0)
                hi2(l, S2_Q + 4)
                block_out(1, S2_KV, AK, 256, 2)
                hi2(l, S2_Q + 5)
                hi2(l, S2_Q + 6)
                block_out(2, S2_P + 1, PP, 512, 0)
                flat = lambda t, o, n: t[:, o:o + n, :].rearrange("p n t -> p (n t)")
                hi2(l, S2_Q + 7)
                copies([(flat(qk_t, 2 * n, 2), 2 * T) for n in range(3)], AT2["T_qk"])
                hi2(l, S2_Q + 8)
                hi2(l, S2_Q + 9)
                exps(0)
                hi2(l, S2_Q + 10)
                exps(1)
                hi2(l, S2_Q + 11)
                copies([(flat(pooled_t, 2 * n, 2), 2 * T) for n in range(2)], AT2["pool"])
                copies([(pt2[:, 0, s, :, :].rearrange("p h n -> p (h n)"), 512) for s in range(4)], AT2["p0"])
                for n in range(2):
                    job = AT2["mixed"] + n
                    wait(G, "job", l, job + 1)
                    for k in range(2):
                        t = 2 * n + k
                        i = nc.scalar.activation(lat_hi[:, t, :], bank[4 + job % 4][:, k * T:k * T + T], ACT.Copy, scale=cur2[:, 24 + t:25 + t])
                    i.then_inc(G["mix_hi"].sem, 1)
                hi2(l, S2_Q + 12)
                hi2(l, S2_Q + 13)
                copies([(pt2[:, 1, s, :, :].rearrange("p h n -> p (h n)"), 512) for s in range(4)], AT2["p1"])
                gate(0)
                hi2(l, S2_Q + 14)
                gate(1)
                for n in range(2):
                    job = AT2["o"] + n
                    wait(G, "job", l, job + 1)
                    nc.scalar.activation(op_hi[:, 2 * n:2 * n + 2, :].rearrange("p k t -> p (k t)"), bank[4 + job % 4][:, :], ACT.Copy).then_inc(G["mix_hi"].sem, 1)
                hi2(l, S2_Q + 15)
                gate(2)
                gate(3)
                hi2(l, S2_Q + 16)
                hi2(l, S2_Q + 17)
                hi2(l, S2_Q + 18)
                operand_hi_c(G, l, 8, 0, ((0, 0), (1, 0), (0, 1), (1, 1)))
                hi2(l, S2_Q + 19)
                hi2(l, S2_Q + 20)
                hi2(l, S2_Q + 21)
                hi2(l, S2_Q + 22)

                operand_hi_k(2, 0)
                squares(2)
                hi2(l, S2_FFN2 + 2)
                wait(G, "rstd", l, 3)
                units_hi(G, l, BASE2, S2, S2_FFN2, NU2, NU2, column)
            for ch in range(NC):
                act.wait_ge(G["x_ready"].sem, G["x_ready"].after(DEPTH, 0))
                act.drain()
                nc.scalar.activation(proj[:, ch, GA:GA + D], x[:, ch, :], ACT.Square, accum_out=ss_raw2[:, ch:ch + 1]).then_inc(G["ss_raw"].sem, 1)

        @block.vector
        def _(dve):
            tt, ts, stt = nc.vector.tensor_tensor, nc.vector.tensor_scalar, nc.vector.scalar_tensor_tensor

            def wait(S, name, l, n):
                dve.wait_ge(S[name].sem, S[name].after(l, n))

            def lo1(l, j):
                split_lo(dve, l * S1 + j, j % RING, *WIDTH1.get(j, WHOLE))

            def lo2(l, j):
                split_lo(dve, slab_number(BASE2, S2, l, j), j % RING)

            def slab_is_done(number):
                dve.wait_ge(slab_done.sem, number + 1 + RING)

            def units_lo(S, l, base, per_layer, j0, count, n0, col):
                def ahead(j_fixed, u):
                    split_lo(dve, l * per_layer + u * 3 + (base + j_fixed), j_fixed % RING)

                def activations(u):
                    for ch in range(NC):
                        wait(S, "sg", l, u * 2 + (2 * n0 + ch + 1))
                        stt(out=av[:, ch, :], in0=bank[HB + ch][:, FE:2 * FE], scalar=col(u, ch), in1=sg[:, ch, :],
                            op0=ALU.mult, op1=ALU.mult).then_inc(S["a"].sem, 1)

                def lo_part(n):
                    wait(S, "a_hi", l, n)
                    tt(act_lo.rearrange("p f t -> p (f t)"), bank[AB][:, :],
                       act_hi.rearrange("p f t -> p (f t)").bitcast(F32), ALU.subtract).then_inc(S["a_lo"].sem, 1)

                ahead(j0 + 3, 0)
                activations(0)
                ahead(j0 + 4, 0)
                def unit(u):
                    lo_part(u + n0)
                    ahead(j0 + 2, u)
                    activations(u)

                with dve.Fori(1, count - 1) as u:
                    unit(u)
                    ahead(j0 + 3, u)
                    ahead(j0 + 4, u)
                unit(count - 1)
                lo_part(n0 + count)
                return lambda j_fixed: ahead(j_fixed, count - 1)

            def operand_lo_c(S, l, n0, banks, order=((0, 0), (0, 1), (1, 0), (1, 1))):
                for n, (ch, h) in enumerate(order):
                    wait(S, "op_hi", l, n0 + n + 1)
                    part = (slice(None), slice(4 * h, 4 * h + 4), slice(ch * P, ch * P + P))
                    tt(op_lo[part], bank[banks + 2 * ch + h][:, :].rearrange("p (k t) -> p k t", k=4), op_hi[part].bitcast(F32),
                       ALU.subtract).then_inc(S["op_lo"].sem, 1)

            def row_max(dst, src):
                nc.vector.tensor_reduce(dst, src, axis=AX.X, op=ALU.max, negate=True)

            def layer_columns(l, vectors, cur, row):
                at = 0
                for _, n in vectors:
                    nc.vector.tensor_copy(cur[:, at:at + n], cols[:, bass.ds(l * n + row, n)])
                    at, row = at + n, row + DEPTH * n

            lo1(0, 0)
            with dve.Fori(0, DEPTH) as l:
                operand_lo_c(F, l, 0, TPB)
                for j in range(1, 6):
                    lo1(l, j)
                wait(F, "cols", l, 1)
                nc.vector.tensor_copy(cols[:], bank[7][:, 0:35 * DEPTH])
                dve.drain()
                layer_columns(l, VECTORS1, cur1, 0)
                dve.wait_ge(set_up.sem, 1)
                ts(nsink[:, 0:12].rearrange("p (c h) -> p c h", c=NC), sinks[:, bass.ds(l, 1), :].to_broadcast([P, NC, SWH]),
                   -1.0, None, ALU.mult).then_inc(F["cur"].sem, 1)
                wait(F, "ss_raw", l, 4)
                ts(ssq[:, 0:2], ss_raw1[:, 0:2], 1.0 / 384, RMS_EPS, ALU.mult, ALU.add)
                ts(ssq[:, 2:4], ss_raw1[:, 2:4], 1.0 / 256, RMS_EPS, ALU.mult, ALU.add).then_inc(F["ssq"].sem, 1)
                for n, tiles in enumerate(((0, 1), (2, 3), (4,))):
                    wait(F, "lat_hi", l, n + 1)
                    for t in tiles:
                        i = stt(out=lat_lo[:, t, :], in0=bank[4 + n][:, (t % 2) * T:(t % 2) * T + T], scalar=cur1[:, t:t + 1],
                                in1=lat_hi[:, t, :].bitcast(F32), op0=ALU.mult, op1=ALU.subtract)
                    i.then_inc(F["lat_lo"].sem, 1)
                for j in range(6, 12):
                    lo1(l, j)

                def masked(group, job, scale, masks):
                    b = group % 2
                    for seg in range(3):
                        n = job + 3 * b + seg
                        wait(F, "job", l, n + 1)
                        m = c(masks[seg]).unsqueeze(1).to_broadcast([P, 3, P])
                        stt(out=s1[:, b, :, seg * P:seg * P + P], in0=bank[4 + n % 4][:, 0:384].rearrange("p (h n) -> p h n", h=3),
                            scalar=scale, in1=m, op0=ALU.mult, op1=ALU.add).then_inc(F["masked"].sem, 1)
                    dve.drain()
                    o = 8 * b
                    row_max(negm[:, o:o + 3], s1[:, b, :, 0:P])
                    nc.vector.tensor_reduce(negm[:, o + 3:o + 6], s1[:, b, :, P:3 * P], axis=AX.X, op=ALU.max, negate=True) \
                        if group < 2 else \
                        nc.vector.tensor_reduce(negm[:, o + 3:o + 6], s1[:, b, :, P:3 * P], axis=AX.X, op=ALU.max, negate=True).then_inc(F["negm"].sem, 1)
                    if group < 2:
                        dve.drain()
                        by = lambda t: t.rearrange("p (c h) -> p c h", c=NC)
                        m, ns = by(negm[:, o:o + 6]), nsink[:, 0:12].rearrange("p (c h e) -> p c h e", c=NC, e=2)[:, :, :, group]
                        tt(m, m, ns, ALU.min)
                        dve.drain()
                        tt(by(dsink[:, o:o + 6]), m, ns, ALU.subtract).then_inc(F["negm"].sem, 1)

                def probs(group):
                    b = group % 2
                    o = 8 * b
                    wait(F, "exped", l, group + 1)
                    if group < 2:
                        tt(rsum[:, o:o + 6], rsum[:, o:o + 6], es[:, o:o + 6], ALU.add)
                        dve.drain()
                    nc.vector.reciprocal(rden[:, o:o + 6], rsum[:, o:o + 6])
                    dve.drain()
                    for seg, k in ((slice(0, P), 0), (slice(P, 3 * P), 3)):
                        v = s1[:, b, :, seg]
                        i = tt(v, v, rden[:, o + k:o + k + 3].unsqueeze(2).to_broadcast([P, 3, seg.stop - seg.start]), ALU.mult)
                    i.then_inc(F["probs"].sem, 1)

                def mix_lo(n, job, t0, nt, scaled=False):
                    wait(F, "mix_hi", l, n + 1)
                    b = bank[4 + job % 4]
                    if not scaled:
                        flat = lambda t: t[:, t0:t0 + nt, :].rearrange("p k t -> p (k t)")
                        i = tt(flat(op_lo), b[:, 0:nt * T], flat(op_hi).bitcast(F32), ALU.subtract)
                    else:
                        for k in range(nt):
                            i = stt(out=op_lo[:, t0 + k, :], in0=b[:, k * T:k * T + T], scalar=cur1[:, 5 + k:6 + k],
                                    in1=op_hi[:, t0 + k, :].bitcast(F32), op0=ALU.mult, op1=ALU.subtract)
                    i.then_inc(F["mix_lo"].sem, 1)

                for g in range(2):
                    masked(g, AT1["s_swa"], HD ** -0.5, ("m_tri", "m_gt", "m_tri"))
                probs(0)
                probs(1)
                lo1(l, 12)
                for g in range(2):
                    masked(2 + g, AT1["s_mla"], MD ** -0.5, ("m_tri", "m_zero", "m_tri"))
                lo1(l, 13)
                decay = per_block[:, 0:RH * 384].rearrange("p (h n) -> p h n", h=RH)
                for h in range(RH):
                    n = AT1["s_ret"] + h
                    wait(F, "job", l, n + 1)
                    tt(ret_w[:, h, :], bank[4 + n % 4][:, 0:384], decay[:, h, :], ALU.mult).then_inc(F["weighted"].sem, 1)
                probs(2)
                probs(3)
                lo1(l, 14)
                mix_lo(0, AT1["o_swa"], 2, 2)
                mix_lo(1, AT1["o_swa"] + 1, 4, 1)
                n = AT1["o_ret"]
                wait(F, "job", l, n + 1)
                heads = lambda t: t.rearrange("p (h d) -> p h d", d=HD)
                by_head = lambda o: gn[:, o:o + 8].unsqueeze(2).to_broadcast([P, 8, HD])
                o = heads(bank[4 + n % 4][:, :])
                nc.vector.tensor_reduce(gn[:, 0:8], o, axis=AX.X, op=ALU.add)
                dve.drain()
                ts(gn[:, 0:8], gn[:, 0:8], 1.0 / HD, None, ALU.mult)
                dve.drain()
                tt(heads(rot1), o, by_head(0), ALU.subtract).then_inc(F["ret_out"].sem, 1)
                dve.drain()
                tt(rot2, rot1, rot1, ALU.mult)
                dve.drain()
                nc.vector.tensor_reduce(gn[:, 8:16], heads(rot2), axis=AX.X, op=ALU.add)
                dve.drain()
                ts(gn[:, 8:16], gn[:, 8:16], 1.0 / HD, LN_EPS, ALU.mult, ALU.add).then_inc(F["ret_var"].sem, 1)
                wait(F, "ret_rstd", l, 1)
                tt(heads(rot1), heads(rot1), by_head(16), ALU.mult)
                dve.drain()
                wait(F, "silu_g", l, 1)
                tt(ret_c, ret_c, proj[:, :, RG:RG + 256], ALU.mult).then_inc(F["ro"].sem, 1)
                lo1(l, 15)
                mix_lo(2, AT1["T_ro"], 0, 2, True)
                mix_lo(3, AT1["o_mla"], 5, 2)
                mix_lo(4, AT1["o_mla"] + 1, 7, 1)
                lo1(l, 16)
                lo1(l, 17)
                lo1(l, 18)

                def layer_norm(n0, there, done):
                    for ch in range(NC):
                        there(ch)
                        if ch == 0:
                            wait(F, "table", l, 16 * (n0 + 2))
                        for nh in range(2):
                            nc.vector.bn_stats(stats[:, ch, 6 * nh:6 * nh + 6], ybank(ch, nh)[:, :])
                        dve.drain()
                        nc.vector.bn_aggr(mv[:, ch, :], stats[:, ch, :])
                        dve.drain()
                        ts(lve[:, ch:ch + 1], mv[:, ch, 1:2], LN_EPS, None, ALU.add).then_inc(F["ln_var"].sem, 1)
                        for nh in range(2):
                            cols_of = slice(512 * nh, 512 * nh + 512)
                            stt(out=x[:, ch, cols_of], in0=ybank(ch, nh)[:, :], scalar=mv[:, ch, 0:1], in1=table[:, 0, cols_of],
                                op0=ALU.subtract, op1=ALU.mult)
                        dve.drain()
                        wait(F, "ln_rstd", l, n0 + ch + 1)
                        stt(out=x[:, ch, :], in0=x[:, ch, :], scalar=lrstd[:, ch:ch + 1], in1=table[:, 1, :],
                            op0=ALU.mult, op1=ALU.add).then_inc(F[done].sem, 1)

                def mixed(ch):
                    if ch == 0:
                        wait(F, "mix_c0", l, 1)
                    else:
                        slab_is_done(slab_number(0, S1, l, S1_OUT + 3))

                layer_norm(0, mixed, "ln1")
                operand_lo_c(F, l, 4, TPB)
                for ch in range(NC):
                    wait(F, "xs_hi", l, ch + 1)
                    tt(xs_lo[:, ch, :], x[:, ch, :], xs_hi[:, ch, :].bitcast(F32), ALU.subtract).then_inc(F["xs_lo"].sem, 1)
                lo1(l, 19)

                wait(F, "routed", l, 1)

                def step(i):
                    dve.drain()

                def wide(t, n):
                    return t.unsqueeze(2).to_broadcast([P, NC, n])

                group = lambda t: t.rearrange("p c (g n) -> p c g n", g=4)
                step(tt(biased, scores, rbias[:].unsqueeze(1).to_broadcast([P, NC, 16]), ALU.add))
                bg = group(biased)
                for o, n in ((0, 1), (3, 2), (5, 3)):
                    i = tt(pairs[:, :, :, o:o + 4 - n], bg[:, :, :, 0:4 - n], bg[:, :, :, n:4], ALU.add)
                step(i)
                step(nc.vector.tensor_reduce(gscore, pairs, axis=AX.X, op=ALU.max))

                def first_best(hot, values, rank, width):
                    cd = cand[:, :, 0:width]
                    step(nc.vector.tensor_reduce(gtop, values, axis=AX.X, op=ALU.max))
                    step(tt(cd, values, wide(gtop, width), ALU.is_equal))
                    step(tt(cd, cd, rank, ALU.mult))
                    step(nc.vector.tensor_reduce(ctop, cd, axis=AX.X, op=ALU.max))
                    step(tt(hot, cd, wide(ctop, width), ALU.is_equal))

                first_best(ghot, gscore, c("rank4").rearrange("p (c g) -> p c g", c=NC), 4)
                dve.sem_inc(F["ghot"].sem, 1)
                wait(F, "ranked", l, 1)
                step(stt(out=slot_of, in0=bank[6][:, 0:8].rearrange("p (c g) -> p c g", c=NC), scalar=1.0, in1=ghot, op0=ALU.add, op1=ALU.mult))
                for ch in range(NC):
                    tt(in_slot[:, ch, :, :], c("slot").unsqueeze(1).to_broadcast([P, NG, P]), slot_of[:, ch, :].unsqueeze(2).to_broadcast([P, NG, P]),
                       ALU.is_equal).then_inc(F["in_slot"].sem, 1)
                nc.vector.tensor_reduce(ctop[:, 0:1], bank[6][:, 8:12], axis=AX.X, op=ALU.max)
                dve.drain()
                nc.vector.tensor_copy(overflow[:], ctop[:, 0:1])
                dve.drain()
                dve.sem_inc(F["sized"].sem, 1)
                for k in range(DK):
                    wait(F, "gathered", l, 2 * k + 2)
                    nc.vector.tensor_copy(xg_lo[:, k, :, :].rearrange("p g n -> p (g n)"), bank[4 + (2 * k + 1) % 4][:, :]).then_inc(F["xg_lo"].sem, 1)
                in_group = lambda t: t.unsqueeze(3).to_broadcast([P, NC, 4, 4])
                tt(bg, bg, in_group(ghot), ALU.mult)
                step(ts(gscore, ghot, -NEG, NEG, ALU.mult, ALU.add))
                step(tt(bg, bg, in_group(gscore), ALU.add))
                rank = c("rank16").rearrange("p (c e) -> p c e", c=NC)
                first_best(hot1, biased, rank, 16)
                step(stt(out=biased, in0=hot1, scalar=2 * NEG, in1=biased, op0=ALU.mult, op1=ALU.add))
                first_best(hot2, biased, rank, 16)
                step(tt(hot1, hot1, hot2, ALU.add))
                step(tt(gates, scores, hot1, ALU.mult))
                step(nc.vector.tensor_reduce(gtop, gates, axis=AX.X, op=ALU.add))
                step(nc.vector.reciprocal(ctop, gtop))
                tt(gates, gates, wide(ctop, 16), ALU.mult).then_inc(F["gates"].sem, 1)
                dve.drain()
                lo1(l, 20)
                size = dve.value_load(overflow[0:1, 0:1], min_val=0, max_val=T)

                def ahead(j_fixed, u):
                    split_lo(dve, l * S1 + u * 3 + j_fixed, j_fixed % RING)

                def expert_act(u, gate):
                    wait(F, "sg", l, u * 2 + 2)
                    stt(out=av[:, 0, :], in0=bank[HB][:, FE:2 * FE], scalar=gate, in1=sg[:, 0, :], op0=ALU.mult, op1=ALU.mult).then_inc(F["a"].sem, 2)

                def expert_lo(n):
                    wait(F, "a_hi", l, n)
                    tt(act_lo[:, :, 0:P], bank[5][:, 0:2 * P].rearrange("p (f n) -> p f n", f=2), act_hi[:, :, 0:P].bitcast(F32),
                       ALU.subtract).then_inc(F["a_lo"].sem, 1)

                def group_lo(n):
                    wait(F, "yg_hi", l, n)
                    for nh in range(2):
                        cols_of = slice(512 * nh, 512 * nh + 512)
                        i = tt(yg_lo[:, cols_of], bank[6 + nh][:, :], yg_hi[:, cols_of].bitcast(F32), ALU.subtract)
                    i.then_inc(F["yg_lo"].sem, 1)

                with dve.If(size > P):
                    units_lo(F, l, 0, S1, S1_MOE, NE, 0, lambda u, ch: gates[:, ch, u:u + 1] if isinstance(u, int) else gates[:, ch, bass.ds(u, 1)])(S1_MOE + 3)
                    dve.sem_inc(F["yg_lo"].sem, NG)
                with dve.Else():
                    def expert(u, groups_done, gate, last=False):
                        ahead(S1_MOE + 2, u)
                        expert_act(u, gate)
                        if last:
                            expert_lo(NE)
                        ahead(S1_MOE + 3, u)
                        if last:
                            group_lo(NG)
                        else:
                            expert_lo(u + 1)
                            ahead(S1_MOE + 4, u)
                        if groups_done is not None:
                            group_lo(groups_done)

                    wait(F, "slot_gates", l, 1)
                    nc.vector.tensor_copy(slot_gates, bank[5][:, 0:16])
                    dve.drain()
                    expert_act(0, slot_gates[:, 0:1])
                    ahead(S1_MOE + 3, 0)
                    expert_lo(1)
                    ahead(S1_MOE + 4, 0)
                    gate = lambda u: slot_gates[:, u:u + 1]
                    for e in range(1, GE):
                        expert(e, None, gate(e))
                    with dve.Fori(1, NG - 1) as g:
                        for e in range(GE):
                            u = g * GE + e
                            expert(u, g if e == 0 else None, slot_gates[:, bass.ds(u, 1)])
                    for e in range(GE):
                        u = (NG - 1) * GE + e
                        expert(u, NG - 1 if e == 0 else None, gate(u), e == GE - 1)
                layer_norm(2, lambda ch: wait(F, "y", l, ch + 1), "x_ready")

            with dve.Fori(0, DEPTH) as l:
                layer_columns(l, VECTORS2, cur2, 7 * DEPTH)
                ts(nsink[:, 0:16].rearrange("p (c h) -> p c h", c=NC), sinks2[:, bass.ds(l, 1), :].to_broadcast([P, NC, AH]),
                   -1.0, None, ALU.mult).then_inc(G["cur"].sem, 1)

                def operand_lo_k(stage, banks=TPB):
                    for n in range(4):
                        wait(G, "op_hi", l, (0, 4, 12)[stage] + n + 1)
                        for k in range(2):
                            t = 2 * n + k
                            i = stt(out=op_lo[:, t, :], in0=bank[banks + n][:, k * T:k * T + T], scalar=cur2[:, 8 * stage + t:8 * stage + t + 1],
                                    in1=op_hi[:, t, :].bitcast(F32), op0=ALU.mult, op1=ALU.subtract)
                        i.then_inc(G["op_lo"].sem, 1)

                def mean_squares(stage):
                    wait(G, "ss_raw", l, 2 * stage + 2)
                    ts(ss2, ss_raw2, 1.0 / D, RMS_EPS, ALU.mult, ALU.add).then_inc(G["ss"].sem, 1)

                def ffn_residual(run, last_slab):
                    for ch in range(NC):
                        if ch == 0:
                            wait(G, "y_c0", l, run + 1)
                        else:
                            slab_is_done(last_slab)
                        for nh in range(2):
                            v = x[:, ch, 512 * nh:512 * nh + 512]
                            i = stt(out=v, in0=ybank(ch, nh)[:, :], scalar=0.5, in1=v, op0=ALU.mult, op1=ALU.add)
                        i.then_inc(G["x_ready"].sem, 1)

                column = lambda u, ch: rms2[:, ch:ch + 1]
                num = lambda j: slab_number(BASE2, S2, l, j)

                operand_lo_k(0)
                lo2(l, 1)
                mean_squares(0)
                lo2(l, 2)
                following = units_lo(G, l, BASE2, S2, 0, NU2, 0, column)
                following(3)
                ffn_residual(0, num(S2_Q - 1))

                operand_lo_k(1)
                following(4)
                mean_squares(1)
                for j in range(2, 9):
                    lo2(l, S2_Q + j)

                def gate_in(b):
                    for ch in range(NC):
                        if ch == 0:
                            wait(G, "q_c0", l, 3 + b + 1)
                        else:
                            slab_is_done(num(S2_GATE + 2 * b + 1))
                        o = GATES[b] - GA
                        stt(out=proj[:, ch, GA + o:GA + o + 512], in0=bank[(2 if b % 2 == 0 else 0) + ch][:, :], scalar=rms2[:, ch:ch + 1],
                            in1=table[:, o // D, o % D:o % D + 512], op0=ALU.mult, op1=ALU.add).then_inc(G["gate_in"].sem, 1)

                def masked(g):
                    for seg, name in enumerate(("m_zero", "m_tri", "m_ge", "m_zero")):
                        n = AT2["s"] + 4 * g + seg
                        wait(G, "job", l, n + 1)
                        stt(out=s2[:, g, :, seg * P:seg * P + P], in0=bank[4 + n % 4][:, :].rearrange("p (h n) -> p h n", h=4), scalar=HD ** -0.5,
                            in1=c(name).unsqueeze(1).to_broadcast([P, 4, P]), op0=ALU.mult, op1=ALU.add).then_inc(G["masked"].sem, 1)
                    dve.drain()
                    o = 8 * g
                    for ch in range(NC):
                        row_max(negm[:, o + 4 * ch:o + 4 * ch + 4], s2[:, g, :, ch * T:ch * T + T])
                    dve.drain()
                    by = lambda t: t.rearrange("p (c h) -> p c h", c=NC)
                    m, ns = by(negm[:, o:o + 8]), nsink[:, 0:16].rearrange("p (c h e) -> p c h e", c=NC, e=2)[:, :, :, g]
                    tt(m, m, ns, ALU.min)
                    dve.drain()
                    tt(by(dsink[:, o:o + 8]), m, ns, ALU.subtract).then_inc(G["negm"].sem, 1)

                def probs(g):
                    o = 8 * g
                    wait(G, "exped", l, g + 1)
                    tt(rsum[:, o:o + 8], rsum[:, o:o + 8], es[:, o:o + 8], ALU.add)
                    dve.drain()
                    nc.vector.reciprocal(rden[:, o:o + 8], rsum[:, o:o + 8])
                    dve.drain()
                    for ch in range(NC):
                        v = s2[:, g, :, ch * T:ch * T + T]
                        i = tt(v, v, rden[:, o + 4 * ch:o + 4 * ch + 4].unsqueeze(2).to_broadcast([P, 4, T]), ALU.mult)
                    i.then_inc(G["probs"].sem, 1)

                wait(G, "bgate", l, 16)
                gate_in(0)
                masked(0)
                lo2(l, S2_Q + 9)
                lo2(l, S2_Q + 10)
                probs(0)
                gate_in(1)
                masked(1)
                lo2(l, S2_Q + 11)
                probs(1)
                gate_in(2)
                for n in range(2):
                    job = AT2["mixed"] + n
                    wait(G, "mix_hi", l, n + 1)
                    for k in range(2):
                        t = 2 * n + k
                        i = stt(out=lat_lo[:, t, :], in0=bank[4 + job % 4][:, k * T:k * T + T], scalar=cur2[:, 24 + t:25 + t],
                                in1=lat_hi[:, t, :].bitcast(F32), op0=ALU.mult, op1=ALU.subtract)
                    i.then_inc(G["mix_lo"].sem, 1)
                lo2(l, S2_Q + 12)
                lo2(l, S2_Q + 13)
                gate_in(3)
                lo2(l, S2_Q + 14)
                for n in range(2):
                    job = AT2["o"] + n
                    wait(G, "mix_hi", l, 2 + n + 1)
                    flat = lambda t: t[:, 2 * n:2 * n + 2, :].rearrange("p k t -> p (k t)")
                    tt(flat(op_lo), bank[4 + job % 4][:, :], flat(op_hi).bitcast(F32), ALU.subtract).then_inc(G["mix_lo"].sem, 1)
                lo2(l, S2_Q + 15)

                def branch_part(branch, nh, ch):
                    o = GATES[2 * branch + nh]
                    return bank[4 * branch + 2 * ch + nh][:, :], proj[:, ch, o:o + 512]

                def gated(branch, nh):
                    wait(G, "gate", l, 2 * branch + nh + 1)
                    for ch in range(NC):
                        if nh == 0 or ch == 1:
                            slab_is_done(num(S2_BR + 2 * branch + nh))
                        else:
                            wait(G, "br_c0", l, branch + 1)
                        b, v = branch_part(branch, nh, ch)
                        tt(v, b, v, ALU.mult)

                gated(0, 0)
                lo2(l, S2_Q + 16)
                gated(0, 1)
                lo2(l, S2_Q + 17)
                for nh in range(2):
                    gated(1, nh)
                    dve.drain()
                    for ch in range(NC):
                        v, w = branch_part(1, nh, ch)[1], branch_part(0, nh, ch)[1]
                        tt(v, v, w, ALU.add).then_inc(G["z"].sem, 1)
                    if nh == 0:
                        lo2(l, S2_Q + 18)
                operand_lo_c(G, l, 8, 0, ((0, 0), (1, 0), (0, 1), (1, 1)))
                for j in range(19, 23):
                    lo2(l, S2_Q + j)
                for ch in range(NC):
                    if ch == 0:
                        wait(G, "out_c0", l, 1)
                    else:
                        slab_is_done(num(S2_OUT + 3))
                    for nh in range(2):
                        v = x[:, ch, 512 * nh:512 * nh + 512]
                        i = tt(v, bank[4 + 2 * ch + nh][:, :], v, ALU.add)
                    i.then_inc(G["x_ready"].sem, 1)

                operand_lo_k(2, 0)
                mean_squares(2)
                lo2(l, S2_FFN2 + 2)
                following = units_lo(G, l, BASE2, S2, S2_FFN2, NU2, NU2, column)
                following(S2_FFN2 + 3)
                ffn_residual(1, num(S2 - 1))

            dve.wait_ge(G["ss_raw"].sem, G["ss_raw"].after(DEPTH, 2))
            ts(ss2, ss_raw2, 1.0 / D, RMS_EPS, ALU.mult, ALU.add).then_inc(final_ss.sem, 1)
            dve.wait_ge(block2_in.sem, 16)
            dve.wait_ge(final_rstd.sem, 1)
            for ch in range(NC):
                stt(out=x[:, ch, :], in0=x[:, ch, :], scalar=rms2[:, ch:ch + 1], in1=table[:, 0, :], op0=ALU.mult, op1=ALU.mult).then_inc(final_out.sem, 1)


NAMES = (
    "x", "w_in", "ret_gn_w", "swa_sinks", "mla_q_norm_w", "mla_kv_norm_w", "mla_w_uq", "mla_w_ukv", "w_out",
    "ln1_g", "ln1_b", "router_w", "router_bias", "exp_w_gate_up", "exp_w_down", "ln2_g", "ln2_b", "ffn1_norm_2",
    "ffn1_w1_2", "ffn1_w3_2", "ffn1_w2_2", "mix_norm_2", "w_in_2", "b_gate_2", "attn_sink_2", "pool_w_2",
    "pool_scale_2", "w_branch_attn_2", "w_branch_pool_2", "w_out_2", "ffn2_norm_2", "ffn2_w1_2", "ffn2_w3_2",
    "ffn2_w2_2", "final_norm_2",
)


def kernel(**inputs):
    import concourse.bacc as bacc
    from concourse.bass_utils import run_bass_kernel_spmd

    nc = bacc.Bacc("TRN2", target_bir_lowering=False, num_devices=1)
    arrays = {name: np.ascontiguousarray(inputs[name]) for name in NAMES}
    arrays["constants"] = CONSTANTS
    aps = {n: nc.dram_tensor(n, v.shape, mybir.dt.from_np(v.dtype), kind="ExternalInput").ap() for n, v in arrays.items()}
    out = nc.dram_tensor("out", (1, T, D), F32, kind="ExternalOutput").ap()
    program(nc, aps, out)
    result = run_bass_kernel_spmd(nc, [arrays], core_ids=[0])
    return result.results[0]["out"]
```
